# Optimizing a Trainium2 kernel written in Bass

```python
import jax, jax.numpy as jnp
from jax import lax
import numpy as np

D_MODEL = 1024
BATCH = 1
SEQ = 256
DEPTH = 2

N_GROUPS = 4
GROUP_W = D_MODEL // N_GROUPS
EPS = 1e-6

MLSTM_HEADS = 4
MLSTM_DH = GROUP_W // MLSTM_HEADS
MLSTM_CONV = 4
MLSTM_CHUNK = 64

MLA_HEADS = 4
MLA_NOPE = 64
MLA_ROPE = 32
MLA_V = GROUP_W // MLA_HEADS
MLA_Q_RANK = 192
MLA_KV_RANK = 128
ROPE_BASE = 10000.0
Q_BLOCK = 128

GLA_HEADS = 4
GLA_DK = GROUP_W // (2 * GLA_HEADS)
GLA_DV = GROUP_W // GLA_HEADS
GLA_GATE_RANK = 16
GLA_TAU = 16.0
GLA_CHUNK = 64

CONV_CH = GROUP_W
CONV_WIDTH = 31

D_FF = 256 * ((8 * D_MODEL // 3 + 255) // 256)
N_EXPERTS = 8
TOP_K = 2
MOE_BLOCK = 256
N_DENSE = (DEPTH + 1) // 2
N_MOE = DEPTH // 2

IN_SPLITS = (
    2 * MLSTM_HEADS * MLSTM_DH,
    MLSTM_HEADS * MLSTM_DH,
    MLSTM_HEADS * MLSTM_DH,
    2 * MLSTM_HEADS,
    MLA_Q_RANK,
    MLA_KV_RANK,
    MLA_ROPE,
    GLA_HEADS * GLA_DK,
    GLA_HEADS * GLA_DK,
    GLA_HEADS * GLA_DV,
    GLA_HEADS * GLA_DV,
    GLA_GATE_RANK,
    2 * CONV_CH,
)
D_IN = sum(IN_SPLITS)

kernel_name = 'hybrid_mlstm_mla_gla_conformer_moe'

def rms_norm(x, g):
    xf = x.astype(jnp.float32)
    y = xf * lax.rsqrt(jnp.mean(xf * xf, axis=-1, keepdims=True) + EPS)
    return (y * g.astype(jnp.float32)).astype(x.dtype)

def layer_norm(x, g, b):
    xf = x.astype(jnp.float32)
    mu = jnp.mean(xf, axis=-1, keepdims=True)
    var = jnp.mean(jnp.square(xf - mu), axis=-1, keepdims=True)
    y = (xf - mu) * lax.rsqrt(var + EPS)
    return (y * g.astype(jnp.float32) + b.astype(jnp.float32)).astype(x.dtype)

def group_rms_norm(y, g, n_groups):
    B, S, W = y.shape
    yf = y.reshape(B, S, n_groups, W // n_groups).astype(jnp.float32)
    yf = yf * lax.rsqrt(jnp.mean(yf * yf, axis=-1, keepdims=True) + EPS)
    return (yf.reshape(B, S, W) * g.astype(jnp.float32)).astype(y.dtype)

def causal_dwconv(x, w, b):
    k, c = w.shape
    y = lax.conv_general_dilated(x, w[:, None, :].astype(x.dtype), (1,), [(k - 1, 0)],
                                 dimension_numbers=('NWC', 'WIO', 'NWC'),
                                 feature_group_count=c)
    return y + b.astype(x.dtype)

def rotary(x, cos, sin):
    half = x.shape[-1] // 2
    x1, x2 = x[..., :half], x[..., half:]
    return jnp.concatenate([x1 * cos - x2 * sin, x2 * cos + x1 * sin], axis=-1).astype(x.dtype)

def split_cols(z, sizes):
    return jnp.split(z, np.cumsum(sizes)[:-1].tolist(), axis=-1)

def heads(a, n_heads):
    B, S, W = a.shape
    return a.reshape(B, S, n_heads, W // n_heads).transpose(0, 2, 1, 3)

def to_chunks(a, L):
    B, H, S = a.shape[:3]
    return jnp.moveaxis(a.reshape(B, H, S // L, L, *a.shape[3:]), 2, 0)

def from_chunks(a):
    nC, B, H, L = a.shape[:4]
    a = jnp.moveaxis(a, 0, 2).reshape(B, H, nC * L, *a.shape[4:])
    return jnp.swapaxes(a, 1, 2)

def mlstm_mixer(qk_pre, v_pre, o_pre, if_pre, conv_w, conv_b, gate_b):
    f32 = jnp.float32
    B, S, _ = v_pre.shape
    qk = jax.nn.silu(causal_dwconv(qk_pre, conv_w, conv_b))
    q, k = jnp.split(qk, 2, axis=-1)
    q = heads(q, MLSTM_HEADS).astype(f32) * (MLSTM_DH ** -0.5)
    k = heads(k, MLSTM_HEADS).astype(f32)
    v = heads(v_pre, MLSTM_HEADS).astype(f32)
    gates = if_pre.astype(f32) + gate_b.astype(f32)
    ig = gates[..., :MLSTM_HEADS].transpose(0, 2, 1)
    lf = jax.nn.log_sigmoid(gates[..., MLSTM_HEADS:]).transpose(0, 2, 1)
    L = MLSTM_CHUNK
    causal = jnp.tril(jnp.ones((L, L), dtype=bool))

    def step(carry, xs):
        c, n, m = carry
        qc, kc, vc, ic, fc = xs
        b = jnp.cumsum(fc, axis=-1)
        log_d = jnp.where(causal, b[..., :, None] - b[..., None, :] + ic[..., None, :], -jnp.inf)
        log_inter = b + m[..., None]
        m_t = jnp.maximum(log_inter, jnp.max(log_d, axis=-1))
        w_inter = jnp.exp(log_inter - m_t)
        s = jnp.einsum('bhtd,bhjd->bhtj', qc, kc) * jnp.exp(log_d - m_t[..., None])
        num = w_inter[..., None] * jnp.einsum('bhtd,bhdv->bhtv', qc, c) + jnp.einsum('bhtj,bhjv->bhtv', s, vc)
        den = w_inter * jnp.einsum('bhtd,bhd->bht', qc, n) + jnp.sum(s, axis=-1)
        h = num / jnp.maximum(jnp.abs(den), jnp.exp(-m_t))[..., None]
        b_end = b[..., -1]
        log_w = b_end[..., None] - b + ic
        m_new = jnp.maximum(b_end + m, jnp.max(log_w, axis=-1))
        carry_decay = jnp.exp(b_end + m - m_new)
        kw = jnp.exp(log_w - m_new[..., None])[..., None] * kc
        c = carry_decay[..., None, None] * c + jnp.einsum('bhjd,bhjv->bhdv', kw, vc)
        n = carry_decay[..., None] * n + jnp.sum(kw, axis=-2)
        return (c, n, m_new), h

    init = (jnp.zeros((B, MLSTM_HEADS, MLSTM_DH, MLSTM_DH), f32),
            jnp.zeros((B, MLSTM_HEADS, MLSTM_DH), f32),
            jnp.zeros((B, MLSTM_HEADS), f32))
    _, h = lax.scan(step, init, (to_chunks(q, L), to_chunks(k, L), to_chunks(v, L),
                                 to_chunks(ig, L), to_chunks(lf, L)))
    h = from_chunks(h).reshape(B, S, MLSTM_HEADS * MLSTM_DH)
    return (jax.nn.sigmoid(o_pre.astype(f32)) * h).astype(v_pre.dtype)

def mla_mixer(c_q, c_kv, k_rope, cos, sin, q_norm_g, w_uq, kv_norm_g, w_ukv):
    B, S, _ = c_q.shape
    q = (rms_norm(c_q, q_norm_g) @ w_uq).reshape(B, S, MLA_HEADS, MLA_NOPE + MLA_ROPE)
    q_nope = q[..., :MLA_NOPE]
    q_rot = rotary(q[..., MLA_NOPE:], cos[:, :, None], sin[:, :, None])
    kv = (rms_norm(c_kv, kv_norm_g) @ w_ukv).reshape(B, S, MLA_HEADS, MLA_NOPE + MLA_V)
    k_nope = kv[..., :MLA_NOPE].transpose(0, 2, 1, 3)
    v = kv[..., MLA_NOPE:].transpose(0, 2, 1, 3)
    k_rot = rotary(k_rope, cos, sin)
    nq = S // Q_BLOCK
    qn_b = jnp.moveaxis(q_nope.reshape(B, nq, Q_BLOCK, MLA_HEADS, MLA_NOPE), 1, 0)
    qr_b = jnp.moveaxis(q_rot.reshape(B, nq, Q_BLOCK, MLA_HEADS, MLA_ROPE), 1, 0)
    scale = (MLA_NOPE + MLA_ROPE) ** -0.5
    k_pos = jnp.arange(S)

    def attend(args):
        qn, qr, blk = args
        s = jnp.einsum('bqhd,bhkd->bhqk', qn, k_nope) + jnp.einsum('bqhd,bkd->bhqk', qr, k_rot)
        q_pos = blk * Q_BLOCK + jnp.arange(Q_BLOCK)
        mask = k_pos[None, :] <= q_pos[:, None]
        s = jnp.where(mask, s.astype(jnp.float32) * scale, -jnp.inf)
        p = jax.nn.softmax(s, axis=-1).astype(v.dtype)
        return jnp.einsum('bhqk,bhkd->bqhd', p, v)

    o = lax.map(attend, (qn_b, qr_b, jnp.arange(nq)))
    return jnp.moveaxis(o, 0, 1).reshape(B, S, MLA_HEADS * MLA_V)

def gla_mixer(q_pre, k_pre, v_pre, r_pre, a_pre, w_alpha, b_alpha):
    f32 = jnp.float32
    B, S, _ = v_pre.shape
    q = heads(q_pre, GLA_HEADS).astype(f32) * (GLA_DK ** -0.5)
    k = heads(k_pre, GLA_HEADS).astype(f32)
    v = heads(v_pre, GLA_HEADS).astype(f32)
    g = jax.nn.log_sigmoid((a_pre @ w_alpha + b_alpha).astype(f32)) / GLA_TAU
    g = heads(g, GLA_HEADS)
    L = GLA_CHUNK
    causal = jnp.tril(jnp.ones((L, L), dtype=bool))

    def step(state, xs):
        qc, kc, vc, gc = xs
        b = jnp.cumsum(gc, axis=-2)
        diff = b[:, :, :, None, :] - b[:, :, None, :, :]
        decay = jnp.exp(jnp.where(causal[:, :, None], diff, -jnp.inf))
        a = jnp.einsum('bhtd,bhjd,bhtjd->bhtj', qc, kc, decay)
        o = jnp.einsum('bhtj,bhjv->bhtv', a, vc) + jnp.einsum('bhtd,bhdv->bhtv', qc * jnp.exp(b), state)
        b_end = b[:, :, -1:, :]
        state = (jnp.exp(b_end)[:, :, 0, :, None] * state
                 + jnp.einsum('bhjd,bhjv->bhdv', kc * jnp.exp(b_end - b), vc))
        return state, o

    init = jnp.zeros((B, GLA_HEADS, GLA_DK, GLA_DV), f32)
    _, o = lax.scan(step, init, (to_chunks(q, L), to_chunks(k, L), to_chunks(v, L), to_chunks(g, L)))
    o = from_chunks(o)
    o = o * lax.rsqrt(jnp.mean(o * o, axis=-1, keepdims=True) + EPS)
    o = o.reshape(B, S, GLA_HEADS * GLA_DV) * jax.nn.silu(r_pre.astype(f32))
    return o.astype(v_pre.dtype)

def conformer_conv(glu_pre, conv_w, conv_b, ln_g, ln_b):
    val, gate = jnp.split(glu_pre, 2, axis=-1)
    u = causal_dwconv(val * jax.nn.sigmoid(gate), conv_w, conv_b)
    return jax.nn.silu(layer_norm(u, ln_g, ln_b))

def swiglu(t, w_gate, w_up, w_down):
    return (jax.nn.silu(t @ w_gate) * (t @ w_up)) @ w_down

def moe_ffn(u, router, w_gate, w_up, w_down):
    B, S, D = u.shape
    t = u.reshape(-1, D)
    n = t.shape[0]
    logits = (t @ router).astype(jnp.float32)
    top_v, top_e = lax.top_k(logits, TOP_K)
    top_w = jax.nn.softmax(top_v, axis=-1)
    a = n * TOP_K
    flat_e = top_e.reshape(-1)
    flat_tok = jnp.repeat(jnp.arange(n, dtype=jnp.int32), TOP_K)
    flat_w = top_w.reshape(-1)
    order = jnp.argsort(flat_e)
    e_sorted = flat_e[order]
    counts = jnp.bincount(flat_e, length=N_EXPERTS)
    starts = jnp.cumsum(counts) - counts
    padded = (counts + MOE_BLOCK - 1) // MOE_BLOCK * MOE_BLOCK
    padded_end = jnp.cumsum(padded)
    padded_start = padded_end - padded
    dest = padded_start[e_sorted] + jnp.arange(a) - starts[e_sorted]
    n_blocks = -(-a // MOE_BLOCK) + N_EXPERTS
    rows = n_blocks * MOE_BLOCK
    row_tok = jnp.zeros((rows,), jnp.int32).at[dest].set(flat_tok[order])
    row_w = jnp.zeros((rows,), jnp.float32).at[dest].set(flat_w[order])
    block_e = jnp.minimum(jnp.searchsorted(padded_end, jnp.arange(n_blocks) * MOE_BLOCK, side='right'),
                          N_EXPERTS - 1)
    xb = t[row_tok].reshape(n_blocks, MOE_BLOCK, D)

    def expert_block(args):
        xe, e = args
        return swiglu(xe, w_gate[e], w_up[e], w_down[e])

    yb = lax.map(expert_block, (xb, block_e)).reshape(rows, D)
    out = jnp.zeros_like(t).at[row_tok].add((yb * row_w[:, None]).astype(t.dtype))
    return out.reshape(B, S, D)

def setup_inputs(seed: int = 0) -> dict:
    key = jax.random.key(seed)
    ks = jax.random.split(key, 32)
    f32 = jnp.float32

    def nrm(k, shape, scale):
        return jax.random.normal(k, shape, f32) * scale

    def gain(k, shape):
        return 1.0 + nrm(k, shape, 0.02)

    offset = jax.random.randint(ks[1], (BATCH, 1), 0, 1024, dtype=jnp.int32)
    positions = offset + jnp.arange(SEQ, dtype=jnp.int32)[None, :]
    gate_i = nrm(ks[6], (DEPTH, MLSTM_HEADS), 0.1)
    gate_f = jnp.linspace(3.0, 6.0, MLSTM_HEADS, dtype=f32)[None, :] + nrm(ks[7], (DEPTH, MLSTM_HEADS), 0.1)
    return {
        'x': nrm(ks[0], (BATCH, SEQ, D_MODEL), 1.0),
        'positions': positions,
        'norm1_g': gain(ks[2], (DEPTH, D_MODEL)),
        'w_in': nrm(ks[3], (DEPTH, D_MODEL, D_IN), D_MODEL ** -0.5),
        'mlstm_conv_w': nrm(ks[4], (DEPTH, MLSTM_CONV, 2 * MLSTM_HEADS * MLSTM_DH), MLSTM_CONV ** -0.5),
        'mlstm_conv_b': nrm(ks[5], (DEPTH, 2 * MLSTM_HEADS * MLSTM_DH), 0.02),
        'mlstm_gate_b': jnp.concatenate([gate_i, gate_f], axis=-1),
        'mla_q_norm_g': gain(ks[8], (DEPTH, MLA_Q_RANK)),
        'mla_w_uq': nrm(ks[9], (DEPTH, MLA_Q_RANK, MLA_HEADS * (MLA_NOPE + MLA_ROPE)), MLA_Q_RANK ** -0.5),
        'mla_kv_norm_g': gain(ks[10], (DEPTH, MLA_KV_RANK)),
        'mla_w_ukv': nrm(ks[11], (DEPTH, MLA_KV_RANK, MLA_HEADS * (MLA_NOPE + MLA_V)), MLA_KV_RANK ** -0.5),
        'gla_w_alpha': nrm(ks[12], (DEPTH, GLA_GATE_RANK, GLA_HEADS * GLA_DK), GLA_GATE_RANK ** -0.5),
        'gla_b_alpha': nrm(ks[13], (DEPTH, GLA_HEADS * GLA_DK), 0.1),
        'conv_w': nrm(ks[14], (DEPTH, CONV_WIDTH, CONV_CH), CONV_WIDTH ** -0.5),
        'conv_b': nrm(ks[15], (DEPTH, CONV_CH), 0.02),
        'conv_ln_g': gain(ks[16], (DEPTH, CONV_CH)),
        'conv_ln_b': nrm(ks[17], (DEPTH, CONV_CH), 0.02),
        'fuse_g': gain(ks[18], (DEPTH, D_MODEL)),
        'w_out': nrm(ks[19], (DEPTH, D_MODEL, D_MODEL), D_MODEL ** -0.5),
        'norm2_g': gain(ks[20], (DEPTH, D_MODEL)),
        'ffn_w_gate': nrm(ks[21], (N_DENSE, D_MODEL, D_FF), D_MODEL ** -0.5),
        'ffn_w_up': nrm(ks[22], (N_DENSE, D_MODEL, D_FF), D_MODEL ** -0.5),
        'ffn_w_down': nrm(ks[23], (N_DENSE, D_FF, D_MODEL), D_FF ** -0.5),
        'moe_router': nrm(ks[24], (N_MOE, D_MODEL, N_EXPERTS), D_MODEL ** -0.5),
        'moe_w_gate': nrm(ks[25], (N_MOE, N_EXPERTS, D_MODEL, D_FF), D_MODEL ** -0.5),
        'moe_w_up': nrm(ks[26], (N_MOE, N_EXPERTS, D_MODEL, D_FF), D_MODEL ** -0.5),
        'moe_w_down': nrm(ks[27], (N_MOE, N_EXPERTS, D_FF, D_MODEL), D_FF ** -0.5),
        'final_norm_g': gain(ks[28], (D_MODEL,)),
    }

def reference(x, positions, norm1_g, w_in, mlstm_conv_w, mlstm_conv_b, mlstm_gate_b,
              mla_q_norm_g, mla_w_uq, mla_kv_norm_g, mla_w_ukv, gla_w_alpha, gla_b_alpha,
              conv_w, conv_b, conv_ln_g, conv_ln_b, fuse_g, w_out, norm2_g,
              ffn_w_gate, ffn_w_up, ffn_w_down, moe_router, moe_w_gate, moe_w_up, moe_w_down,
              final_norm_g):
    inv_freq = 1.0 / (ROPE_BASE ** (jnp.arange(0, MLA_ROPE, 2, dtype=jnp.float32) / MLA_ROPE))
    ang = positions.astype(jnp.float32)[..., None] * inv_freq
    cos, sin = jnp.cos(ang), jnp.sin(ang)
    h = x
    for l in range(DEPTH):
        z = rms_norm(h, norm1_g[l]) @ w_in[l]
        (m_qk, m_v, m_o, m_if, a_cq, a_ckv, a_kr,
         g_q, g_k, g_v, g_r, g_a, c_glu) = split_cols(z, IN_SPLITS)
        y = jnp.concatenate([
            mlstm_mixer(m_qk, m_v, m_o, m_if, mlstm_conv_w[l], mlstm_conv_b[l], mlstm_gate_b[l]),
            mla_mixer(a_cq, a_ckv, a_kr, cos, sin, mla_q_norm_g[l], mla_w_uq[l],
                      mla_kv_norm_g[l], mla_w_ukv[l]),
            gla_mixer(g_q, g_k, g_v, g_r, g_a, gla_w_alpha[l], gla_b_alpha[l]),
            conformer_conv(c_glu, conv_w[l], conv_b[l], conv_ln_g[l], conv_ln_b[l]),
        ], axis=-1)
        h = h + group_rms_norm(y, fuse_g[l], N_GROUPS) @ w_out[l]
        u = rms_norm(h, norm2_g[l])
        j = l // 2
        if l % 2 == 0:
            f = swiglu(u, ffn_w_gate[j], ffn_w_up[j], ffn_w_down[j])
        else:
            f = moe_ffn(u, moe_router[j], moe_w_gate[j], moe_w_up[j], moe_w_down[j])
        h = h + f
    return rms_norm(h, final_norm_g)


_drawn_inputs = setup_inputs


def setup_inputs(seed=0):
    import zlib

    import numpy as np

    out = dict(_drawn_inputs(seed))
    spreads = {}
    factors = {'mla_q_norm_g': 4.216, 'final_norm_g': 7.479, 'conv_ln_b': 2.787}
    for name, (base, spread) in spreads.items():
        noise = np.random.default_rng([zlib.crc32(name.encode()), seed]).standard_normal(out[name].shape)
        drawn = base * np.exp(spread * noise) if base else spread * noise
        out[name] = __import__('jax').numpy.asarray(drawn.astype(out[name].dtype))
    for name, factor in factors.items():
        out[name] = (out[name] * factor).astype(out[name].dtype)
    return out
```

```python
import math
from contextlib import ExitStack

import numpy as np
import concourse.bass as bass
from concourse import mybir

F32 = mybir.dt.float32
F32R = mybir.dt.float32r
I32 = mybir.dt.int32
U32 = mybir.dt.uint32
ALU = mybir.AluOpType
ACT = mybir.ActivationFunctionType
AX_X = mybir.AxisListType.X

P = 128
EPS = 1e-6
NEG = -1e30

PIECE = 2048
RING = 11
SPLIT = 3

W_IN_PIECES = [
    [(2168, 256)],
    [(2424, 256)],
    [(0, 256)],
    [(256, 256)],
    [(1024, 200)],
    [(1224, 160), (2152, 16)],
    [(1384, 256)],
    [(512, 256)],
    [(768, 256)],
    [(1640, 256)],
    [(1896, 256)],
]
N_IN = len(W_IN_PIECES)
FEATURE_MAJOR = (0, 1, 2, 3, 6)
N_OUT = 4
CHUNKS = 11
N_FFN = 3 * CHUNKS


def ffn_pieces():
    order = []
    for c in range(CHUNKS):
        order += [("a", c), ("b", c)]
        if c:
            order.append(("d", c - 1))
    return order + [("d", CHUNKS - 1)]


FFN_ORDER = ffn_pieces()
FFN_AT = {key: n for n, key in enumerate(FFN_ORDER)}


class Chain:

    def __init__(self, eng, sem):
        self.eng, self.sem, self.n = eng, sem, 0

    def done(self, ins):
        self.n += 1
        ins.then_inc(self.sem, 1)

    def wait(self, lag=0):
        if self.n > lag:
            self.eng.wait_ge(self.sem, self.n - lag)


def build(nc, x, positions, norm1_g, w_in, mlstm_conv_w, mlstm_conv_b, mlstm_gate_b,
          mla_q_norm_g, mla_w_uq, mla_kv_norm_g, mla_w_ukv, gla_w_alpha, gla_b_alpha,
          conv_w, conv_b, conv_ln_g, conv_ln_b, fuse_g, w_out, norm2_g,
          ffn_w_gate, ffn_w_up, ffn_w_down, moe_router, moe_w_gate, moe_w_up, moe_w_down,
          final_norm_g, out):
    DEPTH, D, _ = w_in.shape
    S = x.shape[1]
    TT = S // P
    KD = D // P
    HEADS = 4
    DH = 64
    CONV, MCONV = conv_w.shape[1], mlstm_conv_w.shape[1]
    E = moe_w_gate.shape[1]
    OVER = 3
    JOBS = E + OVER
    F_CH = moe_w_gate.shape[3] // CHUNKS
    assert (TT, KD, F_CH, E) == (2, 8, 256, 8)
    LAYER_PIECES = [0, N_IN + N_OUT + N_FFN]
    MOE0 = LAYER_PIECES[1] + N_IN + N_OUT
    DENSE0 = N_IN + N_OUT
    assert N_FFN % RING == 0 and N_FFN % SPLIT == 0

    ctx = ExitStack()

    def sb(name, shape, dt=F32, where=ctx):
        return where.enter_context(nc.sbuf_tensor(name, shape, dt))

    with ctx:
        ring = sb("ring", [P, RING, PIECE])
        h = sb("h", [P, TT, D])
        ident = sb("ident", [P, P])
        ones = sb("ones", [P, S])
        iota = sb("iota", [P, P])
        mask_kt = sb("mask_kt", [P, P])
        mask_qt = sb("mask_qt", [P, P])
        gla_mask = sb("gla_mask", [P, 3, P])
        before = sb("before", [P, P])
        cols = sb("cols", [P, 2, P])
        gate_b = sb("gate_b", [P, DEPTH, 8])
        ln_gb = sb("ln_gb", [P, 2, 256])
        router = sb("router", [P, KD, E])
        invf = sb("invf", [P, 16])
        pos_i = sb("pos_i", [P, TT], I32)
        pos_f = sb("pos_f", [P, TT])
        ang = sb("ang", [P, 2, TT, 16])
        turn = sb("turn", [P, 2, TT, 16])
        cossin = sb("cossin", [P, 2, TT, 16])
        epst = sb("epst", [P, 1])
        ss = sb("ss", [P, TT, 4])
        lnv = sb("lnv", [P, TT, 4])
        rstd = sb("rstd", [P, TT, 4])
        tiny = sb("tiny", [P, 1])
        logits = sb("logits", [P, TT, E])
        top8 = sb("top8", [P, TT, 8])
        idx8 = sb("idx8", [P, TT, 8], U32)
        idf = sb("idf", [P, TT, 8])
        gap = sb("gap", [P, TT])
        egap = sb("egap", [P, TT])
        w1 = sb("w1", [P, TT])
        w2 = sb("w2", [P, TT])
        oh1 = sb("oh1", [P, TT, E])
        oh2 = sb("oh2", [P, TT, E])
        routed = sb("routed", [P, TT, E])
        rank1 = sb("rank1", [P, TT, E])
        keys = sb("keys", [P, TT, JOBS])
        wts = sb("wts", [P, TT, JOBS])
        over = sb("over", [P, E])
        over_n = sb("over_n", [P, E])
        over_oh = sb("over_oh", [P, OVER, E])
        pick = sb("pick", [P, TT, E])
        jobs_f = sb("jobs_f", [P, 4])
        jobs_i = sb("jobs_i", [P, 4], I32)
        keycol = sb("keycol", [P, TT])
        wcol = sb("wcol", [P, TT])
        wslot = sb("wslot", [P, 1])

        with ExitStack() as part:
            un = sb("un", [P, TT, D], F32, part)
            probs = un[:, :, :].rearrange("p t d -> p (t d)")
        with ExitStack() as part:
            yh = sb("yh", [P, D], F32R, part)
            yl = sb("yl", [P, D], F32R, part)
        keep_un = ctx.enter_context(nc.sbuf_tensor("keep_un", [P, TT, D], F32))

        with ExitStack() as part:
            glu = sb("glu", [P, 2, CONV - 1 + S], F32, part)
            gsig = sb("gsig", [P, 2, S], F32, part)
            cacc = sb("cacc", [P, 2, S], F32, part)
            qkpre = sb("qkpre", [P, 4, MCONV - 1 + S], F32, part)
            qkc = sb("qkc", [P, 4, S], F32, part)
            vaug = sb("vaug", [P, TT, HEADS, DH + 1], F32, part)
            osig = sb("osig", [P, TT, 256], F32, part)
            zif = sb("zif", [P, TT, 200], F32, part)
            zkv = sb("zkv", [P, TT, 176], F32, part)
            aT = sb("aT", [16, S], F32, part)
            gqk = sb("gqk", [P, 2, S], F32, part)
            gv = sb("gv", [P, TT, 256], F32, part)
            grs = sb("grs", [P, TT, 256], F32, part)
            size_b = 4 * (2 * (CONV - 1 + S) + 4 * S + 4 * (MCONV - 1 + S) + 4 * S + 2 * 260 + 512
                          + 400 + 352 + S + 2 * S + 512 + 512)
        with ExitStack() as part:
            moe_g = sb("moe_g", [P, D], F32, part)
        with ExitStack() as part:
            sg = sb("sg", [P, TT, 256], F32, part)
            hid = sb("hid", [P, TT, 256], F32, part)
            hTh = sb("hTh", [P, 2, TT, P], F32R, part)
            hTl = sb("hTl", [P, 2, TT, P], F32R, part)
            unh = sb("unh", [P, TT, D], F32R, part)
            unl = sb("unl", [P, TT, D], F32R, part)
            sel = sb("sel", [P, TT, P], F32R, part)
            selT = sb("selT", [P, TT, P], F32R, part)
            size_f = 4 * (512 + 512 + 512 + 512 + 4096 + 256 + 256)
        ctx.enter_context(nc.sbuf_tensor("keep_b", [P, max(size_b, size_f) // 4 + 8], F32))

        with ExitStack() as part:
            y = sb("y", [P, TT, D], F32, part)
            stage = y[:, 0, 0:2 * P].rearrange("p (a n) -> p a n", a=2)
            gb = sb("gb", [P, TT, 8], F32, part)
            gmn = sb("gmn", [P, TT, 4], F32, part)
            gab = sb("gab", [P, TT, 4], F32, part)
            gln = sb("gln", [P, TT, 4], F32, part)
            cumf = sb("cumf", [4, S], F32, part)
            aj = sb("aj", [4, S], F32, part)
            mrun = sb("mrun", [4, S], F32, part)
            negm = sb("negm", [4, S], F32, part)
            expnm = sb("expnm", [4, S], F32, part)
            mcol = sb("mcol", [P, 16], F32, part)
            dec = sb("dec", [P, HEADS, 384], F32, part)
            mden = sb("mden", [P, TT, HEADS], F32, part)
            uq = sb("uq", [P, 2, 384], F32, part)
            ukv = sb("ukv", [P, 512], F32, part)
            walpha = sb("walpha", [16, P], F32, part)
            lss = sb("lss", [P, 2, TT], F32, part)
            lln = sb("lln", [P, 2, TT], F32, part)
            lrs = sb("lrs", [P, 2, TT], F32, part)
            cqT = sb("cqT", [P, 2, S], F32, part)
            ckvT = sb("ckvT", [P, S], F32, part)
            qtok = sb("qtok", [P, TT, HEADS, 96], F32, part)
            ktok = sb("ktok", [P, TT, HEADS, 96], F32, part)
            rin = sb("rin", [P, TT, 5, 32], F32, part)
            rot = sb("rot", [P, TT, 5, 32], F32, part)
            rt1 = sb("rt1", [P, TT, 5, 16], F32, part)
            rt2 = sb("rt2", [P, TT, 5, 16], F32, part)
            vm = sb("vm", [P, TT, 256], F32, part)
            qT = sb("qT", [96, HEADS, S], F32, part)
            kT = sb("kT", [96, HEADS, S], F32, part)
            smax = sb("smax", [P, TT, HEADS], F32, part)
            psums = sb("psums", [P, TT, HEADS], F32, part)
            gx = sb("gx", [P, S], F32, part)
            gmn2 = sb("gmn2", [P, S], F32, part)
            gab2 = sb("gab2", [P, S], F32, part)
            b16 = gx
            gref = sb("gref", [P, 2, 2], F32, part)
            gE = sb("gE", [P, 5, P], F32, part)
            gS = sb("gS", [P, HEADS, 3, P], F32, part)
            probT = gS[:, :, :, :].rearrange("p h b n -> p (h b n)").rearrange("p (b h n) -> p b h n", b=3, h=HEADS)
            osq = sb("osq", [P, TT, HEADS, DH], F32, part)
            gss = sb("gss", [P, TT, HEADS], F32, part)
            gls = sb("gls", [P, TT, HEADS], F32, part)
            grd = sb("grd", [P, TT, HEADS], F32, part)
            ctok = cqT[:, :, :]
            bst = sb("bst", [P, TT, 6], F32, part)
            bag = sb("bag", [P, TT, 2], F32, part)
        uTh = sb("uTh", [P, KD, S], F32R)
        uTl = sb("uTl", [P, KD, S], F32R)
        high = sb("high", [P, SPLIT, PIECE], F32R)
        low = sb("low", [P, SPLIT, PIECE], F32R)

        bank = [ctx.enter_context(nc.psum_tensor(f"bank{i}", [P, 512], F32)) for i in range(8)]
        NORM_BANKS = (0, 1, 4, 7)
        Z_BANKS = (2, 3, 5, 6)

        fin_g = ring[:, 0, 0:D]
        xh, xl = uTh[:, :, 0:P], uTl[:, :, 0:P]

        sems = {}
        for name in (
                "x_in", "pos_in", "rows_in", "gateb_in", "ln_in", "router_in", "moe_g_in", "ung_ready", "ukv_in", "final_in",
                "consts", "cols_tr", "cols_ready", "ang_ready", "sin_ready",
                "high_ready", "low_ready", "piece_used",
                "h_ready", "rstd_ready", "un_ready", "norm_tr", "uth_ready", "utl_ready",
                "z_act", "z_dve", "qk_conv", "qk_sig", "qk_ready", "conv_done",
                "lat_rstd", "lat_ready", "lat_tr", "lat_T", "gates_abs", "gates_ln", "lf_ready",
                "gate_tr", "gpre_ready", "gla_abs", "gla_ln", "gla_cum", "mcum_ready", "expnm_ready",
                "mcol_tr", "mcol_ready", "q_ready", "kv_ready", "qkv_evac", "rot_ready",
                "gla_exp", "gla_qk", "x_ready", "s_ready", "dt_ready", "pt_ready", "num_ready",
                "y_m", "qkT_tr", "qT_ready", "kT_ready", "sc_ready", "smax_ready", "p_ready",
                "p_tr", "pT_ready", "pv_ready", "y_a", "ga_ready", "gs_ready", "go_ready",
                "osq_ready", "gss_ready", "grd_ready", "y_g", "conf_tr", "bn_ready", "conf_rstd",
                "conf_n", "conf_ln", "conf_sig", "y_c",
                "silu_ready", "hid_ready", "hid_tr", "hTh_ready",
                "hTl_ready", "logit_ready", "gap_ready", "egap_ready", "routed_ready",
                "rank_ready", "jobs_ready", "unh_ready", "unl_ready", "key_copied", "sel_ready",
                "gath_ready", "xh_ready", "xl_ready", "selT_ready", "yh_ready", "yl_ready",
                "scat_ready", "added", "out_ready", "stored",
                "aT_tr", "act_chain", "dve_chain", "pool_chain"):
            sems[name] = ctx.enter_context(nc.semaphore(name))
        loaded = [ctx.enter_context(nc.semaphore(f"loaded{i}")) for i in range(RING)]
        s = sems

        def bc(ap, shape):
            return ap.to_broadcast(shape)

        def col(i):
            return cols[:, i // P, i % P:i % P + 1]

        NORM1, NORM2, FUSE, CONVB, MCONVB, MCONVW, GLAB, KVG, QG1, QG2 = 0, 16, 32, 48, 52, 60, 92, 94, 96, 98
        CONVW = P

        def slot(n):
            return ring[:, n % RING, :]

        def jobs(eng, body):
            with eng.Fori(0, E) as j:
                body(j)
            eng.wait_ge(s["jobs_ready"], 1)
            n_over = eng.value_load(jobs_i[0:1, 3:4], min_val=0, max_val=OVER)
            with eng.If(n_over > 0):
                with eng.Fori(E, n_over + E) as j:
                    body(j)

        block = ctx.enter_context(nc.Block())

        @block.sync
        def _(sp):
            def load(n, dst_src, rounds=None):
                if rounds is not None:
                    sp.wait_ge(s["low_ready"], rounds * N_FFN + (n - RING + 1))
                elif n >= RING:
                    sp.wait_ge(s["low_ready"], n - RING + 1)
                assert len(dst_src) == 2
                for dst, src in dst_src:
                    sp.dma_start(dst, src).then_inc(loaded[n % RING], 16)

            def load_in(l, p):
                n = LAYER_PIECES[l] + p
                segs = W_IN_PIECES[p]
                width = sum(w for _, w in segs)
                dst = slot(n)[:, 0:KD * width].rearrange("p (k n) -> p k n", k=KD)
                src = w_in[l].rearrange("(k p) n -> p k n", p=P)
                if len(segs) == 2:
                    (c0, a), (c1, b) = segs
                    load(n, [(dst[:, :, 0:a], src[:, :, c0:c0 + a]),
                             (dst[:, :, a:a + b], src[:, :, c1:c1 + b])])
                else:
                    c0, a = segs[0]
                    half = KD // 2
                    load(n, [(dst[:, i:i + half, :], src[:, i:i + half, c0:c0 + a]) for i in (0, half)])

            def load_out(l, p):
                n = LAYER_PIECES[l] + N_IN + p
                dst = slot(n).rearrange("p (k n) -> p k n", k=2)
                src = w_out[l].rearrange("(k p) n -> p k n", p=P)
                load(n, [(dst[:, i:i + 1, :], src[:, 2 * p + i:2 * p + i + 1, :]) for i in (0, 1)])

            def load_ffn(n0, wg, wu, wd, rounds=None):
                for i, (kind, c) in enumerate(FFN_ORDER):
                    n = n0 + i
                    if kind == "d":
                        dst = slot(n).rearrange("p (f n) -> p f n", f=2)
                        src = wd.rearrange("(f p) n -> p f n", p=P)
                        load(n, [(dst[:, f:f + 1, :], src[:, 2 * c + f:2 * c + f + 1, :]) for f in (0, 1)], rounds)
                    else:
                        dst = slot(n).rearrange("p (k n) -> p k n", k=4)
                        k0 = 0 if kind == "a" else 4
                        load(n, [(dst[:, :, g * 256:(g + 1) * 256],
                                  w.rearrange("(k p) n -> p k n", p=P)[:, k0:k0 + 4, c * F_CH:(c + 1) * F_CH])
                                 for g, w in enumerate((wg, wu))], rounds)

            for t in range(TT):
                sp.dma_start(h[:, t, :], x[0, t * P:(t + 1) * P, :]).then_inc(s["x_in"], 16)
            for p in range(RING):
                load_in(0, p)
            for p in range(N_OUT):
                load_out(0, p)
            load_ffn(DENSE0, ffn_w_gate[0], ffn_w_up[0], ffn_w_down[0])
            for p in range(N_IN):
                load_in(1, p)
            for p in range(N_OUT):
                load_out(1, p)

            def expert(e, j):
                pick_e = lambda w: w[0, bass.ds(e, 1)].rearrange("a k n -> (a k) n")
                load_ffn(MOE0, pick_e(moe_w_gate), pick_e(moe_w_up), pick_e(moe_w_down), j)

            with sp.Fori(0, E) as j:
                expert(j, j)
            sp.wait_ge(s["jobs_ready"], 1)
            n_over = sp.value_load(jobs_i[0:1, 3:4], min_val=0, max_val=OVER)
            with sp.If(n_over > 0):
                with sp.Fori(0, n_over) as o:
                    e = sp.value_load(jobs_i[0:1, bass.ds(o, 1)], min_val=0, max_val=E - 1)
                    expert(e, o + E)
            sp.wait_ge(s["h_ready"], 4)
            sp.dma_start(fin_g, bc(final_norm_g.rearrange("(a d) -> a d", a=1), [P, D])).then_inc(s["final_in"], 16)
            sp.wait_ge(s["out_ready"], 1)
            sp.dma_start(out[0].rearrange("(t p) d -> p t d", p=P), h[:, :, :]).then_inc(s["stored"], 16)
            sp.wait_ge(s["stored"], 16)

        @block.gpsimd
        def _(pool):
            chain = Chain(pool, s["pool_chain"])
            pool.dma_start(pos_i[:, :], positions.rearrange("a (t p) -> p (a t)", p=P), allow_slow_non_contiguous=True).then_inc(s["pos_in"], 16)
            chain.done(pool.memset(stage[:, :, :], 0.0))
            chain.wait()
            rows = lambda i, n: stage[i:i + n, 0, :]
            groups = [
                (rows(NORM1, 16), norm1_g.rearrange("l (k p) -> (l k) p", p=P)),
                (rows(NORM2, 16), norm2_g.rearrange("l (k p) -> (l k) p", p=P)),
                (rows(FUSE, 16), fuse_g.rearrange("l (k p) -> (l k) p", p=P)),
                (rows(CONVB, 4), conv_b.rearrange("l (k p) -> (l k) p", p=P)),
                (rows(MCONVB, 8), mlstm_conv_b.rearrange("l (k p) -> (l k) p", p=P)),
                (rows(MCONVW, 32), mlstm_conv_w.rearrange("l i (k p) -> (l i k) p", p=P)),
                (rows(GLAB, 2), gla_b_alpha),
                (rows(KVG, 2), mla_kv_norm_g),
                (rows(QG1, 2), mla_q_norm_g[:, 0:P]),
                (stage[QG2:QG2 + 2, 0, 0:64], mla_q_norm_g[:, P:192]),
                (stage[0:2 * CONV * DEPTH, 1, :], conv_w.rearrange("l i (k p) -> (l i k) p", p=P)),
            ]
            for dst, src in groups:
                pool.dma_start(dst, src).then_inc(s["rows_in"], 16)
            for l in range(DEPTH):
                pool.dma_start(gate_b[:, l, :], bc(mlstm_gate_b[l:l + 1, :], [P, 8])).then_inc(s["gateb_in"], 16)
            pool.dma_start(router[:, :, :], moe_router[0].rearrange("(k p) e -> p k e", p=P)).then_inc(s["router_in"], 16)
            fills = [pool.memset(ident[:, :], 0.0), pool.memset(ones[:, :], 1.0), pool.memset(epst[:, :], EPS),
                     pool.memset(mask_kt[:, :], 0.0), pool.memset(mask_qt[:, :], 0.0),
                     pool.memset(gla_mask[:, :, :], 32.0 ** -0.5), pool.memset(before[:, :], 1.0)]
            for i in range(16):
                pool.memset(invf[:, i:i + 1], float(np.float32(1.0) / np.float32(10000.0) ** np.float32(i / 16)))
            chain.done(pool.iota(iota[:, :], [[1, P]], base=0, channel_multiplier=0,
                                 allow_small_or_imprecise_dtypes=True))
            chain.wait()
            pool.affine_select(out=ident[:, :], in_=ident[:, :], compare_op=ALU.not_equal, fill=1.0,
                               base=0, pattern=[[-1, P]], channel_multiplier=1)
            pool.affine_select(out=mask_kt[:, :], in_=mask_kt[:, :], compare_op=ALU.is_ge, fill=NEG,
                               base=0, pattern=[[1, P]], channel_multiplier=-1)
            pool.affine_select(out=mask_qt[:, :], in_=mask_qt[:, :], compare_op=ALU.is_ge, fill=NEG,
                               base=0, pattern=[[-1, P]], channel_multiplier=1)
            for b in (0, 2):
                pool.affine_select(out=gla_mask[:, b, :], in_=gla_mask[:, b, :], compare_op=ALU.is_ge, fill=0.0,
                                   base=0, pattern=[[1, P]], channel_multiplier=-1)
            pool.affine_select(out=before[:, :], in_=before[:, :], compare_op=ALU.is_ge, fill=0.0,
                               base=-1, pattern=[[1, P]], channel_multiplier=-1).then_inc(s["consts"], 1)

            for l in range(DEPTH):
                if l:
                    pool.wait_ge(s["conf_ln"], l)
                for i, src in enumerate((conv_ln_g, conv_ln_b)):
                    pool.dma_start(ln_gb[:, i, :], bc(src[l:l + 1, :], [P, 256])).then_inc(s["ln_in"], 16)
                pool.wait_ge(s["qk_sig"], l + 1)
                pool.tensor_tensor(qkc[:, :, :], qkc[:, :, :], qkpre[:, :, 0:S], ALU.mult).then_inc(s["qk_ready"], 1)
                pool.wait_ge(s["piece_used"], LAYER_PIECES[l] + N_IN)
                pool.dma_start(walpha[:, :], gla_w_alpha[l]).then_inc(s["ukv_in"], 16)
                pool.dma_start(uq[:, 0, :], mla_w_uq[l, 0:P, :]).then_inc(s["ukv_in"], 16)
                pool.dma_start(uq[0:64, 1, :], mla_w_uq[l, P:192, :]).then_inc(s["ukv_in"], 16)
                pool.dma_start(ukv[:, :], mla_w_ukv[l]).then_inc(s["ukv_in"], 16)
                pool.wait_ge(s["gla_exp"], l + 1)
                q, k = gqk[:, 0, :], gqk[:, 1, :]
                for i, part in enumerate((q[:, 0:P], q[:, P:S], k[:, 0:P], k[:, 0:P], k[:, P:S])):
                    last = pool.tensor_tensor(gE[:, i, :], gE[:, i, :], part, ALU.mult)
                last.then_inc(s["gla_qk"], 1)
                pool.wait_ge(s["ln_in"], 32 * (l + 1))
                pool.wait_ge(s["conf_n"], l + 1)
                chain.done(pool.tensor_tensor(ctok[:, :, :], ctok[:, :, :],
                                              bc(ln_gb[:, 0:1, :], [P, TT, 256]), ALU.mult))
                chain.wait()
                pool.tensor_tensor(ctok[:, :, :], ctok[:, :, :], bc(ln_gb[:, 1:2, :], [P, TT, 256]),
                                   ALU.add).then_inc(s["conf_ln"], 1)
            for name in ("y_m", "y_a", "y_g", "y_c"):
                pool.wait_ge(s[name], DEPTH)
            pool.dma_start(moe_g[:, :], bc(norm2_g[DEPTH - 1:DEPTH, :], [P, D])).then_inc(s["moe_g_in"], 16)

        @block.scalar
        def _(act):
            chain = Chain(act, s["act_chain"])
            next_piece = [0]

            def split_high(n, job=None, width=PIECE):
                jobbed = job is not None
                rounds, pieces = (3 * job, N_FFN * job) if jobbed else (0, 0)
                act.wait_ge(loaded[n % RING], 32 * rounds + 32 * (n // RING + 1))
                if jobbed or n >= SPLIT:
                    act.wait_ge(s["piece_used"], pieces + (n - SPLIT + 1))
                act.activation(high[:, n % SPLIT, 0:width], slot(n)[:, 0:width], ACT.Copy).then_inc(s["high_ready"], 1)

            def in_width(p):
                return KD * sum(w for _, w in W_IN_PIECES[p])

            def norm(k, source, groups, wait):
                wait()
                w = D // groups
                for t in range(TT):
                    for g in range(groups):
                        chain.done(act.activation(un[:, t, g * w:(g + 1) * w], source[:, t, g * w:(g + 1) * w],
                                                  ACT.Square, accum_out=ss[:, t, g:g + 1]))
                chain.wait()
                chain.done(act.activation(lnv[:, :, 0:groups], ss[:, :, 0:groups], ACT.Ln, bias=epst[:, :], scale=1.0 / w))
                chain.wait()
                act.activation(rstd[:, :, 0:groups], lnv[:, :, 0:groups], ACT.Exp, scale=-0.5).then_inc(s["rstd_ready"], 1)

            def gains(k, first):
                for g in range(4):
                    act.wait_ge(s["norm_tr"], 4 * k + g + 1)
                    for i in range(2):
                        kd = 2 * g + i
                        last = act.activation(uTh[:, kd, :], bank[NORM_BANKS[g]][:, i * S:(i + 1) * S], ACT.Copy,
                                              scale=col(first + kd))
                    last.then_inc(s["uth_ready"], 1)

            def ffn(n0, job, job_n, tiles):
                done = [0]

                def upto(i):
                    while done[0] <= min(i, N_FFN - 1):
                        split_high(n0 + done[0], job)
                        done[0] += 1

                for c in range(CHUNKS):
                    at = FFN_AT[("b", c)]
                    upto(at + 2)
                    act.wait_ge(s["piece_used"], (N_FFN * job if job is not None else 0) + (n0 + at + 1))
                    for t in range(tiles):
                        last = act.activation(sg[:, t, :], bank[t][:, 0:256], ACT.Silu)
                    last.then_inc(s["silu_ready"], 1)
                    upto(at + 3)
                    act.wait_ge(s["hid_tr"], job_n * CHUNKS + (c + 1))
                    act.activation(hTh[:, :, 0:tiles, :],
                                   bank[4][:, 0:2 * tiles * P].rearrange("p (f t n) -> p f t n", f=2, t=tiles),
                                   ACT.Copy).then_inc(s["hTh_ready"], 1)

            act.wait_ge(s["x_in"], 32)
            act.wait_ge(s["consts"], 1)
            for l in range(DEPTH):
                n0 = LAYER_PIECES[l]
                norm(3 * l, h, 1, (lambda: act.wait_ge(s["h_ready"], 2)) if l else (lambda: None))
                if l == 0:
                    act.wait_ge(s["cols_ready"], 1)
                gains(3 * l, NORM1 + KD * l)
                for n in range(SPLIT):
                    split_high(n0 + n, width=in_width(n))
                for p in range(N_IN):
                    if p + SPLIT < N_IN:
                        split_high(n0 + p + SPLIT, width=in_width(p + SPLIT))
                    src = bank[Z_BANKS[p % 4]]
                    tiles2 = lambda w: src[:, 0:TT * w].rearrange("p (t n) -> p t n", t=TT)
                    if p in (1, 4, 5, 6, 7, 8, 9, 10):
                        act.wait_ge(s["piece_used"], n0 + p + 1)
                    if p == 1:
                        act.activation(gsig[:, :, :], tiles2(256), ACT.Sigmoid).then_inc(s["z_act"], 1)
                    if p == 4:
                        act.activation(zif[:, :, :], tiles2(200), ACT.Copy).then_inc(s["z_act"], 1)
                    if p == 5:
                        act.activation(zkv[:, :, :], tiles2(176), ACT.Copy).then_inc(s["z_act"], 1)
                    if p == 6:
                        act.wait_ge(s["aT_tr"], l + 1)
                        act.activation(aT[:, :], bank[7][0:16, 0:S], ACT.Copy).then_inc(s["z_act"], 1)
                        act.activation(gqk[:, :, :], tiles2(256), ACT.Copy).then_inc(s["z_act"], 1)
                    if p == 7:
                        act.activation(vaug[:, :, :, 0:DH], src[:, :].rearrange("p (t h n) -> p t h n", t=TT, h=HEADS),
                                       ACT.Copy).then_inc(s["z_act"], 1)
                        act.wait_ge(s["qk_conv"], l + 1)
                        act.activation(qkpre[:, :, 0:S], qkc[:, :, :], ACT.Sigmoid).then_inc(s["qk_sig"], 1)
                    if p == 8:
                        act.activation(osig[:, :, :], tiles2(256), ACT.Sigmoid).then_inc(s["z_act"], 1)
                    if p == 9:
                        act.activation(gv[:, :, :], tiles2(256), ACT.Copy).then_inc(s["z_act"], 1)
                    if p == 10:
                        act.activation(grs[:, :, :], tiles2(256), ACT.Sigmoid).then_inc(s["z_act"], 1)

                if l == 0:
                    act.wait_ge(s["ang_ready"], 1)
                    act.activation(cossin[:, :, :, :], ang[:, :, :, :], ACT.Sin).then_inc(s["sin_ready"], 1)
                for t in range(TT):
                    chain.done(act.activation(qtok[:, t, :, :].rearrange("p h n -> p (h n)")[:, 0:192],
                                              zif[:, t, 8:200], ACT.Square, accum_out=lss[:, 0, t:t + 1]))
                    chain.done(act.activation(ktok[:, t, :, :].rearrange("p h n -> p (h n)")[:, 0:128],
                                              zkv[:, t, 0:128], ACT.Square, accum_out=lss[:, 1, t:t + 1]))
                chain.wait()
                chain.done(act.activation(lln[:, 0, :], lss[:, 0, :], ACT.Ln, bias=epst[:, :], scale=1.0 / 192))
                chain.done(act.activation(lln[:, 1, :], lss[:, 1, :], ACT.Ln, bias=epst[:, :], scale=1.0 / 128))
                chain.wait()
                act.activation(lrs[:, :, :], lln[:, :, :], ACT.Exp, scale=-0.5).then_inc(s["lat_rstd"], 1)
                act.wait_ge(s["gates_abs"], l + 1)
                chain.done(act.activation(gln[:, :, :], gab[:, :, :], ACT.Exp))
                chain.wait()
                act.activation(gln[:, :, :], gln[:, :, :], ACT.Ln, bias=1.0).then_inc(s["gates_ln"], 1)
                act.wait_ge(s["gla_abs"], l + 1)
                chain.done(act.activation(gab2[:, :], gab2[:, :], ACT.Exp))
                chain.wait()
                act.activation(gab2[:, :], gab2[:, :], ACT.Ln, bias=1.0).then_inc(s["gla_ln"], 1)
                act.wait_ge(s["mcum_ready"], l + 1)
                act.activation(expnm[:, :], mrun[:, :], ACT.Exp, scale=-1.0).then_inc(s["expnm_ready"], 1)
                act.wait_ge(s["q_ready"], l + 1)
                for t in range(TT):
                    src = bank[(3, 5)[t]][:, 0:384].rearrange("p (h n) -> p h n", h=HEADS)
                    act.activation(rin[:, t, 0:4, :], src[:, :, 64:96], ACT.Copy)
                    act.activation(qtok[:, t, :, 0:64], src[:, :, 0:64], ACT.Copy)
                act.activation(rin[:, :, 4, :], zkv[:, :, 128:160], ACT.Copy)
                act.wait_ge(s["kv_ready"], l + 1)
                for t in range(TT):
                    src = bank[(6, 1)[t]][:, :].rearrange("p (h n) -> p h n", h=HEADS)
                    act.activation(ktok[:, t, :, 0:64], src[:, :, 0:64], ACT.Copy)
                    last = act.activation(vm[:, t, :].rearrange("p (h n) -> p h n", h=HEADS), src[:, :, 64:128], ACT.Copy)
                last.then_inc(s["qkv_evac"], 1)
                act.wait_ge(s["gla_cum"], l + 1)
                for i in range(2):
                    act.activation(gE[:, i, :], b16[:, i * P:(i + 1) * P], ACT.Exp, bias=gref[:, 0, i:i + 1], scale=1.0 / 16)
                act.activation(gE[:, 2, :], b16[:, 0:P], ACT.Exp, bias=gref[:, 1, 0:1], scale=-1.0 / 16)
                act.activation(gE[:, 3:5, :].rearrange("p a n -> p (a n)"), b16[:, :], ACT.Exp,
                               bias=gref[:, 1, 1:2], scale=-1.0 / 16).then_inc(s["gla_exp"], 1)
                act.wait_ge(s["mcol_ready"], l + 1)
                for hd in range(HEADS):
                    act.wait_ge(s["x_ready"], HEADS * l + hd + 1)
                    xb = bank[(2, 4, 7, 0)[hd]]
                    act.activation(dec[:, hd, 0:256], xb[:, 0:256], ACT.Exp, bias=mcol[:, hd:hd + 1])
                    act.activation(dec[:, hd, 256:384], xb[:, 256:384], ACT.Exp,
                                   bias=mcol[:, 4 + hd:5 + hd]).then_inc(s["dt_ready"], 1)
                for i in range(2):
                    act.wait_ge(s["qkT_tr"], 4 * l + i + 1)
                    act.activation(qT[:, 2 * i:2 * i + 2, :], bank[(2, 4)[i]][0:96, :].rearrange("p (h n) -> p h n", h=2),
                                   ACT.Copy).then_inc(s["qT_ready"], 1)
                act.wait_ge(s["bn_ready"], l + 1)
                chain.done(act.activation(bst[:, :, 0], bag[:, :, 1], ACT.Ln, bias=epst[:, :]))
                chain.wait()
                act.activation(bst[:, :, 1], bst[:, :, 0], ACT.Exp, scale=-0.5).then_inc(s["conf_rstd"], 1)
                act.wait_ge(s["smax_ready"], l + 1)
                scale = 96.0 ** -0.5
                for hd in range(HEADS):
                    chain.done(act.activation(probs[:, hd * P:(hd + 1) * P], bank[6][:, hd * P:(hd + 1) * P], ACT.Exp,
                                              bias=smax[:, 0, hd:hd + 1], scale=scale, accum_out=psums[:, 0, hd:hd + 1]))
                for hd in range(HEADS):
                    src = bank[(0, 1)[hd // 2]][:, (hd % 2) * S:(hd % 2 + 1) * S]
                    last = act.activation(probs[:, 512 + hd * S:512 + (hd + 1) * S], src, ACT.Exp,
                                          bias=smax[:, 1, hd:hd + 1], scale=scale, accum_out=psums[:, 1, hd:hd + 1])
                last.then_inc(s["p_ready"], 1)
                act.wait_ge(s["go_ready"], l + 1)
                act.activation(osq[:, :, :, :].rearrange("p t h n -> p (t h n)"), bank[7][:, :],
                               ACT.Square).then_inc(s["osq_ready"], 1)
                act.wait_ge(s["gss_ready"], l + 1)
                chain.done(act.activation(gls[:, :, :], gss[:, :, :], ACT.Ln, bias=epst[:, :], scale=1.0 / DH))
                chain.wait()
                act.activation(grd[:, :, :], gls[:, :, :], ACT.Exp, scale=-0.5).then_inc(s["grd_ready"], 1)
                for i in range(3):
                    act.wait_ge(s["p_tr"], 3 * l + i + 1)
                    act.activation(probT[:, i, :, :], bank[(3, 5, 6)[i]][:, :].rearrange("p (h n) -> p h n", h=HEADS),
                                   ACT.Copy).then_inc(s["pT_ready"], 1)
                act.wait_ge(s["conf_ln"], l + 1)
                act.activation(cacc[:, :, :], ctok[:, :, :],
                               ACT.Sigmoid).then_inc(s["conf_sig"], 1)

                def mixers_done():
                    for name in ("y_m", "y_a", "y_g", "y_c"):
                        act.wait_ge(s[name], l + 1)
                norm(3 * l + 1, y, 4, mixers_done)
                for n in range(SPLIT):
                    split_high(n0 + N_IN + n)
                gains(3 * l + 1, FUSE + KD * l)
                split_high(n0 + N_IN + SPLIT)
                norm(3 * l + 2, h, 1, lambda: act.wait_ge(s["h_ready"], 2 * l + 1))
                gains(3 * l + 2, NORM2 + KD * l)
                if l == 0:
                    ffn(DENSE0, None, 0, TT)

            act.wait_ge(s["ung_ready"], 1)
            act.activation(unh[:, :, :], un[:, :, :], ACT.Copy).then_inc(s["unh_ready"], 1)
            act.wait_ge(s["gap_ready"], 1)
            act.activation(egap[:, :], gap[:, :], ACT.Exp).then_inc(s["egap_ready"], 1)

            def job(j):
                act.wait_ge(s["gath_ready"], j + 1)
                for i in range(2):
                    last = act.activation(xh[:, 4 * i:4 * i + 4, :], bank[5 + i][:, :].rearrange("p (k n) -> p k n", k=4), ACT.Copy)
                last.then_inc(s["xh_ready"], 1)
                ffn(MOE0, j, j + 1, 1)
                act.wait_ge(s["piece_used"], N_FFN * j + (MOE0 + N_FFN))
                for i in range(2):
                    last = act.activation(yh[:, i * 512:(i + 1) * 512], bank[2 + i][:, :], ACT.Copy, scale=wslot[:, :])
                last.then_inc(s["yh_ready"], 1)

            jobs(act, job)
            norm(6, h, 1, lambda: act.wait_ge(s["h_ready"], 4))

        @block.vector
        def _(dve):
            chain = Chain(dve, s["dve_chain"])

            def split_low(n, job=None, width=PIECE):
                pieces = N_FFN * job if job is not None else 0
                dve.wait_ge(s["high_ready"], pieces + (n + 1))
                dve.tensor_tensor(low[:, n % SPLIT, 0:width], slot(n)[:, 0:width],
                                  high[:, n % SPLIT, 0:width].bitcast(F32), ALU.subtract).then_inc(s["low_ready"], 1)

            def in_width(p):
                return KD * sum(w for _, w in W_IN_PIECES[p])

            def normalize(k, source, groups):
                dve.wait_ge(s["rstd_ready"], k + 1)
                if groups == 1:
                    for t in range(TT):
                        last = dve.tensor_scalar(un[:, t, :], source[:, t, :], rstd[:, t, 0:1], None, ALU.mult)
                else:
                    w = D // groups
                    last = dve.tensor_tensor(
                        un[:, :, :].rearrange("p t (g n) -> p (t g) n", g=groups),
                        source[:, :, :].rearrange("p t (g n) -> p (t g) n", g=groups),
                        bc(rstd[:, :, :].rearrange("p t g -> p (t g)").unsqueeze(2), [P, TT * groups, w]), ALU.mult)
                last.then_inc(s["un_ready"], 1)

            def gains(k, first):
                for g in range(4):
                    dve.wait_ge(s["uth_ready"], 4 * k + g + 1)
                    for i in range(2):
                        kd = 2 * g + i
                        last = dve.scalar_tensor_tensor(
                            out=uTl[:, kd, :], in0=bank[NORM_BANKS[g]][:, i * S:(i + 1) * S], scalar=col(first + kd),
                            in1=uTh[:, kd, :].bitcast(F32), op0=ALU.mult, op1=ALU.subtract)
                    last.then_inc(s["utl_ready"], 1)

            def ffn(n0, job, job_n, tiles):
                done = [0]

                def upto(i):
                    while done[0] <= min(i, N_FFN - 1):
                        split_low(n0 + done[0], job)
                        done[0] += 1

                for c in range(CHUNKS):
                    at = FFN_AT[("b", c)]
                    upto(at + 2)
                    dve.wait_ge(s["silu_ready"], job_n * CHUNKS + (c + 1))
                    for t in range(tiles):
                        last = dve.tensor_tensor(hid[:, t, :], bank[t][:, 256:512], sg[:, t, :], ALU.mult)
                    last.then_inc(s["hid_ready"], 1)
                    upto(at + 3)
                    dve.wait_ge(s["hTh_ready"], job_n * CHUNKS + (c + 1))
                    dve.tensor_tensor(hTl[:, :, 0:tiles, :],
                                      bank[4][:, 0:2 * tiles * P].rearrange("p (f t n) -> p f t n", f=2, t=tiles),
                                      hTh[:, :, 0:tiles, :].bitcast(F32), ALU.subtract).then_inc(s["hTl_ready"], 1)

            def add_to_h(banks, sem, values):
                for i, b in enumerate(banks):
                    t, half = divmod(i, 2)
                    dve.wait_ge(sem, values[i])
                    dst = h[:, t, half * 512:(half + 1) * 512]
                    last = dve.tensor_tensor(dst, bank[b][:, :], dst, ALU.add)
                return last

            def angles():
                c1 = 6.28125
                c2 = float(np.float32(2 * math.pi - c1))
                c3 = 2 * math.pi - c1 - c2
                magic = 1.5 * 2.0 ** 23
                dve.wait_ge(s["pos_in"], 16)
                chain.done(dve.tensor_copy(pos_f[:, :], pos_i[:, :]))
                chain.wait()
                for i in range(2):
                    for t in range(TT):
                        chain.done(dve.tensor_scalar(ang[:, i, t, :], invf[:, :], pos_f[:, t:t + 1], None, ALU.mult))
                chain.wait()
                for i in range(2):
                    chain.done(dve.tensor_scalar(turn[:, i, :, :], ang[:, i, :, :], 1 / (2 * math.pi),
                                                 0.0 if i else 0.25, ALU.mult, ALU.add))
                chain.wait()
                for v in (magic, -magic):
                    chain.done(dve.tensor_scalar(turn[:, :, :, :], turn[:, :, :, :], v, None, ALU.add))
                    chain.wait()
                flat = lambda a: a[:, :, :, :].rearrange("p i t n -> p (i t n)")
                for c in (c1, c2, c3):
                    chain.done(dve.scalar_tensor_tensor(out=flat(ang), in0=flat(turn), scalar=-c, in1=flat(ang),
                                                        op0=ALU.mult, op1=ALU.add))
                    chain.wait()
                chain.done(dve.tensor_scalar(ang[:, 0, :, :], ang[:, 0, :, :], math.pi / 2, None, ALU.add))
                chain.wait()
                lim = float(np.nextafter(np.float32(math.pi), np.float32(0)))
                dve.tensor_scalar(flat(ang), flat(ang), lim, -lim, ALU.min, ALU.max).then_inc(s["ang_ready"], 1)

            dve.wait_ge(s["cols_tr"], 1)
            dve.tensor_copy(cols[:, :, :], bank[7][:, 0:2 * P].rearrange("p (a n) -> p a n", a=2)).then_inc(s["cols_ready"], 1)
            dve.wait_ge(s["cols_ready"], 1)
            for l in range(DEPTH):
                n0 = LAYER_PIECES[l]
                normalize(3 * l, h, 1)
                gains(3 * l, NORM1 + KD * l)
                dve.memset(glu[:, :, 0:CONV - 1], 0.0)
                dve.memset(qkpre[:, :, 0:MCONV - 1], 0.0)
                chain.done(dve.memset(vaug[:, :, :, DH:DH + 1], 1.0))
                for n in range(SPLIT):
                    split_low(n0 + n, width=in_width(n))

                def conv_step(i):
                    tap, c = divmod(i, 2)
                    taps = glu[:, c, tap:tap + S]
                    w = col(CONVW + (l * CONV + tap) * 2 + c)
                    chain.wait(1)
                    if tap == 0:
                        ins = dve.tensor_scalar(cacc[:, c, :], taps, w, col(CONVB + 2 * l + c), ALU.mult, ALU.add)
                    else:
                        ins = dve.scalar_tensor_tensor(out=cacc[:, c, :], in0=taps, scalar=w, in1=cacc[:, c, :],
                                                       op0=ALU.mult, op1=ALU.add)
                    chain.done(ins)
                    if i == 2 * CONV - 1:
                        chain.wait()

                def qk_step(i):
                    tap, c = divmod(i, 4)
                    taps = qkpre[:, c, tap:tap + S]
                    w = col(MCONVW + (l * MCONV + tap) * 4 + c)
                    chain.wait(3)
                    if tap == 0:
                        ins = dve.tensor_scalar(qkc[:, c, :], taps, w, col(MCONVB + 4 * l + c), ALU.mult, ALU.add)
                    else:
                        ins = dve.scalar_tensor_tensor(out=qkc[:, c, :], in0=taps, scalar=w, in1=qkc[:, c, :],
                                                       op0=ALU.mult, op1=ALU.add)
                    chain.done(ins)

                conv_at = [0]

                def conv_steps(n):
                    for _ in range(n):
                        if conv_at[0] < 2 * CONV:
                            conv_step(conv_at[0])
                            conv_at[0] += 1

                for p in range(N_IN):
                    if p + SPLIT < N_IN:
                        split_low(n0 + p + SPLIT, width=in_width(p + SPLIT))
                    src = bank[Z_BANKS[p % 4]]
                    if p == 1:
                        dve.wait_ge(s["z_act"], 9 * l + 1)
                        chain.wait()
                        ins = dve.tensor_tensor(glu[:, :, CONV - 1:], bank[Z_BANKS[0]][:, :].rearrange("p (c n) -> p c n", c=2),
                                                gsig[:, :, :], ALU.mult)
                        ins.then_inc(s["z_dve"], 1)
                        dve.wait_ge(s["z_dve"], 4 * l + 1)
                    if p in (2, 3):
                        dve.wait_ge(s["piece_used"], n0 + p + 1)
                        c = 2 * (p - 2)
                        dve.tensor_copy(qkpre[:, c:c + 2, MCONV - 1:], src[:, :].rearrange("p (c n) -> p c n", c=2)).then_inc(s["z_dve"], 1)
                    if p == 4:
                        dve.wait_ge(s["z_dve"], 4 * l + 3)
                        for i in range(4 * MCONV):
                            qk_step(i)
                        chain.wait()
                        dve.memset(tiny[:, :], 0.0).then_inc(s["qk_conv"], 1)
                    elif p >= 1:
                        conv_steps(8)
                    if p == 10:
                        dve.wait_ge(s["z_act"], 9 * l + 9)
                        dve.tensor_tensor(grs[:, :, :], src[:, :].rearrange("p (t n) -> p t n", t=TT),
                                          grs[:, :, :], ALU.mult).then_inc(s["z_dve"], 1)
                        dve.wait_ge(s["z_dve"], 4 * l + 4)
                conv_steps(2 * CONV)
                if l == 0:
                    angles()
                dve.memset(tiny[:, :], 0.0).then_inc(s["conv_done"], 1)

                dve.wait_ge(s["piece_used"], n0 + N_IN)
                dve.wait_ge(s["gateb_in"], 32)
                chain.done(dve.tensor_tensor(gb[:, :, :], zif[:, :, 0:8], bc(gate_b[:, l:l + 1, :], [P, TT, 8]), ALU.add))
                chain.wait()
                chain.done(dve.tensor_scalar(gmn[:, :, :], gb[:, :, 4:8], 0.0, None, ALU.min))
                chain.done(dve.tensor_scalar(gab[:, :, :], gb[:, :, 4:8], 0.0, None, ALU.max))
                chain.wait()
                dve.tensor_tensor(gab[:, :, :], gmn[:, :, :], gab[:, :, :], ALU.subtract).then_inc(s["gates_abs"], 1)
                dve.wait_ge(s["lat_rstd"], l + 1)
                for t in range(TT):
                    dve.tensor_scalar(zif[:, t, 8:200], zif[:, t, 8:200], lrs[:, 0, t:t + 1], None, ALU.mult)
                    last = dve.tensor_scalar(zkv[:, t, 0:128], zkv[:, t, 0:128], lrs[:, 1, t:t + 1], None, ALU.mult)
                last.then_inc(s["lat_ready"], 1)
                dve.wait_ge(s["gates_ln"], l + 1)
                dve.tensor_tensor(gb[:, :, 4:8], gmn[:, :, :], gln[:, :, :], ALU.subtract).then_inc(s["lf_ready"], 1)
                dve.wait_ge(s["gpre_ready"], l + 1)
                chain.done(dve.tensor_scalar(gx[:, :], bank[0][:, 0:S], col(GLAB + l), None, ALU.add))
                chain.wait()
                chain.done(dve.tensor_scalar(gmn2[:, :], gx[:, :], 0.0, None, ALU.min))
                chain.done(dve.tensor_scalar(gab2[:, :], gx[:, :], 0.0, None, ALU.max))
                chain.wait()
                dve.tensor_tensor(gab2[:, :], gmn2[:, :], gab2[:, :], ALU.subtract).then_inc(s["gla_abs"], 1)
                dve.wait_ge(s["lat_tr"], l + 1)
                dve.tensor_scalar(cqT[:, 0, :], bank[4][:, 0:S], col(QG1 + l), None, ALU.mult)
                dve.tensor_scalar(cqT[0:64, 1, :], bank[4][0:64, S:2 * S], cols[0:64, 0, QG2 + l:QG2 + l + 1], None, ALU.mult)
                dve.tensor_scalar(ckvT[:, :], bank[7][:, 0:S], col(KVG + l), None, ALU.mult).then_inc(s["lat_T"], 1)
                dve.wait_ge(s["gate_tr"], l + 1)
                chain.done(dve.tensor_tensor_scan(cumf[:, :], ones[0:4, :], bank[2][0:4, S:2 * S], 0.0, ALU.mult, ALU.add))
                chain.wait()
                chain.done(dve.tensor_tensor(aj[:, :], bank[2][0:4, 0:S], cumf[:, :], ALU.subtract))
                chain.wait()
                chain.done(dve.tensor_tensor_scan(mrun[:, :], aj[:, :], aj[:, :], 0.0, ALU.max, ALU.max))
                chain.wait()
                dve.tensor_scalar(negm[:, :], mrun[:, :], -1.0, None, ALU.mult)
                dve.tensor_tensor(mrun[:, :], mrun[:, :], cumf[:, :], ALU.add).then_inc(s["mcum_ready"], 1)
                dve.wait_ge(s["gla_ln"], l + 1)
                chain.done(dve.tensor_tensor(gmn2[:, :], gmn2[:, :], gab2[:, :], ALU.subtract))
                chain.wait()
                chain.done(dve.tensor_tensor_scan(b16[:, :], ones[:, :], gmn2[:, :], 0.0, ALU.mult, ALU.add))
                chain.wait()
                for i in range(2):
                    mid = b16[:, i * P + P // 2:i * P + P // 2 + 1]
                    dve.tensor_scalar(gref[:, 0, i:i + 1], mid, -1.0 / 16, None, ALU.mult)
                    last = dve.tensor_scalar(gref[:, 1, i:i + 1], mid, 1.0 / 16, None, ALU.mult)
                last.then_inc(s["gla_cum"], 1)
                dve.wait_ge(s["mcol_tr"], l + 1)
                dve.tensor_copy(mcol[:, :], bank[0][:, 0:16]).then_inc(s["mcol_ready"], 1)
                if l == 0:
                    dve.wait_ge(s["sin_ready"], 1)
                dve.wait_ge(s["qkv_evac"], l + 1)
                cos = bc(cossin[:, 0, :, :].unsqueeze(2), [P, TT, 5, 16])
                sin = bc(cossin[:, 1, :, :].unsqueeze(2), [P, TT, 5, 16])
                x1, x2 = rin[:, :, :, 0:16], rin[:, :, :, 16:32]
                for lo, (a, ca, b, cb, op) in ((0, (x1, cos, x2, sin, ALU.subtract)), (16, (x2, cos, x1, sin, ALU.add))):
                    chain.done(dve.tensor_tensor(rt1[:, :, :, :], a, ca, ALU.mult))
                    chain.done(dve.tensor_tensor(rt2[:, :, :, :], b, cb, ALU.mult))
                    chain.wait()
                    chain.done(dve.tensor_tensor(rot[:, :, :, lo:lo + 16], rt1[:, :, :, :], rt2[:, :, :, :], op))
                    chain.wait()
                for t in range(TT):
                    dve.tensor_copy(qtok[:, t, :, 64:96], rot[:, t, 0:4, :])
                    last = dve.tensor_copy(ktok[:, t, :, 64:96], bc(rot[:, t, 4:5, :], [P, HEADS, 32]))
                last.then_inc(s["rot_ready"], 1)
                for hd in range(HEADS):
                    dve.wait_ge(s["dt_ready"], HEADS * l + hd + 1)
                    dve.wait_ge(s["s_ready"], HEADS * l + hd + 1)
                    dve.scalar_tensor_tensor(out=dec[:, hd, :], in0=bank[(1, 3, 5, 6)[hd]][:, 0:384], scalar=DH ** -0.5,
                                             in1=dec[:, hd, :], op0=ALU.mult, op1=ALU.mult).then_inc(s["pt_ready"], 1)
                for i in range(2):
                    dve.wait_ge(s["qkT_tr"], 4 * l + 2 + i + 1)
                    dve.tensor_copy(kT[:, 2 * i:2 * i + 2, :], bank[(7, 0)[i]][0:96, :].rearrange("p (h n) -> p h n", h=2)).then_inc(s["kT_ready"], 1)
                dve.wait_ge(s["conf_tr"], l + 1)
                for t in range(TT):
                    chain.done(dve.bn_stats(bst[:, t, :], bank[1][:, t * 256:(t + 1) * 256]))
                chain.wait()
                for t in range(TT):
                    last = dve.bn_aggr(bag[:, t, :], bst[:, t, :])
                last.then_inc(s["bn_ready"], 1)
                for hd in range(HEADS):
                    dve.wait_ge(s["ga_ready"], HEADS * l + hd + 1)
                    dve.tensor_tensor(gS[:, hd, :, :], bank[(3, 5, 6, 7)[hd]][:, 0:384].rearrange("p (b n) -> p b n", b=3),
                                      gla_mask[:, :, :], ALU.mult).then_inc(s["gs_ready"], 1)
                dve.wait_ge(s["conf_rstd"], l + 1)
                for t in range(TT):
                    last = dve.tensor_scalar(ctok[:, t, :], bank[1][:, t * 256:(t + 1) * 256], bag[:, t, 0:1],
                                             bst[:, t, 1:2], ALU.subtract, ALU.mult)
                last.then_inc(s["conf_n"], 1)
                dve.wait_ge(s["num_ready"], l + 1)
                den = lambda t: bank[(2, 4)[t]][:, 0:260].rearrange("p (h n) -> p h n", h=HEADS)[:, :, DH]
                for t in range(TT):
                    chain.done(dve.scalar_tensor_tensor(out=mden[:, t, :], in0=den(t), scalar=-1.0,
                                                        in1=mcol[:, 8 + 4 * t:12 + 4 * t], op0=ALU.mult, op1=ALU.max))
                chain.wait()
                for t in range(TT):
                    chain.done(dve.tensor_tensor(mden[:, t, :], den(t), mden[:, t, :], ALU.max))
                chain.wait()
                chain.done(dve.reciprocal(mden[:, :, :], mden[:, :, :]))
                chain.wait()
                for t in range(TT):
                    nb = bank[(2, 4)[t]][:, 0:260].rearrange("p (h n) -> p h n", h=HEADS)
                    chain.done(dve.tensor_tensor(y[:, t, 0:256].rearrange("p (h n) -> p h n", h=HEADS), nb[:, :, 0:DH],
                                                 bc(mden[:, t, :].unsqueeze(2), [P, HEADS, DH]), ALU.mult))
                chain.wait()
                dve.tensor_tensor(y[:, :, 0:256], y[:, :, 0:256],
                                  osig[:, :, :], ALU.mult).then_inc(s["y_m"], 1)
                dve.wait_ge(s["sc_ready"], l + 1)
                chain.done(dve.tensor_reduce(smax[:, 0, :], bank[6][:, :].rearrange("p (h n) -> p h n", h=HEADS), AX_X, ALU.max))
                for i in range(2):
                    chain.done(dve.tensor_reduce(smax[:, 1, 2 * i:2 * i + 2],
                                                 bank[(0, 1)[i]][:, :].rearrange("p (h n) -> p h n", h=2), AX_X, ALU.max))
                chain.wait()
                dve.tensor_scalar(smax[:, :, :], smax[:, :, :], -(96.0 ** -0.5), None, ALU.mult).then_inc(s["smax_ready"], 1)
                dve.wait_ge(s["osq_ready"], l + 1)
                dve.tensor_reduce(gss[:, :, :], osq[:, :, :, :], AX_X, ALU.add).then_inc(s["gss_ready"], 1)
                dve.wait_ge(s["grd_ready"], l + 1)
                chain.done(dve.tensor_tensor(osq[:, :, :, :], bank[7][:, :].rearrange("p (t h n) -> p t h n", t=TT, h=HEADS),
                                             bc(grd[:, :, :].unsqueeze(3), [P, TT, HEADS, DH]), ALU.mult))
                chain.wait()
                dve.tensor_tensor(y[:, :, 512:768], osq[:, :, :, :].rearrange("p t h n -> p t (h n)"), grs[:, :, :],
                                  ALU.mult).then_inc(s["y_g"], 1)
                dve.wait_ge(s["conf_sig"], l + 1)
                dve.tensor_tensor(y[:, :, 768:1024], ctok[:, :, :], cacc[:, :, :], ALU.mult).then_inc(s["y_c"], 1)
                dve.wait_ge(s["pv_ready"], l + 1)
                chain.done(dve.reciprocal(psums[:, :, :], psums[:, :, :]))
                chain.wait()
                dve.tensor_tensor(y[:, :, 256:512].rearrange("p t (h n) -> p t h n", h=HEADS),
                                  bank[4][:, :].rearrange("p (t h n) -> p t h n", t=TT, h=HEADS),
                                  bc(psums[:, :, :].unsqueeze(3), [P, TT, HEADS, DH]), ALU.mult).then_inc(s["y_a"], 1)

                normalize(3 * l + 1, y, 4)
                for n in range(SPLIT):
                    split_low(n0 + N_IN + n)
                gains(3 * l + 1, FUSE + KD * l)
                split_low(n0 + N_IN + SPLIT)
                add_to_h((2, 3, 5, 6), s["piece_used"], [n0 + N_IN + N_OUT] * 4).then_inc(s["h_ready"], 1)
                normalize(3 * l + 2, h, 1)
                gains(3 * l + 2, NORM2 + KD * l)
                if l == 0:
                    ffn(DENSE0, None, 0, TT)
                    add_to_h((2, 3, 5, 6), s["piece_used"], [DENSE0 + N_FFN] * 4).then_inc(s["h_ready"], 1)

            dve.wait_ge(s["moe_g_in"], 16)
            dve.tensor_tensor(un[:, :, :], un[:, :, :], bc(moe_g[:, :].unsqueeze(1), [P, TT, D]),
                              ALU.mult).then_inc(s["ung_ready"], 1)
            dve.wait_ge(s["logit_ready"], 1)
            dve.tensor_copy(logits[:, :, :], bank[2][:, 0:TT * E].rearrange("p (t e) -> p t e", t=TT)).then_inc(s["routed_ready"], 1)
            dve.wait_ge(s["routed_ready"], 1)
            for t in range(TT):
                chain.done(dve.max(top8[:, t, :], logits[:, t, :]))
            chain.wait()
            for t in range(TT):
                chain.done(dve.max_index(idx8[:, t, :], top8[:, t, :], logits[:, t, :]))
            dve.tensor_tensor(gap[:, :], top8[:, :, 1], top8[:, :, 0], ALU.subtract).then_inc(s["gap_ready"], 1)
            chain.wait()
            chain.done(dve.tensor_copy(idf[:, :, :], idx8[:, :, :]))
            chain.wait()
            for t in range(TT):
                chain.done(dve.tensor_scalar(oh1[:, t, :], iota[:, 0:E], idf[:, t, 0:1], None, ALU.is_equal))
                chain.done(dve.tensor_scalar(oh2[:, t, :], iota[:, 0:E], idf[:, t, 1:2], None, ALU.is_equal))
            chain.wait()
            dve.tensor_tensor(routed[:, :, :], oh1[:, :, :], oh2[:, :, :], ALU.add).then_inc(s["routed_ready"], 1)
            dve.wait_ge(s["egap_ready"], 1)
            chain.done(dve.tensor_scalar(w1[:, :], egap[:, :], 1.0, None, ALU.add))
            chain.wait()
            chain.done(dve.reciprocal(w1[:, :], w1[:, :]))
            chain.wait()
            chain.done(dve.tensor_tensor(w2[:, :], w1[:, :], egap[:, :], ALU.mult))
            chain.wait()
            for t in range(TT):
                chain.done(dve.tensor_scalar(wts[:, t, 0:E], oh2[:, t, :], w2[:, t:t + 1], None, ALU.mult))
            chain.wait()
            for t in range(TT):
                chain.done(dve.scalar_tensor_tensor(out=wts[:, t, 0:E], in0=oh1[:, t, :], scalar=w1[:, t:t + 1],
                                                    in1=wts[:, t, 0:E], op0=ALU.mult, op1=ALU.add))
            dve.wait_ge(s["rank_ready"], 1)
            for t in range(TT):
                chain.done(dve.scalar_tensor_tensor(out=rank1[:, t, :], in0=bank[3][:, t * E:(t + 1) * E], scalar=1.0,
                                                    in1=routed[:, t, :], op0=ALU.add, op1=ALU.mult))
            chain.done(dve.tensor_scalar(over[:, :], bank[3][:, TT * E:(TT + 1) * E], float(P), None, ALU.is_gt))
            chain.wait()
            chain.done(dve.tensor_scalar(keys[:, :, 0:E], rank1[:, :, :], -1.0, None, ALU.add))
            chain.done(dve.tensor_tensor_scan(over_n[:, :], ones[:, 0:E], over[:, :], 0.0, ALU.mult, ALU.add))
            chain.done(dve.tensor_reduce(jobs_f[:, 3:4], over[:, :], AX_X, ALU.add))
            chain.wait()
            for o in range(OVER):
                chain.done(dve.scalar_tensor_tensor(out=over_oh[:, o, :], in0=over_n[:, :], scalar=float(o + 1),
                                                    in1=over[:, :], op0=ALU.is_equal, op1=ALU.mult))
            chain.wait()
            for o in range(OVER):
                oh = bc(over_oh[:, o:o + 1, :], [P, TT, E])
                chain.done(dve.tensor_tensor(pick[:, :, :], rank1[:, :, :], oh, ALU.mult))
                chain.wait()
                chain.done(dve.tensor_reduce(keys[:, :, E + o], pick[:, :, :], AX_X, ALU.add))
                chain.wait()
                chain.done(dve.tensor_tensor(pick[:, :, :], wts[:, :, 0:E], oh, ALU.mult))
                chain.wait()
                chain.done(dve.tensor_reduce(wts[:, :, E + o], pick[:, :, :], AX_X, ALU.add))
                chain.wait()
                chain.done(dve.tensor_tensor(pick[:, 0, :], over_oh[:, o, :], iota[:, 0:E], ALU.mult))
                chain.wait()
                chain.done(dve.tensor_reduce(jobs_f[:, o:o + 1], pick[:, 0, :], AX_X, ALU.add))
                chain.wait()
            chain.done(dve.tensor_scalar(keys[:, :, E:JOBS], keys[:, :, E:JOBS], -float(P + 1), None, ALU.add))
            chain.wait()
            dve.tensor_copy(jobs_i[:, :], jobs_f[:, :]).then_inc(s["jobs_ready"], 1)
            dve.wait_ge(s["unh_ready"], 1)
            dve.tensor_tensor(unl[:, :, :], un[:, :, :], unh[:, :, :].bitcast(F32), ALU.subtract).then_inc(s["unl_ready"], 1)

            def job(j):
                dve.tensor_copy(keycol[:, :], keys[:, :, bass.ds(j, 1)].rearrange("p t a -> p (t a)")).then_inc(s["key_copied"], 1)
                dve.tensor_copy(wcol[:, :], wts[:, :, bass.ds(j, 1)].rearrange("p t a -> p (t a)")).then_inc(s["key_copied"], 1)
                dve.wait_ge(s["key_copied"], 2 * j + 2)
                for t in range(TT):
                    last = dve.tensor_scalar(sel[:, t, :], iota[:, :], keycol[:, t:t + 1], None, ALU.is_equal)
                last.then_inc(s["sel_ready"], 1)
                dve.wait_ge(s["xh_ready"], j + 1)
                for i in range(2):
                    last = dve.tensor_tensor(xl[:, 4 * i:4 * i + 4, :], bank[5 + i][:, :].rearrange("p (k n) -> p k n", k=4),
                                             xh[:, 4 * i:4 * i + 4, :].bitcast(F32), ALU.subtract)
                last.then_inc(s["xl_ready"], 1)
                dve.tensor_copy(selT[:, :, :], bank[7][:, 0:2 * P].rearrange("p (t n) -> p t n", t=TT))
                dve.tensor_copy(wslot[:, :], bank[7][:, 2 * P:2 * P + 1]).then_inc(s["selT_ready"], 1)
                ffn(MOE0, j, j + 1, 1)
                dve.wait_ge(s["yh_ready"], j + 1)
                for i in range(2):
                    last = dve.scalar_tensor_tensor(out=yl[:, i * 512:(i + 1) * 512], in0=bank[2 + i][:, :], scalar=wslot[:, :],
                                                    in1=yh[:, i * 512:(i + 1) * 512].bitcast(F32), op0=ALU.mult, op1=ALU.subtract)
                last.then_inc(s["yl_ready"], 1)
                for i, b in enumerate((0, 1, 5, 6)):
                    t, half = divmod(i, 2)
                    dve.wait_ge(s["scat_ready"], 4 * j + (i + 1))
                    dst = h[:, t, half * 512:(half + 1) * 512]
                    dve.tensor_tensor(dst, bank[b][:, :], dst, ALU.add).then_inc(s["added"], 1)

            dve.memset(tiny[:, :], 0.0).then_inc(s["added"], 1)
            jobs(dve, job)
            dve.memset(tiny[:, :], 0.0).then_inc(s["h_ready"], 2)
            dve.wait_ge(s["rstd_ready"], 7)
            dve.wait_ge(s["final_in"], 16)
            for t in range(TT):
                last = dve.scalar_tensor_tensor(out=h[:, t, :], in0=h[:, t, :], scalar=rstd[:, t, 0:1], in1=fin_g,
                                                op0=ALU.mult, op1=ALU.mult)
            last.then_inc(s["out_ready"], 1)

        @block.tensor
        def _(pe):
            owner = {}

            def claim(b, sem, value):
                if b in owner:
                    pe.wait_ge(*owner[b])
                owner[b] = (s[sem], value)

            def norm_transposes(k):
                pe.wait_ge(s["un_ready"], k + 1)
                for g in range(4):
                    b = NORM_BANKS[g]
                    claim(b, "utl_ready", 4 * k + g + 1)
                    for i in range(2):
                        for t in range(TT):
                            last = pe.transpose(bank[b][:, i * S + t * P:i * S + (t + 1) * P],
                                                un[:, t, (2 * g + i) * P:(2 * g + i + 1) * P], ident[:, :])
                    last.then_inc(s["norm_tr"], 1)

            def product(dst, terms):
                for i, ((ah, al), (bh, bl)) in enumerate(terms):
                    first, final = i == 0, i == len(terms) - 1
                    pe.matmul(dst, ah, bh, start=first, stop=False)
                    pe.matmul(dst, ah, bl, start=False, stop=False)
                    last = pe.matmul(dst, al, bh, start=False, stop=final)
                return last

            def part(n, lo, hi):
                return high[:, n % SPLIT, lo:hi], low[:, n % SPLIT, lo:hi]

            def uT(k, lo, hi):
                return uTh[:, k, lo:hi], uTl[:, k, lo:hi]

            def ffn(n0, job, job_n, tiles, xT, accs, first_claims):
                pieces = N_FFN * job if job is not None else 0
                at = lambda c: job_n * CHUNKS + c

                def down(c):
                    n = n0 + FFN_AT[("d", c)]
                    pe.wait_ge(s["hTl_ready"], at(c + 1))
                    pe.wait_ge(s["low_ready"], pieces + (n + 1))
                    for f in range(2):
                        for t in range(tiles):
                            for half in range(2):
                                o = bank[accs[t][half]][:, :]
                                ah, al = hTh[:, f, t, :], hTl[:, f, t, :]
                                bh, bl = part(n, f * 1024 + half * 512, f * 1024 + half * 512 + 512)
                                pe.matmul(o, ah, bh, start=(c == 0 and f == 0), stop=False)
                                pe.matmul(o, ah, bl, start=False, stop=False)
                                last = pe.matmul(o, al, bh, start=False, stop=(c == CHUNKS - 1 and f == 1))
                    last.then_inc(s["piece_used"], 1)
                    return last

                for c in range(CHUNKS):
                    if c:
                        pe.wait_ge(s["hid_ready"], at(c))
                    else:
                        first_claims()
                    for kh, kind in enumerate("ab"):
                        n = n0 + FFN_AT[(kind, c)]
                        pe.wait_ge(s["low_ready"], pieces + (n + 1))
                        for t in range(tiles):
                            for k in range(4):
                                kd = 4 * kh + k
                                ah, al = xT(kd, t)
                                bh, bl = part(n, k * 512, (k + 1) * 512)
                                o = bank[t][:, :]
                                pe.matmul(o, ah, bh, start=(kd == 0), stop=False)
                                pe.matmul(o, ah, bl, start=False, stop=False)
                                last = pe.matmul(o, al, bh, start=False, stop=(kd == KD - 1))
                        last.then_inc(s["piece_used"], 1)
                    if c:
                        down(c - 1)
                        pe.wait_ge(s["hTl_ready"], at(c))
                    pe.wait_ge(s["hid_ready"], at(c + 1))
                    for f in range(2):
                        for t in range(tiles):
                            o = (f * tiles + t) * P
                            last = pe.transpose(bank[4][:, o:o + P], hid[:, t, f * P:(f + 1) * P], ident[:, :])
                    last.then_inc(s["hid_tr"], 1)
                down(CHUNKS - 1)

            pe.wait_ge(s["consts"], 1)
            pe.wait_ge(s["rows_in"], 16 * 11)
            claim(7, "cols_ready", 1)
            pe.transpose(bank[7][:, 0:P], stage[:, 0, :], ident[:, :])
            pe.transpose(bank[7][:, P:2 * P], stage[:, 1, :], ident[:, :]).then_inc(s["cols_tr"], 1)

            for l in range(DEPTH):
                n0 = LAYER_PIECES[l]
                norm_transposes(3 * l)
                pe.wait_ge(s["utl_ready"], 4 * (3 * l + 1))
                act_reads = {1: 1, 4: 2, 5: 3, 6: 5, 7: 6, 8: 7, 9: 8}
                dve_reads = {0: 1, 2: 2, 3: 3, 10: 4}
                for p in range(N_IN):
                    n = n0 + p
                    w = sum(v for _, v in W_IN_PIECES[p])
                    pe.wait_ge(s["low_ready"], n + 1)
                    b = Z_BANKS[p % 4]
                    claim(b, *(("z_act", 9 * l + act_reads[p]) if p in act_reads else ("z_dve", 4 * l + dve_reads[p])))
                    if p in FEATURE_MAJOR:
                        for c in range(2):
                            last = product(bank[b][:, c * S:(c + 1) * S],
                                           [(part(n, k * w + c * P, k * w + (c + 1) * P), uT(k, 0, S)) for k in range(KD)])
                    else:
                        for t in range(TT):
                            last = product(bank[b][:, t * w:(t + 1) * w],
                                           [(uT(k, t * P, (t + 1) * P), part(n, k * w, (k + 1) * w)) for k in range(KD)])
                    last.then_inc(s["piece_used"], 1)
                    if p == 6:
                        pe.wait_ge(s["z_act"], 9 * l + 3)
                        claim(7, "z_act", 9 * l + 4)
                        for t in range(TT):
                            last = pe.transpose(bank[7][0:16, t * P:(t + 1) * P], zkv[:, t, 160:176], ident[:, :])
                        last.then_inc(s["aT_tr"], 1)

                pe.wait_ge(s["ukv_in"], 64 * (l + 1))
                claim(0, "gla_abs", l + 1)
                pe.wait_ge(s["z_act"], 9 * l + 4)
                pe.matmul(bank[0][:, 0:S], walpha[:, :], aT[:, :], start=True, stop=True).then_inc(s["gpre_ready"], 1)
                pe.wait_ge(s["lat_ready"], l + 1)
                claim(4, "lat_T", l + 1)
                claim(7, "lat_T", l + 1)
                for t in range(TT):
                    pe.transpose(bank[4][:, t * P:(t + 1) * P], zif[:, t, 8:136], ident[:, :])
                    pe.transpose(bank[4][0:64, S + t * P:S + (t + 1) * P], zif[:, t, 136:200], ident[:, :])
                    last = pe.transpose(bank[7][:, t * P:(t + 1) * P], zkv[:, t, 0:P], ident[:, :])
                last.then_inc(s["lat_tr"], 1)
                pe.wait_ge(s["lf_ready"], l + 1)
                claim(2, "mcum_ready", l + 1)
                for t in range(TT):
                    pe.transpose(bank[2][0:4, t * P:(t + 1) * P], gb[:, t, 0:4], ident[:, :])
                    last = pe.transpose(bank[2][0:4, S + t * P:S + (t + 1) * P], gb[:, t, 4:8], ident[:, :])
                last.then_inc(s["gate_tr"], 1)
                pe.wait_ge(s["lat_T"], l + 1)
                for t in range(TT):
                    b = (3, 5)[t]
                    claim(b, "qkv_evac", l + 1)
                    pe.matmul(bank[b][:, 0:384], cqT[:, 0, t * P:(t + 1) * P], uq[:, 0, :], start=True, stop=False)
                    last = pe.matmul(bank[b][:, 0:384], cqT[0:64, 1, t * P:(t + 1) * P], uq[0:64, 1, :], start=False, stop=True)
                last.then_inc(s["q_ready"], 1)
                for t in range(TT):
                    b = (6, 1)[t]
                    claim(b, "qkv_evac", l + 1)
                    last = pe.matmul(bank[b][:, :], ckvT[:, t * P:(t + 1) * P], ukv[:, :], start=True, stop=True)
                last.then_inc(s["kv_ready"], 1)
                pe.wait_ge(s["expnm_ready"], l + 1)
                claim(0, "mcol_ready", l + 1)
                for t in range(TT):
                    pe.transpose(bank[0][:, 4 * t:4 * t + 4], aj[:, t * P:(t + 1) * P], ident[0:4, 0:4])
                    last = pe.transpose(bank[0][:, 8 + 4 * t:12 + 4 * t], expnm[:, t * P:(t + 1) * P], ident[0:4, 0:4])
                last.then_inc(s["mcol_tr"], 1)
                pe.wait_ge(s["qk_ready"], l + 1)
                for hd in range(HEADS):
                    b = (2, 4, 7, 0)[hd]
                    claim(b, "dt_ready", HEADS * l + hd + 1)
                    row = bc(ident[0:4, hd:hd + 1], [4, P])
                    pe.matmul(bank[b][:, 0:S], row, negm[:, :], start=True, stop=False)
                    pe.matmul(bank[b][:, 0:P], ident[:, :], mask_kt[:, :], start=False, stop=True)
                    pe.matmul(bank[b][:, S:S + P], row, negm[:, P:S], start=True, stop=False)
                    pe.matmul(bank[b][:, S:S + P], ident[:, :], mask_kt[:, :], start=False, stop=True).then_inc(s["x_ready"], 1)
                    b = (1, 3, 5, 6)[hd]
                    claim(b, "pt_ready", HEADS * l + hd + 1)
                    r = slice(64 * (hd % 2), 64 * (hd % 2) + 64)
                    q, k = qkc[r, hd // 2, :], qkc[r, 2 + hd // 2, :]
                    pe.matmul(bank[b][:, 0:S], k[:, 0:P], q, start=True, stop=True)
                    pe.matmul(bank[b][:, S:S + P], k[:, P:S], q[:, P:S], start=True, stop=True).then_inc(s["s_ready"], 1)
                pe.wait_ge(s["rot_ready"], l + 1)
                for i, (b, src, sem, v) in enumerate(((2, qtok, "qT_ready", 1), (4, qtok, "qT_ready", 2),
                                                      (7, ktok, "kT_ready", 1), (0, ktok, "kT_ready", 2))):
                    claim(b, sem, 2 * l + v)
                    for a in range(2):
                        for t in range(TT):
                            last = pe.transpose(bank[b][0:96, a * S + t * P:a * S + (t + 1) * P],
                                                src[:, t, 2 * (i % 2) + a, :], ident[:, :])
                    last.then_inc(s["qkT_tr"], 1)
                pe.wait_ge(s["conv_done"], l + 1)
                claim(1, "conf_n", l + 1)
                for t in range(TT):
                    for c in range(2):
                        last = pe.transpose(bank[1][:, t * 256 + c * P:t * 256 + (c + 1) * P],
                                            cacc[:, c, t * P:(t + 1) * P], ident[:, :])
                last.then_inc(s["conf_tr"], 1)
                pe.wait_ge(s["gla_qk"], l + 1)
                for hd in range(HEADS):
                    b = (3, 5, 6, 7)[hd]
                    claim(b, "gs_ready", HEADS * l + hd + 1)
                    r = slice(32 * hd, 32 * hd + 32)
                    for i, (k, q) in enumerate(((2, 0), (3, 1), (4, 1))):
                        last = pe.matmul(bank[b][:, i * P:(i + 1) * P], gE[r, k, :], gE[r, q, :], start=True, stop=True,
                                         tile_position=(32 * hd, 0))
                    last.then_inc(s["ga_ready"], 1)
                for hd in range(HEADS):
                    pe.wait_ge(s["pt_ready"], HEADS * l + hd + 1)
                    for t in range(TT):
                        b = (2, 4)[t]
                        if hd == 0:
                            claim(b, "y_m", l + 1)
                        o = bank[b][:, hd * 65:(hd + 1) * 65]
                        if t == 0:
                            last = pe.matmul(o, dec[:, hd, 0:P], vaug[:, 0, hd, :], start=True, stop=True)
                        else:
                            pe.matmul(o, dec[:, hd, P:S], vaug[:, 0, hd, :], start=True, stop=False)
                            last = pe.matmul(o, dec[:, hd, S:S + P], vaug[:, 1, hd, :], start=False, stop=True)
                last.then_inc(s["num_ready"], 1)
                pe.wait_ge(s["qT_ready"], 2 * (l + 1))
                pe.wait_ge(s["kT_ready"], 2 * (l + 1))
                for hd in range(HEADS):
                    if hd == 0:
                        claim(6, "p_ready", l + 1)
                    o = bank[6][:, hd * P:(hd + 1) * P]
                    pe.matmul(o, qT[:, hd, 0:P], kT[:, hd, 0:P], start=True, stop=False)
                    pe.matmul(o, ident[:, :], mask_qt[:, :], start=False, stop=True)
                for hd in range(HEADS):
                    b = (0, 1)[hd // 2]
                    if hd % 2 == 0:
                        claim(b, "p_ready", l + 1)
                    o = bank[b][:, (hd % 2) * S:(hd % 2 + 1) * S]
                    pe.matmul(o, qT[:, hd, P:S], kT[:, hd, :], start=True, stop=False)
                    last = pe.matmul(o[:, P:S], ident[:, :], mask_qt[:, :], start=False, stop=True)
                last.then_inc(s["sc_ready"], 1)
                for hd in range(HEADS):
                    pe.wait_ge(s["gs_ready"], HEADS * l + hd + 1)
                    if hd == HEADS - 1:
                        break
                claim(7, "y_g", l + 1)
                for t in range(TT):
                    for hd in range(HEADS):
                        o = bank[7][:, t * 256 + hd * DH:t * 256 + (hd + 1) * DH]
                        v = gv[:, :, hd * DH:(hd + 1) * DH]
                        if t == 0:
                            last = pe.matmul(o, gS[:, hd, 0, :], v[:, 0, :], start=True, stop=True)
                        else:
                            pe.matmul(o, gS[:, hd, 1, :], v[:, 0, :], start=True, stop=False)
                            last = pe.matmul(o, gS[:, hd, 2, :], v[:, 1, :], start=False, stop=True)
                last.then_inc(s["go_ready"], 1)
                pe.wait_ge(s["p_ready"], l + 1)
                for i, b in enumerate((3, 5, 6)):
                    claim(b, "pT_ready", 3 * l + i + 1)
                    for hd in range(HEADS):
                        src = probs[:, hd * P:(hd + 1) * P] if i == 0 else \
                            probs[:, 512 + hd * S + (i - 1) * P:512 + hd * S + i * P]
                        last = pe.transpose(bank[b][:, hd * P:(hd + 1) * P], src, ident[:, :])
                    last.then_inc(s["p_tr"], 1)
                pe.wait_ge(s["pT_ready"], 3 * (l + 1))
                claim(4, "y_a", l + 1)
                for t in range(TT):
                    for hd in range(HEADS):
                        o = bank[4][:, t * 256 + hd * DH:t * 256 + (hd + 1) * DH]
                        v = vm[:, :, hd * DH:(hd + 1) * DH]
                        if t == 0:
                            last = pe.matmul(o, probT[:, 0, hd, :], v[:, 0, :], start=True, stop=True)
                        else:
                            pe.matmul(o, probT[:, 1, hd, :], v[:, 0, :], start=True, stop=False)
                            last = pe.matmul(o, probT[:, 2, hd, :], v[:, 1, :], start=False, stop=True)
                last.then_inc(s["pv_ready"], 1)

                norm_transposes(3 * l + 1)
                for i, b in enumerate((2, 3, 5, 6)):
                    claim(b, "h_ready", 2 * l + 1)
                for p in range(N_OUT):
                    n = n0 + N_IN + p
                    pe.wait_ge(s["utl_ready"], 4 * (3 * l + 1) + p + 1)
                    pe.wait_ge(s["low_ready"], n + 1)
                    for i, b in enumerate((2, 3, 5, 6)):
                        t, half = divmod(i, 2)
                        for k in range(2):
                            (ah, al), (bh, bl) = uT(2 * p + k, t * P, (t + 1) * P), part(n, k * D + half * 512, k * D + (half + 1) * 512)
                            pe.matmul(bank[b][:, :], ah, bh, start=(p == 0 and k == 0), stop=False)
                            pe.matmul(bank[b][:, :], ah, bl, start=False, stop=False)
                            last = pe.matmul(bank[b][:, :], al, bh, start=False, stop=(p == N_OUT - 1 and k == 1))
                    last.then_inc(s["piece_used"], 1)
                norm_transposes(3 * l + 2)
                pe.wait_ge(s["utl_ready"], 4 * (3 * l + 3))
                if l == 0:
                    def dense_claims():
                        for b, v in ((0, ("hid_ready", CHUNKS)), (1, ("hid_ready", CHUNKS)), (4, ("hTl_ready", CHUNKS)),
                                     (2, ("h_ready", 2)), (3, ("h_ready", 2)), (5, ("h_ready", 2)), (6, ("h_ready", 2))):
                            claim(b, *v)
                    ffn(DENSE0, None, 0, TT, lambda kd, t: uT(kd, t * P, (t + 1) * P), ((2, 3), (5, 6)), dense_claims)

            pe.wait_ge(s["router_in"], 16)
            claim(2, "routed_ready", 1)
            for t in range(TT):
                for k in range(KD):
                    for i, a in enumerate((uTh, uTl)):
                        last = pe.matmul(bank[2][:, t * E:(t + 1) * E], a[:, k, t * P:(t + 1) * P].bitcast(F32), router[:, k, :],
                                         start=(k == 0 and i == 0), stop=(k == KD - 1 and i == 1))
            last.then_inc(s["logit_ready"], 1)
            pe.wait_ge(s["routed_ready"], 2)
            claim(3, "jobs_ready", 1)
            pe.matmul(bank[3][:, 0:E], before[:, :], routed[:, 0, :], start=True, stop=True)
            pe.matmul(bank[3][:, E:2 * E], ones[:, 0:P], routed[:, 0, :], start=True, stop=False)
            pe.matmul(bank[3][:, E:2 * E], before[:, :], routed[:, 1, :], start=False, stop=True)
            pe.matmul(bank[3][:, 2 * E:3 * E], ones[:, 0:P], routed[:, 0, :], start=True, stop=False)
            pe.matmul(bank[3][:, 2 * E:3 * E], ones[:, 0:P], routed[:, 1, :], start=False, stop=True).then_inc(s["rank_ready"], 1)
            for b in range(8):
                if b in owner:
                    pe.wait_ge(*owner[b])
            pe.wait_ge(s["unl_ready"], 1)

            def job(j):
                pe.wait_ge(s["sel_ready"], j + 1)
                pe.wait_ge(s["added"], 4 * j + 1)
                for kd in range(KD):
                    o = bank[5 + kd // 4][:, (kd % 4) * P:(kd % 4 + 1) * P]
                    for t in range(TT):
                        pe.matmul(o, unh_g[:, t, kd * P:(kd + 1) * P], sel[:, t, :], start=(t == 0), stop=False)
                        pe.matmul(o, unl_g[:, t, kd * P:(kd + 1) * P], sel[:, t, :], start=False, stop=(t == TT - 1))
                for t in range(TT):
                    pe.transpose(bank[7][:, t * P:(t + 1) * P], sel[:, t, :].bitcast(F32), ident[:, :])
                for t in range(TT):
                    last = pe.matmul(bank[7][:, 2 * P:2 * P + 1], sel[:, t, :].bitcast(F32), wcol[:, t:t + 1],
                                     start=(t == 0), stop=(t == TT - 1))
                last.then_inc(s["gath_ready"], 1)
                pe.wait_ge(s["xl_ready"], j + 1)
                ffn(MOE0, j, j + 1, 1, lambda kd, t: (xh[:, kd, :], xl[:, kd, :]), ((2, 3),), lambda: None)
                pe.wait_ge(s["selT_ready"], j + 1)
                pe.wait_ge(s["yl_ready"], j + 1)
                for i, b in enumerate((0, 1, 5, 6)):
                    t, half = divmod(i, 2)
                    pe.matmul(bank[b][:, :], selT[:, t, :], yh[:, half * 512:(half + 1) * 512], start=True, stop=False)
                    pe.matmul(bank[b][:, :], selT[:, t, :], yl[:, half * 512:(half + 1) * 512], start=False, stop=True).then_inc(s["scat_ready"], 1)

            unh_g, unl_g = unh, unl
            jobs(pe, job)


_INS = ['x', 'positions', 'norm1_g', 'w_in', 'mlstm_conv_w', 'mlstm_conv_b', 'mlstm_gate_b', 'mla_q_norm_g',
        'mla_w_uq', 'mla_kv_norm_g', 'mla_w_ukv', 'gla_w_alpha', 'gla_b_alpha', 'conv_w', 'conv_b', 'conv_ln_g',
        'conv_ln_b', 'fuse_g', 'w_out', 'norm2_g', 'ffn_w_gate', 'ffn_w_up', 'ffn_w_down', 'moe_router',
        'moe_w_gate', 'moe_w_up', 'moe_w_down', 'final_norm_g']


def kernel(**inputs):
    import numpy as _np
    import concourse.bacc as _bacc
    from concourse import mybir as _mybir
    from concourse.bass_utils import run_bass_kernel_spmd as _run

    nc = _bacc.Bacc("TRN2", target_bir_lowering=False, num_devices=1)
    arrays, args = {}, []
    for name in _INS:
        a = _np.ascontiguousarray(inputs[name])
        arrays[f"in_{name}_dram"] = a
        args.append(nc.dram_tensor(f"in_{name}_dram", a.shape, _mybir.dt.from_np(a.dtype), kind="ExternalInput").ap())
    out = nc.dram_tensor("out_0_dram", inputs["x"].shape, _mybir.dt.from_np(_np.dtype("float32")), kind="ExternalOutput").ap()
    build(nc, *args, out)
    r = _run(nc, [arrays], core_ids=[0])
    return r.results[0]["out_0_dram"]
```

```python
import math
from contextlib import ExitStack

import numpy as np
import concourse.bass as bass
from concourse import mybir

F32 = mybir.dt.float32
F32R = mybir.dt.float32r
I32 = mybir.dt.int32
U32 = mybir.dt.uint32
ALU = mybir.AluOpType
ACT = mybir.ActivationFunctionType
AX_X = mybir.AxisListType.X
LN_EXP = "natural_log_exp_and_others"

P = 128
EPS = 1e-6
NEG = -1e30

PIECE = 2048
RING = 11
SPLIT = 3

W_IN_PIECES = [
    [(2168, 256)],
    [(2424, 256)],
    [(0, 256)],
    [(256, 256)],
    [(1024, 200)],
    [(1224, 160), (2152, 16)],
    [(1384, 256)],
    [(512, 256)],
    [(768, 256)],
    [(1640, 256)],
    [(1896, 256)],
]
N_IN = len(W_IN_PIECES)
FEATURE_MAJOR = (0, 1, 2, 3, 6)
N_OUT = 4
CHUNKS = 11
N_FFN = 3 * CHUNKS


def ffn_pieces():
    order = []
    for c in range(CHUNKS):
        order += [("a", c), ("b", c)]
        if c:
            order.append(("d", c - 1))
    return order + [("d", CHUNKS - 1)]


FFN_ORDER = ffn_pieces()
FFN_AT = {key: n for n, key in enumerate(FFN_ORDER)}


class Chain:

    def __init__(self, eng, sem):
        self.eng, self.sem, self.n = eng, sem, 0

    def done(self, ins):
        self.n += 1
        ins.then_inc(self.sem, 1)

    def wait(self, lag=0):
        if self.n > lag:
            self.eng.wait_ge(self.sem, self.n - lag)


def build(nc, x, positions, norm1_g, w_in, mlstm_conv_w, mlstm_conv_b, mlstm_gate_b,
          mla_q_norm_g, mla_w_uq, mla_kv_norm_g, mla_w_ukv, gla_w_alpha, gla_b_alpha,
          conv_w, conv_b, conv_ln_g, conv_ln_b, fuse_g, w_out, norm2_g,
          ffn_w_gate, ffn_w_up, ffn_w_down, moe_router, moe_w_gate, moe_w_up, moe_w_down,
          final_norm_g, out):
    DEPTH, D, _ = w_in.shape
    S = x.shape[1]
    TT = S // P
    KD = D // P
    HEADS = 4
    DH = 64
    CONV, MCONV = conv_w.shape[1], mlstm_conv_w.shape[1]
    E = moe_w_gate.shape[1]
    OVER = 3
    JOBS = E + OVER
    F_CH = moe_w_gate.shape[3] // CHUNKS
    assert (TT, KD, F_CH, E) == (2, 8, 256, 8)
    LAYER_PIECES = [0, N_IN + N_OUT + N_FFN]
    MOE0 = LAYER_PIECES[1] + N_IN + N_OUT
    DENSE0 = N_IN + N_OUT
    assert N_FFN % RING == 0 and N_FFN % SPLIT == 0

    ctx = ExitStack()

    def sb(name, shape, dt=F32, where=ctx):
        return where.enter_context(nc.sbuf_tensor(name, shape, dt))

    with ctx:
        ring = sb("ring", [P, RING, PIECE])
        h = sb("h", [P, TT, D])
        ident = sb("ident", [P, P])
        ones = sb("ones", [P, S])
        iota = sb("iota", [P, P])
        mask_kt = sb("mask_kt", [P, P])
        mask_qt = sb("mask_qt", [P, P])
        gla_mask = sb("gla_mask", [P, 3, P])
        before = sb("before", [P, P])
        cols = sb("cols", [P, 2, P])
        gate_b = sb("gate_b", [P, DEPTH, 8])
        ln_gb = sb("ln_gb", [P, 2, 256])
        router = sb("router", [P, KD, E])
        invf = sb("invf", [P, 16])
        pos_i = sb("pos_i", [P, TT], I32)
        pos_f = sb("pos_f", [P, TT])
        ang = sb("ang", [P, 2, TT, 16])
        turn = sb("turn", [P, 2, TT, 16])
        cossin = sb("cossin", [P, 2, TT, 16])
        epst = sb("epst", [P, 1])
        ss = sb("ss", [P, TT, 4])
        lnv = sb("lnv", [P, TT, 4])
        rstd = sb("rstd", [P, TT, 4])
        tiny = sb("tiny", [P, 1])
        logits = sb("logits", [P, TT, E])
        top8 = sb("top8", [P, TT, 8])
        idx8 = sb("idx8", [P, TT, 8], U32)
        idf = sb("idf", [P, TT, 8])
        gap = sb("gap", [P, TT])
        egap = sb("egap", [P, TT])
        w1 = sb("w1", [P, TT])
        w2 = sb("w2", [P, TT])
        oh1 = sb("oh1", [P, TT, E])
        oh2 = sb("oh2", [P, TT, E])
        routed = sb("routed", [P, TT, E])
        rank1 = sb("rank1", [P, TT, E])
        keys = sb("keys", [P, TT, JOBS + 1])
        wts = sb("wts", [P, TT, JOBS])
        over = sb("over", [P, E])
        over_n = sb("over_n", [P, E])
        over_oh = sb("over_oh", [P, OVER, E])
        pick = sb("pick", [P, TT, E])
        jobs_f = sb("jobs_f", [P, 4])
        jobs_i = sb("jobs_i", [P, 4], I32)
        keycol = sb("keycol", [P, TT])
        wcol = sb("wcol", [P, TT])
        wslot = sb("wslot", [P, 1])

        with ExitStack() as part:
            un = sb("un", [P, TT, D], F32, part)
            probs = un[:, :, :].rearrange("p t d -> p (t d)")
        with ExitStack() as part:
            yh = sb("yh", [P, D], F32R, part)
            yl = sb("yl", [P, D], F32R, part)
        keep_un = ctx.enter_context(nc.sbuf_tensor("keep_un", [P, TT, D], F32))

        with ExitStack() as part:
            glu = sb("glu", [P, 2, CONV - 1 + S], F32, part)
            gsig = sb("gsig", [P, 2, S], F32, part)
            cacc = sb("cacc", [P, 2, S], F32, part)
            qkpre = sb("qkpre", [P, 4, MCONV - 1 + S], F32, part)
            qkc = sb("qkc", [P, 4, S], F32, part)
            vaug = sb("vaug", [P, TT, HEADS, DH + 1], F32, part)
            osig = sb("osig", [P, TT, 256], F32, part)
            zif = sb("zif", [P, TT, 200], F32, part)
            zkv = sb("zkv", [P, TT, 176], F32, part)
            aT = sb("aT", [16, S], F32, part)
            gqk = sb("gqk", [P, 2, S], F32, part)
            gv = sb("gv", [P, TT, 256], F32, part)
            grs = sb("grs", [P, TT, 256], F32, part)
            size_b = 4 * (2 * (CONV - 1 + S) + 4 * S + 4 * (MCONV - 1 + S) + 4 * S + 2 * 260 + 512
                          + 400 + 352 + S + 2 * S + 512 + 512)
        with ExitStack() as part:
            moe_g = sb("moe_g", [P, D], F32, part)
        with ExitStack() as part:
            sg = sb("sg", [P, TT, 256], F32, part)
            hid = sb("hid", [P, TT, 256], F32, part)
            hTh = sb("hTh", [P, 2, TT, P], F32R, part)
            hTl = sb("hTl", [P, 2, TT, P], F32R, part)
            unh = sb("unh", [P, TT, D], F32R, part)
            unl = sb("unl", [P, TT, D], F32R, part)
            sel = sb("sel", [P, TT, P], F32R, part)
            selT = sb("selT", [P, TT, P], F32R, part)
            size_f = 4 * (512 + 512 + 512 + 512 + 4096 + 256 + 256)
        ctx.enter_context(nc.sbuf_tensor("keep_b", [P, max(size_b, size_f) // 4 + 8], F32))

        with ExitStack() as part:
            y = sb("y", [P, TT, D], F32, part)
            stage = y[:, 0, 0:2 * P].rearrange("p (a n) -> p a n", a=2)
            gb = sb("gb", [P, TT, 8], F32, part)
            gmn = sb("gmn", [P, TT, 4], F32, part)
            gab = sb("gab", [P, TT, 4], F32, part)
            gln = sb("gln", [P, TT, 4], F32, part)
            cumf = sb("cumf", [4, S], F32, part)
            aj = sb("aj", [4, S], F32, part)
            mrun = sb("mrun", [4, S], F32, part)
            negm = sb("negm", [4, S], F32, part)
            expnm = sb("expnm", [4, S], F32, part)
            mcol = sb("mcol", [P, 16], F32, part)
            dec = sb("dec", [P, HEADS, 384], F32, part)
            mden = sb("mden", [P, TT, HEADS], F32, part)
            uq = sb("uq", [P, 2, 384], F32, part)
            ukv = sb("ukv", [P, 512], F32, part)
            walpha = sb("walpha", [16, P], F32, part)
            lss = sb("lss", [P, 2, TT], F32, part)
            lln = sb("lln", [P, 2, TT], F32, part)
            lrs = sb("lrs", [P, 2, TT], F32, part)
            cqT = sb("cqT", [P, 2, S], F32, part)
            ckvT = sb("ckvT", [P, S], F32, part)
            qtok = sb("qtok", [P, TT, HEADS, 96], F32, part)
            ktok = sb("ktok", [P, TT, HEADS, 96], F32, part)
            rin = sb("rin", [P, TT, 5, 32], F32, part)
            rot = sb("rot", [P, TT, 5, 32], F32, part)
            rt1 = sb("rt1", [P, TT, 5, 16], F32, part)
            rt2 = sb("rt2", [P, TT, 5, 16], F32, part)
            vm = sb("vm", [P, TT, 256], F32, part)
            qT = sb("qT", [96, HEADS, S], F32, part)
            kT = sb("kT", [96, HEADS, S], F32, part)
            smax = sb("smax", [P, TT, HEADS], F32, part)
            psums = sb("psums", [P, TT, HEADS], F32, part)
            gx = sb("gx", [P, S], F32, part)
            gmn2 = sb("gmn2", [P, S], F32, part)
            gab2 = sb("gab2", [P, S], F32, part)
            b16 = gx
            gref = sb("gref", [P, 2, 2], F32, part)
            gE = sb("gE", [P, 5, P], F32, part)
            gS = sb("gS", [P, HEADS, 3, P], F32, part)
            probT = gS[:, :, :, :].rearrange("p h b n -> p (h b n)").rearrange("p (b h n) -> p b h n", b=3, h=HEADS)
            osq = sb("osq", [P, TT, HEADS, DH], F32, part)
            gss = sb("gss", [P, TT, HEADS], F32, part)
            gls = sb("gls", [P, TT, HEADS], F32, part)
            grd = sb("grd", [P, TT, HEADS], F32, part)
            ctok = cqT[:, :, :]
            bst = sb("bst", [P, TT, 6], F32, part)
            bag = sb("bag", [P, TT, 2], F32, part)
        with ExitStack() as part:
            u32 = sb("u32", [P, KD, S], F32, part)
        uTh = sb("uTh", [P, KD, S], F32R)
        uTl = sb("uTl", [P, KD, S], F32R)
        high = sb("high", [P, SPLIT, PIECE], F32R)
        low = sb("low", [P, SPLIT, PIECE], F32R)

        bank = [ctx.enter_context(nc.psum_tensor(f"bank{i}", [P, 512], F32)) for i in range(8)]
        NORM_BANKS = (0, 1, 4, 7)
        Z_BANKS = (2, 3, 5, 6)
        SCATTER_BANKS = (1, 5, 6, 7)
        SLOTS_AT, SELECT_AT, GATHER_AT = 2, 4, 6

        fin_g = ring[:, 0, 0:D]
        xh, xl = uTh[:, :, 0:P], uTl[:, :, 0:P]
        xs = u32[:, :, P:2 * P]

        sems = {}
        for name in (
                "x_in", "pos_in", "stage_zero", "rows_in", "gateb_in", "ln_in", "router_in", "moe_g_in", "ung_ready", "ukv_in", "final_in",
                "consts", "cols_tr", "cols_ready", "ang_ready", "sin_ready",
                "high_ready", "low_ready", "piece_used",
                "h_ready", "rstd_ready", "un_ready", "norm_tr", "uth_ready", "utl_ready",
                "z_act", "z_dve", "qk_conv", "qk_sig", "qk_ready", "conv_done",
                "lat_rstd", "lat_ready", "lat_tr", "lat_T", "gates_abs", "gates_ln", "lf_ready",
                "gate_tr", "gpre_ready", "gla_abs", "gla_ln", "gla_cum", "mcum_ready", "expnm_ready",
                "mcol_tr", "mcol_ready", "q_ready", "kv_ready", "qkv_evac", "rot_ready",
                "gla_exp", "gla_qk", "x_ready", "s_ready", "dt_ready", "pt_ready", "num_ready",
                "y_m", "qkT_tr", "qT_ready", "kT_ready", "sc_ready", "smax_ready", "p_ready",
                "p_tr", "pT_ready", "pv_ready", "y_a", "ga_ready", "gs_ready", "go_ready",
                "osq_ready", "gss_ready", "grd_ready", "y_g", "conf_tr", "bn_ready", "conf_rstd",
                "conf_n", "conf_ln", "conf_sig", "y_c",
                "silu_ready", "hid_ready", "hid_tr", "hTh_ready",
                "hTl_ready", "logit_ready", "gap_ready", "egap_ready", "routed_ready",
                "rank_ready", "jobs_ready", "unh_ready", "unl_ready", "key_copied", "u32_act", "u32_dve", "over_ready", "xs_act", "xs_dve", "xT_tr", "sel_ready", "selT_tr", "wcol_ready",
                "gath_ready", "xh_ready", "xl_ready", "selT_ready", "yh_ready", "yl_ready",
                "scat_ready", "added", "out_ready", "stored",
                "aT_tr", "act_chain", "dve_chain", "pool_chain"):
            sems[name] = ctx.enter_context(nc.semaphore(name))
        loaded = [ctx.enter_context(nc.semaphore(f"loaded{i}")) for i in range(RING)]
        s = sems

        def bc(ap, shape):
            return ap.to_broadcast(shape)

        def col(i):
            return cols[:, i // P, i % P:i % P + 1]

        NORM1, NORM2, FUSE, CONVB, MCONVB, MCONVW, GLAB, KVG, QG1, QG2 = 0, 16, 32, 48, 52, 60, 92, 94, 96, 98
        CONVW = P

        def slot(n):
            return ring[:, n % RING, :]

        def jobs(eng, body):
            body(0, True)
            with eng.Fori(1, E) as j:
                body(j, False)
            eng.wait_ge(s["jobs_ready"], 1)
            n_over = eng.value_load(jobs_i[0:1, 3:4], min_val=0, max_val=OVER)
            with eng.If(n_over > 0):
                with eng.Fori(E, n_over + E) as j:
                    body(j, False)
            return n_over + E

        block = ctx.enter_context(nc.Block())

        @block.sync
        def _(sp):
            def load(n, dst_src, rounds=None):
                if rounds is not None:
                    sp.wait_ge(s["low_ready"], rounds * N_FFN + (n - RING + 1))
                elif n >= RING:
                    sp.wait_ge(s["low_ready"], n - RING + 1)
                assert len(dst_src) == 2
                for dst, src in dst_src:
                    sp.dma_start(dst, src).then_inc(loaded[n % RING], 16)

            def load_in(l, p):
                n = LAYER_PIECES[l] + p
                segs = W_IN_PIECES[p]
                width = sum(w for _, w in segs)
                dst = slot(n)[:, 0:KD * width].rearrange("p (k n) -> p k n", k=KD)
                src = w_in[l].rearrange("(k p) n -> p k n", p=P)
                if len(segs) == 2:
                    (c0, a), (c1, b) = segs
                    load(n, [(dst[:, :, 0:a], src[:, :, c0:c0 + a]),
                             (dst[:, :, a:a + b], src[:, :, c1:c1 + b])])
                else:
                    c0, a = segs[0]
                    half = KD // 2
                    load(n, [(dst[:, i:i + half, :], src[:, i:i + half, c0:c0 + a]) for i in (0, half)])

            def load_out(l, p):
                n = LAYER_PIECES[l] + N_IN + p
                dst = slot(n).rearrange("p (k n) -> p k n", k=2)
                src = w_out[l].rearrange("(k p) n -> p k n", p=P)
                load(n, [(dst[:, i:i + 1, :], src[:, 2 * p + i:2 * p + i + 1, :]) for i in (0, 1)])

            def load_ffn(n0, wg, wu, wd, rounds=None):
                for i, (kind, c) in enumerate(FFN_ORDER):
                    n = n0 + i
                    if kind == "d":
                        dst = slot(n).rearrange("p (f n) -> p f n", f=2)
                        src = wd.rearrange("(f p) n -> p f n", p=P)
                        load(n, [(dst[:, f:f + 1, :], src[:, 2 * c + f:2 * c + f + 1, :]) for f in (0, 1)], rounds)
                    else:
                        dst = slot(n).rearrange("p (k n) -> p k n", k=4)
                        k0 = 0 if kind == "a" else 4
                        load(n, [(dst[:, :, g * 256:(g + 1) * 256],
                                  w.rearrange("(k p) n -> p k n", p=P)[:, k0:k0 + 4, c * F_CH:(c + 1) * F_CH])
                                 for g, w in enumerate((wg, wu))], rounds)

            for t in range(TT):
                sp.dma_start(h[:, t, :], x[0, t * P:(t + 1) * P, :]).then_inc(s["x_in"], 16)
            for p in range(RING):
                load_in(0, p)
            for p in range(N_OUT):
                load_out(0, p)
            load_ffn(DENSE0, ffn_w_gate[0], ffn_w_up[0], ffn_w_down[0])
            for p in range(N_IN):
                load_in(1, p)
            for p in range(N_OUT):
                load_out(1, p)

            def expert(e, j):
                pick_e = lambda w: w[0, bass.ds(e, 1)].rearrange("a k n -> (a k) n")
                load_ffn(MOE0, pick_e(moe_w_gate), pick_e(moe_w_up), pick_e(moe_w_down), j)

            with sp.Fori(0, E) as j:
                expert(j, j)
            sp.wait_ge(s["jobs_ready"], 1)
            n_over = sp.value_load(jobs_i[0:1, 3:4], min_val=0, max_val=OVER)
            with sp.If(n_over > 0):
                with sp.Fori(0, n_over) as o:
                    e = sp.value_load(jobs_i[0:1, bass.ds(o, 1)], min_val=0, max_val=E - 1)
                    expert(e, o + E)
            sp.wait_ge(s["low_ready"], N_FFN * n_over + (MOE0 + N_FFN * E))
            sp.dma_start(fin_g, bc(final_norm_g.rearrange("(a d) -> a d", a=1), [P, D])).then_inc(s["final_in"], 16)
            sp.wait_ge(s["out_ready"], 1)
            sp.dma_start(out[0].rearrange("(t p) d -> p t d", p=P), h[:, :, :]).then_inc(s["stored"], 16)
            sp.wait_ge(s["stored"], 16)

        @block.gpsimd
        def _(pool):
            chain = Chain(pool, s["pool_chain"])
            fills = [pool.memset(ident[:, :], 0.0), pool.memset(ones[:, :], 1.0), pool.memset(epst[:, :], EPS),
                     pool.memset(mask_kt[:, :], 0.0), pool.memset(mask_qt[:, :], 0.0),
                     pool.memset(gla_mask[:, :, :], 32.0 ** -0.5), pool.memset(before[:, :], 1.0)]
            for i in range(16):
                pool.memset(invf[:, i:i + 1], float(np.float32(1.0) / np.float32(10000.0) ** np.float32(i / 16)))
            chain.done(pool.iota(iota[:, :], [[1, P]], base=0, channel_multiplier=0,
                                 allow_small_or_imprecise_dtypes=True))
            chain.wait()
            pool.affine_select(out=ident[:, :], in_=ident[:, :], compare_op=ALU.not_equal, fill=1.0,
                               base=0, pattern=[[-1, P]], channel_multiplier=1)
            pool.affine_select(out=mask_kt[:, :], in_=mask_kt[:, :], compare_op=ALU.is_ge, fill=NEG,
                               base=0, pattern=[[1, P]], channel_multiplier=-1)
            pool.affine_select(out=mask_qt[:, :], in_=mask_qt[:, :], compare_op=ALU.is_ge, fill=NEG,
                               base=0, pattern=[[-1, P]], channel_multiplier=1)
            for b in (0, 2):
                pool.affine_select(out=gla_mask[:, b, :], in_=gla_mask[:, b, :], compare_op=ALU.is_ge, fill=0.0,
                                   base=0, pattern=[[1, P]], channel_multiplier=-1)
            pool.affine_select(out=before[:, :], in_=before[:, :], compare_op=ALU.is_ge, fill=0.0,
                               base=-1, pattern=[[1, P]], channel_multiplier=-1).then_inc(s["consts"], 1)

            pool.dma_start(pos_i[:, :], positions.rearrange("a (t p) -> p (a t)", p=P),
                           allow_slow_non_contiguous=True).then_inc(s["pos_in"], 16)
            for l in range(DEPTH):
                pool.dma_start(gate_b[:, l, :], bc(mlstm_gate_b[l:l + 1, :], [P, 8])).then_inc(s["gateb_in"], 16)
            pool.dma_start(router[:, :, :], moe_router[0].rearrange("(k p) e -> p k e", p=P)).then_inc(s["router_in"], 16)
            for l in range(DEPTH):
                if l:
                    pool.wait_ge(s["conf_ln"], l)
                for i, src in enumerate((conv_ln_g, conv_ln_b)):
                    pool.dma_start(ln_gb[:, i, :], bc(src[l:l + 1, :], [P, 256])).then_inc(s["ln_in"], 16)
                pool.wait_ge(s["qk_sig"], l + 1)
                pool.tensor_tensor(qkc[:, :, :], qkc[:, :, :], qkpre[:, :, 0:S], ALU.mult).then_inc(s["qk_ready"], 1)
                pool.wait_ge(s["piece_used"], LAYER_PIECES[l] + N_IN)
                pool.dma_start(walpha[:, :], gla_w_alpha[l]).then_inc(s["ukv_in"], 16)
                pool.dma_start(uq[:, 0, :], mla_w_uq[l, 0:P, :]).then_inc(s["ukv_in"], 16)
                pool.dma_start(uq[0:64, 1, :], mla_w_uq[l, P:192, :]).then_inc(s["ukv_in"], 16)
                pool.dma_start(ukv[:, :], mla_w_ukv[l]).then_inc(s["ukv_in"], 16)
                pool.wait_ge(s["gla_exp"], l + 1)
                q, k = gqk[:, 0, :], gqk[:, 1, :]
                for i, part in enumerate((q[:, 0:P], q[:, P:S], k[:, 0:P], k[:, 0:P], k[:, P:S])):
                    last = pool.tensor_tensor(gE[:, i, :], gE[:, i, :], part, ALU.mult)
                last.then_inc(s["gla_qk"], 1)
                pool.wait_ge(s["ln_in"], 32 * (l + 1))
                pool.wait_ge(s["conf_n"], l + 1)
                chain.done(pool.tensor_tensor(ctok[:, :, :], ctok[:, :, :],
                                              bc(ln_gb[:, 0:1, :], [P, TT, 256]), ALU.mult))
                chain.wait()
                pool.tensor_tensor(ctok[:, :, :], ctok[:, :, :], bc(ln_gb[:, 1:2, :], [P, TT, 256]),
                                   ALU.add).then_inc(s["conf_ln"], 1)
            for name in ("y_m", "y_a", "y_g", "y_c"):
                pool.wait_ge(s[name], DEPTH)
            pool.dma_start(moe_g[:, :], bc(norm2_g[DEPTH - 1:DEPTH, :], [P, D])).then_inc(s["moe_g_in"], 16)

        @block.scalar
        def _(act):
            chain = Chain(act, s["act_chain"])
            next_piece = [0]

            def split_high(n, job=None, width=PIECE):
                jobbed = job is not None
                rounds, pieces = (3 * job, N_FFN * job) if jobbed else (0, 0)
                act.wait_ge(loaded[n % RING], 32 * rounds + 32 * (n // RING + 1))
                if jobbed or n >= SPLIT:
                    act.wait_ge(s["piece_used"], pieces + (n - SPLIT + 1))
                act.activation(high[:, n % SPLIT, 0:width], slot(n)[:, 0:width], ACT.Copy).then_inc(s["high_ready"], 1)

            def in_width(p):
                return KD * sum(w for _, w in W_IN_PIECES[p])

            def norm(k, source, groups, wait):
                act.preload_act_table_set(LN_EXP)
                wait()
                w = D // groups
                for t in range(TT):
                    for g in range(groups):
                        chain.done(act.activation(un[:, t, g * w:(g + 1) * w], source[:, t, g * w:(g + 1) * w],
                                                  ACT.Square, accum_out=ss[:, t, g:g + 1]))
                chain.wait()
                chain.done(act.activation(lnv[:, :, 0:groups], ss[:, :, 0:groups], ACT.Ln, bias=epst[:, :], scale=1.0 / w))
                chain.wait()
                act.activation(rstd[:, :, 0:groups], lnv[:, :, 0:groups], ACT.Exp, scale=-0.5).then_inc(s["rstd_ready"], 1)

            def gains(k, first):
                for g in range(4):
                    act.wait_ge(s["norm_tr"], 4 * k + g + 1)
                    for i in range(2):
                        kd = 2 * g + i
                        last = act.activation(uTh[:, kd, :], bank[NORM_BANKS[g]][:, i * S:(i + 1) * S], ACT.Copy,
                                              scale=col(first + kd))
                    last.then_inc(s["uth_ready"], 1)

            def ffn(n0, job, job_n, tiles, after_split={}, after_chunk={}, scale=None):
                done = [0]

                def upto(i):
                    while done[0] <= min(i, N_FFN - 1):
                        split_high(n0 + done[0], job)
                        after_split.get(done[0], lambda: None)()
                        done[0] += 1

                for c in range(CHUNKS):
                    at = FFN_AT[("b", c)]
                    upto(at + 2)
                    act.wait_ge(s["piece_used"], (N_FFN * job if job is not None else 0) + (n0 + at + 1))
                    for t in range(tiles):
                        last = act.activation(sg[:, t, :], bank[t][:, 0:256], ACT.Silu,
                                              scale=1.0 if scale is None else scale[:, t, 0:1])
                    last.then_inc(s["silu_ready"], 1)
                    upto(at + 3)
                    act.wait_ge(s["hid_tr"], job_n * CHUNKS + (c + 1))
                    act.activation(hTh[:, :, 0:tiles, :],
                                   bank[4][:, 0:2 * tiles * P].rearrange("p (f t n) -> p f t n", f=2, t=tiles),
                                   ACT.Copy).then_inc(s["hTh_ready"], 1)
                    after_chunk.get(c, lambda: None)()

            act.wait_ge(s["stage_zero"], 1)
            rows = lambda i, n: stage[i:i + n, 0, :]
            for dst, src in [
                    (rows(NORM1, 16), norm1_g.rearrange("l (k p) -> (l k) p", p=P)),
                    (rows(NORM2, 16), norm2_g.rearrange("l (k p) -> (l k) p", p=P)),
                    (rows(FUSE, 16), fuse_g.rearrange("l (k p) -> (l k) p", p=P)),
                    (rows(CONVB, 4), conv_b.rearrange("l (k p) -> (l k) p", p=P)),
                    (rows(MCONVB, 8), mlstm_conv_b.rearrange("l (k p) -> (l k) p", p=P)),
                    (rows(MCONVW, 32), mlstm_conv_w.rearrange("l i (k p) -> (l i k) p", p=P)),
                    (rows(GLAB, 2), gla_b_alpha),
                    (rows(KVG, 2), mla_kv_norm_g),
                    (rows(QG1, 2), mla_q_norm_g[:, 0:P]),
                    (stage[QG2:QG2 + 2, 0, 0:64], mla_q_norm_g[:, P:192]),
                    (stage[0:2 * CONV * DEPTH, 1, :], conv_w.rearrange("l i (k p) -> (l i k) p", p=P))]:
                act.dma_start(dst, src).then_inc(s["rows_in"], 16)
            act.preload_act_table_set(LN_EXP)
            act.wait_ge(s["x_in"], 32)
            act.wait_ge(s["consts"], 1)
            for l in range(DEPTH):
                n0 = LAYER_PIECES[l]
                norm(3 * l, h, 1, (lambda: act.wait_ge(s["h_ready"], 4)) if l else (lambda: None))
                if l == 0:
                    act.wait_ge(s["cols_ready"], 1)
                gains(3 * l, NORM1 + KD * l)
                act.preload_act_table(ACT.Sigmoid)
                for n in range(SPLIT):
                    split_high(n0 + n, width=in_width(n))
                for p in range(N_IN):
                    if p + SPLIT < N_IN:
                        split_high(n0 + p + SPLIT, width=in_width(p + SPLIT))
                    src = bank[Z_BANKS[p % 4]]
                    tiles2 = lambda w: src[:, 0:TT * w].rearrange("p (t n) -> p t n", t=TT)
                    if p in (1, 4, 5, 6, 7, 8, 9, 10):
                        act.wait_ge(s["piece_used"], n0 + p + 1)
                    if p == 1:
                        act.activation(gsig[:, :, :], tiles2(256), ACT.Sigmoid).then_inc(s["z_act"], 1)
                    if p == 4:
                        act.activation(zif[:, :, :], tiles2(200), ACT.Copy).then_inc(s["z_act"], 1)
                    if p == 5:
                        act.activation(zkv[:, :, :], tiles2(176), ACT.Copy).then_inc(s["z_act"], 1)
                    if p == 6:
                        act.wait_ge(s["aT_tr"], l + 1)
                        act.activation(aT[:, :], bank[7][0:16, 0:S], ACT.Copy).then_inc(s["z_act"], 1)
                        act.activation(gqk[:, :, :], tiles2(256), ACT.Copy).then_inc(s["z_act"], 1)
                    if p == 7:
                        act.activation(vaug[:, :, :, 0:DH], src[:, :].rearrange("p (t h n) -> p t h n", t=TT, h=HEADS),
                                       ACT.Copy).then_inc(s["z_act"], 1)
                        act.wait_ge(s["qk_conv"], l + 1)
                        act.activation(qkpre[:, :, 0:S], qkc[:, :, :], ACT.Sigmoid).then_inc(s["qk_sig"], 1)
                    if p == 8:
                        act.activation(osig[:, :, :], tiles2(256), ACT.Sigmoid).then_inc(s["z_act"], 1)
                    if p == 9:
                        act.activation(gv[:, :, :], tiles2(256), ACT.Copy).then_inc(s["z_act"], 1)
                    if p == 10:
                        act.activation(grs[:, :, :], tiles2(256), ACT.Sigmoid).then_inc(s["z_act"], 1)

                act.preload_act_table_set(LN_EXP)
                if l == 0:
                    act.wait_ge(s["ang_ready"], 1)
                    act.activation(cossin[:, :, :, :], ang[:, :, :, :], ACT.Sin).then_inc(s["sin_ready"], 1)
                for t in range(TT):
                    chain.done(act.activation(qtok[:, t, :, :].rearrange("p h n -> p (h n)")[:, 0:192],
                                              zif[:, t, 8:200], ACT.Square, accum_out=lss[:, 0, t:t + 1]))
                    chain.done(act.activation(ktok[:, t, :, :].rearrange("p h n -> p (h n)")[:, 0:128],
                                              zkv[:, t, 0:128], ACT.Square, accum_out=lss[:, 1, t:t + 1]))
                chain.wait()
                chain.done(act.activation(lln[:, 0, :], lss[:, 0, :], ACT.Ln, bias=epst[:, :], scale=1.0 / 192))
                chain.done(act.activation(lln[:, 1, :], lss[:, 1, :], ACT.Ln, bias=epst[:, :], scale=1.0 / 128))
                chain.wait()
                act.activation(lrs[:, :, :], lln[:, :, :], ACT.Exp, scale=-0.5).then_inc(s["lat_rstd"], 1)
                act.wait_ge(s["gates_abs"], l + 1)
                chain.done(act.activation(gln[:, :, :], gab[:, :, :], ACT.Exp))
                chain.wait()
                act.activation(gln[:, :, :], gln[:, :, :], ACT.Ln, bias=1.0).then_inc(s["gates_ln"], 1)
                act.wait_ge(s["gla_abs"], l + 1)
                chain.done(act.activation(gab2[:, :], gab2[:, :], ACT.Exp))
                chain.wait()
                act.activation(gab2[:, :], gab2[:, :], ACT.Ln, bias=1.0).then_inc(s["gla_ln"], 1)
                act.wait_ge(s["mcum_ready"], l + 1)
                act.activation(expnm[:, :], mrun[:, :], ACT.Exp, scale=-1.0).then_inc(s["expnm_ready"], 1)
                act.wait_ge(s["q_ready"], l + 1)
                for t in range(TT):
                    src = bank[(3, 5)[t]][:, 0:384].rearrange("p (h n) -> p h n", h=HEADS)
                    act.activation(rin[:, t, 0:4, :], src[:, :, 64:96], ACT.Copy)
                    act.activation(qtok[:, t, :, 0:64], src[:, :, 0:64], ACT.Copy)
                act.activation(rin[:, :, 4, :], zkv[:, :, 128:160], ACT.Copy)
                act.wait_ge(s["kv_ready"], l + 1)
                for t in range(TT):
                    src = bank[(6, 1)[t]][:, :].rearrange("p (h n) -> p h n", h=HEADS)
                    act.activation(ktok[:, t, :, 0:64], src[:, :, 0:64], ACT.Copy)
                    last = act.activation(vm[:, t, :].rearrange("p (h n) -> p h n", h=HEADS), src[:, :, 64:128], ACT.Copy)
                last.then_inc(s["qkv_evac"], 1)
                act.wait_ge(s["gla_cum"], l + 1)
                for i in range(2):
                    act.activation(gE[:, i, :], b16[:, i * P:(i + 1) * P], ACT.Exp, bias=gref[:, 0, i:i + 1], scale=1.0 / 16)
                act.activation(gE[:, 2, :], b16[:, 0:P], ACT.Exp, bias=gref[:, 1, 0:1], scale=-1.0 / 16)
                act.activation(gE[:, 3:5, :].rearrange("p a n -> p (a n)"), b16[:, :], ACT.Exp,
                               bias=gref[:, 1, 1:2], scale=-1.0 / 16).then_inc(s["gla_exp"], 1)
                act.wait_ge(s["mcol_ready"], l + 1)
                for hd in range(HEADS):
                    act.wait_ge(s["x_ready"], HEADS * l + hd + 1)
                    xb = bank[(2, 4, 7, 0)[hd]]
                    act.activation(dec[:, hd, 0:256], xb[:, 0:256], ACT.Exp, bias=mcol[:, hd:hd + 1])
                    act.activation(dec[:, hd, 256:384], xb[:, 256:384], ACT.Exp,
                                   bias=mcol[:, 4 + hd:5 + hd]).then_inc(s["dt_ready"], 1)
                for i in range(2):
                    act.wait_ge(s["qkT_tr"], 4 * l + i + 1)
                    act.activation(qT[:, 2 * i:2 * i + 2, :], bank[(2, 4)[i]][0:96, :].rearrange("p (h n) -> p h n", h=2),
                                   ACT.Copy).then_inc(s["qT_ready"], 1)
                act.wait_ge(s["bn_ready"], l + 1)
                chain.done(act.activation(bst[:, :, 0], bag[:, :, 1], ACT.Ln, bias=epst[:, :]))
                chain.wait()
                act.activation(bst[:, :, 1], bst[:, :, 0], ACT.Exp, scale=-0.5).then_inc(s["conf_rstd"], 1)
                act.wait_ge(s["smax_ready"], l + 1)
                scale = 96.0 ** -0.5
                for hd in range(HEADS):
                    chain.done(act.activation(probs[:, hd * P:(hd + 1) * P], bank[6][:, hd * P:(hd + 1) * P], ACT.Exp,
                                              bias=smax[:, 0, hd:hd + 1], scale=scale, accum_out=psums[:, 0, hd:hd + 1]))
                for hd in range(HEADS):
                    src = bank[(0, 1)[hd // 2]][:, (hd % 2) * S:(hd % 2 + 1) * S]
                    last = act.activation(probs[:, 512 + hd * S:512 + (hd + 1) * S], src, ACT.Exp,
                                          bias=smax[:, 1, hd:hd + 1], scale=scale, accum_out=psums[:, 1, hd:hd + 1])
                last.then_inc(s["p_ready"], 1)
                act.wait_ge(s["go_ready"], l + 1)
                act.activation(osq[:, :, :, :].rearrange("p t h n -> p (t h n)"), bank[7][:, :],
                               ACT.Square).then_inc(s["osq_ready"], 1)
                act.wait_ge(s["gss_ready"], l + 1)
                chain.done(act.activation(gls[:, :, :], gss[:, :, :], ACT.Ln, bias=epst[:, :], scale=1.0 / DH))
                chain.wait()
                act.activation(grd[:, :, :], gls[:, :, :], ACT.Exp, scale=-0.5).then_inc(s["grd_ready"], 1)
                act.preload_act_table(ACT.Sigmoid)
                for i in range(3):
                    act.wait_ge(s["p_tr"], 3 * l + i + 1)
                    act.activation(probT[:, i, :, :], bank[(3, 5, 6)[i]][:, :].rearrange("p (h n) -> p h n", h=HEADS),
                                   ACT.Copy).then_inc(s["pT_ready"], 1)
                act.wait_ge(s["conf_ln"], l + 1)
                act.activation(cacc[:, :, :], ctok[:, :, :],
                               ACT.Sigmoid).then_inc(s["conf_sig"], 1)

                def mixers_done():
                    for name in ("y_m", "y_a", "y_g", "y_c"):
                        act.wait_ge(s[name], l + 1)
                norm(3 * l + 1, y, 4, mixers_done)
                for n in range(SPLIT):
                    split_high(n0 + N_IN + n)
                gains(3 * l + 1, FUSE + KD * l)
                split_high(n0 + N_IN + SPLIT)
                if l == 0:
                    gains(3 * l + 2, NORM2 + KD * l)
                    norm(3 * l + 2, h, 1, lambda: act.wait_ge(s["h_ready"], 4 * l + 2))
                    act.preload_act_table(ACT.Silu)
                    ffn(DENSE0, None, 0, TT, scale=rstd)
            for g in (0, 1):
                act.wait_ge(s["norm_tr"], 4 * 5 + g + 1)
                for i in range(2):
                    kd = 2 * g + i
                    last = act.activation(u32[:, kd, :], bank[NORM_BANKS[g]][:, i * S:(i + 1) * S], ACT.Copy,
                                          scale=col(NORM2 + KD + kd))
                last.then_inc(s["u32_act"], 1)
            norm(5, h, 1, lambda: act.wait_ge(s["h_ready"], 6))

            for t in range(TT):
                act.wait_ge(s["ung_ready"], t + 1)
                act.activation(unh[:, t, :], un[:, t, :], ACT.Copy).then_inc(s["unh_ready"], 1)
            act.wait_ge(s["gap_ready"], 1)
            act.activation(egap[:, :], gap[:, :], ACT.Exp).then_inc(s["egap_ready"], 1)
            act.preload_act_table(ACT.Silu)

            def tokens_out(n):
                act.wait_ge(s["gath_ready"], n + 1)
                act.activation(xs[:, 0:4, :], bank[5][:, :].rearrange("p (k n) -> p k n", k=4), ACT.Copy).then_inc(s["xs_act"], 1)

            def tokens_high(j):
                act.wait_ge(s["xT_tr"], j + 1)
                for i in range(2):
                    last = act.activation(xh[:, 4 * i:4 * i + 4, :], bank[5 + i][:, :].rearrange("p (k n) -> p k n", k=4), ACT.Copy)
                last.then_inc(s["xh_ready"], 1)

            def result_high(n):
                act.wait_ge(s["piece_used"], N_FFN * n + MOE0)
                for i in range(2):
                    last = act.activation(yh[:, i * 512:(i + 1) * 512], bank[2 + i][:, :], ACT.Copy, scale=wslot[:, :])
                last.then_inc(s["yh_ready"], 1)

            def job(j, first):
                def slots():
                    act.wait_ge(s["selT_tr"], j + 1)
                    if not first:
                        act.wait_ge(s["yl_ready"], j)
                    act.activation(selT[:, :, :], bank[7][:, 0:2 * P].rearrange("p (t n) -> p t n", t=TT), ACT.Copy)
                    act.activation(wslot[:, :], bank[7][:, 2 * P:2 * P + 1], ACT.Copy).then_inc(s["selT_ready"], 1)

                def next_tokens():
                    act.wait_ge(s["piece_used"], N_FFN * j + (MOE0 + FFN_AT[("b", CHUNKS - 1)] + 1))
                    tokens_high(j + 1)

                ffn(MOE0, j, j + 1, 1, {} if first else {2: lambda: result_high(j)},
                    {SLOTS_AT: slots, GATHER_AT: lambda: tokens_out(j + 1), CHUNKS - 1: next_tokens})

            tokens_out(0)
            tokens_high(0)
            result_high(jobs(act, job))
            norm(6, h, 1, lambda: act.wait_ge(s["h_ready"], 8))

        @block.vector
        def _(dve):
            chain = Chain(dve, s["dve_chain"])

            def split_low(n, job=None, width=PIECE):
                pieces = N_FFN * job if job is not None else 0
                dve.wait_ge(s["high_ready"], pieces + (n + 1))
                dve.tensor_tensor(low[:, n % SPLIT, 0:width], slot(n)[:, 0:width],
                                  high[:, n % SPLIT, 0:width].bitcast(F32), ALU.subtract).then_inc(s["low_ready"], 1)

            def in_width(p):
                return KD * sum(w for _, w in W_IN_PIECES[p])

            def normalize(k, source, groups):
                dve.wait_ge(s["rstd_ready"], k + 1)
                if groups == 1:
                    for t in range(TT):
                        last = dve.tensor_scalar(un[:, t, :], source[:, t, :], rstd[:, t, 0:1], None, ALU.mult)
                else:
                    w = D // groups
                    last = dve.tensor_tensor(
                        un[:, :, :].rearrange("p t (g n) -> p (t g) n", g=groups),
                        source[:, :, :].rearrange("p t (g n) -> p (t g) n", g=groups),
                        bc(rstd[:, :, :].rearrange("p t g -> p (t g)").unsqueeze(2), [P, TT * groups, w]), ALU.mult)
                last.then_inc(s["un_ready"], 1)

            def gains(k, first):
                for g in range(4):
                    dve.wait_ge(s["uth_ready"], 4 * k + g + 1)
                    for i in range(2):
                        kd = 2 * g + i
                        last = dve.scalar_tensor_tensor(
                            out=uTl[:, kd, :], in0=bank[NORM_BANKS[g]][:, i * S:(i + 1) * S], scalar=col(first + kd),
                            in1=uTh[:, kd, :].bitcast(F32), op0=ALU.mult, op1=ALU.subtract)
                    last.then_inc(s["utl_ready"], 1)

            def ffn(n0, job, job_n, tiles, after_split={}, after_chunk={}, scale=None):
                done = [0]

                def upto(i):
                    while done[0] <= min(i, N_FFN - 1):
                        split_low(n0 + done[0], job)
                        after_split.get(done[0], lambda: None)()
                        done[0] += 1

                for c in range(CHUNKS):
                    at = FFN_AT[("b", c)]
                    upto(at + 2)
                    dve.wait_ge(s["silu_ready"], job_n * CHUNKS + (c + 1))
                    for t in range(tiles):
                        if scale is None:
                            last = dve.tensor_tensor(hid[:, t, :], bank[t][:, 256:512], sg[:, t, :], ALU.mult)
                        else:
                            last = dve.scalar_tensor_tensor(out=hid[:, t, :], in0=bank[t][:, 256:512], scalar=scale[:, t, 0:1],
                                                            in1=sg[:, t, :], op0=ALU.mult, op1=ALU.mult)
                    last.then_inc(s["hid_ready"], 1)
                    upto(at + 3)
                    dve.wait_ge(s["hTh_ready"], job_n * CHUNKS + (c + 1))
                    dve.tensor_tensor(hTl[:, :, 0:tiles, :],
                                      bank[4][:, 0:2 * tiles * P].rearrange("p (f t n) -> p f t n", f=2, t=tiles),
                                      hTh[:, :, 0:tiles, :].bitcast(F32), ALU.subtract).then_inc(s["hTl_ready"], 1)
                    after_chunk.get(c, lambda: None)()

            def add_to_h(banks, sem, values):
                for i, b in enumerate(banks):
                    t, half = divmod(i, 2)
                    dve.wait_ge(sem, values[i])
                    dst = h[:, t, half * 512:(half + 1) * 512]
                    last = dve.tensor_tensor(dst, bank[b][:, :], dst, ALU.add)
                    if half == 1:
                        last.then_inc(s["h_ready"], 1)

            def angles():
                c1 = 6.28125
                c2 = float(np.float32(2 * math.pi - c1))
                c3 = 2 * math.pi - c1 - c2
                magic = 1.5 * 2.0 ** 23
                dve.wait_ge(s["pos_in"], 16)
                chain.done(dve.tensor_copy(pos_f[:, :], pos_i[:, :]))
                chain.wait()
                for i in range(2):
                    for t in range(TT):
                        chain.done(dve.tensor_scalar(ang[:, i, t, :], invf[:, :], pos_f[:, t:t + 1], None, ALU.mult))
                chain.wait()
                for i in range(2):
                    chain.done(dve.tensor_scalar(turn[:, i, :, :], ang[:, i, :, :], 1 / (2 * math.pi),
                                                 0.0 if i else 0.25, ALU.mult, ALU.add))
                chain.wait()
                for v in (magic, -magic):
                    chain.done(dve.tensor_scalar(turn[:, :, :, :], turn[:, :, :, :], v, None, ALU.add))
                    chain.wait()
                flat = lambda a: a[:, :, :, :].rearrange("p i t n -> p (i t n)")
                for c in (c1, c2, c3):
                    chain.done(dve.scalar_tensor_tensor(out=flat(ang), in0=flat(turn), scalar=-c, in1=flat(ang),
                                                        op0=ALU.mult, op1=ALU.add))
                    chain.wait()
                chain.done(dve.tensor_scalar(ang[:, 0, :, :], ang[:, 0, :, :], math.pi / 2, None, ALU.add))
                chain.wait()
                lim = float(np.nextafter(np.float32(math.pi), np.float32(0)))
                dve.tensor_scalar(flat(ang), flat(ang), lim, -lim, ALU.min, ALU.max).then_inc(s["ang_ready"], 1)

            dve.memset(stage[:, :, :], 0.0).then_inc(s["stage_zero"], 1)
            dve.wait_ge(s["cols_tr"], 1)
            dve.tensor_copy(cols[:, :, :], bank[7][:, 0:2 * P].rearrange("p (a n) -> p a n", a=2)).then_inc(s["cols_ready"], 1)
            dve.wait_ge(s["cols_ready"], 1)
            for l in range(DEPTH):
                n0 = LAYER_PIECES[l]
                normalize(3 * l, h, 1)
                gains(3 * l, NORM1 + KD * l)
                dve.memset(glu[:, :, 0:CONV - 1], 0.0)
                dve.memset(qkpre[:, :, 0:MCONV - 1], 0.0)
                chain.done(dve.memset(vaug[:, :, :, DH:DH + 1], 1.0))
                for n in range(SPLIT):
                    split_low(n0 + n, width=in_width(n))

                def conv_step(i):
                    tap, c = divmod(i, 2)
                    taps = glu[:, c, tap:tap + S]
                    w = col(CONVW + (l * CONV + tap) * 2 + c)
                    chain.wait(1)
                    if tap == 0:
                        ins = dve.tensor_scalar(cacc[:, c, :], taps, w, col(CONVB + 2 * l + c), ALU.mult, ALU.add)
                    else:
                        ins = dve.scalar_tensor_tensor(out=cacc[:, c, :], in0=taps, scalar=w, in1=cacc[:, c, :],
                                                       op0=ALU.mult, op1=ALU.add)
                    chain.done(ins)
                    if i == 2 * CONV - 1:
                        chain.wait()

                def qk_step(i):
                    tap, c = divmod(i, 4)
                    taps = qkpre[:, c, tap:tap + S]
                    w = col(MCONVW + (l * MCONV + tap) * 4 + c)
                    chain.wait(3)
                    if tap == 0:
                        ins = dve.tensor_scalar(qkc[:, c, :], taps, w, col(MCONVB + 4 * l + c), ALU.mult, ALU.add)
                    else:
                        ins = dve.scalar_tensor_tensor(out=qkc[:, c, :], in0=taps, scalar=w, in1=qkc[:, c, :],
                                                       op0=ALU.mult, op1=ALU.add)
                    chain.done(ins)

                conv_at = [0]

                def conv_steps(n):
                    for _ in range(n):
                        if conv_at[0] < 2 * CONV:
                            conv_step(conv_at[0])
                            conv_at[0] += 1

                for p in range(N_IN):
                    if p + SPLIT < N_IN:
                        split_low(n0 + p + SPLIT, width=in_width(p + SPLIT))
                    src = bank[Z_BANKS[p % 4]]
                    if p == 1:
                        dve.wait_ge(s["z_act"], 9 * l + 1)
                        chain.wait()
                        ins = dve.tensor_tensor(glu[:, :, CONV - 1:], bank[Z_BANKS[0]][:, :].rearrange("p (c n) -> p c n", c=2),
                                                gsig[:, :, :], ALU.mult)
                        ins.then_inc(s["z_dve"], 1)
                        dve.wait_ge(s["z_dve"], 4 * l + 1)
                    if p in (2, 3):
                        dve.wait_ge(s["piece_used"], n0 + p + 1)
                        c = 2 * (p - 2)
                        dve.tensor_copy(qkpre[:, c:c + 2, MCONV - 1:], src[:, :].rearrange("p (c n) -> p c n", c=2)).then_inc(s["z_dve"], 1)
                    if p == 4:
                        dve.wait_ge(s["z_dve"], 4 * l + 3)
                        for i in range(4 * MCONV):
                            qk_step(i)
                        chain.wait()
                        dve.memset(tiny[:, :], 0.0).then_inc(s["qk_conv"], 1)
                    elif p >= 1:
                        conv_steps(8)
                    if p == 10:
                        dve.wait_ge(s["z_act"], 9 * l + 9)
                        dve.tensor_tensor(grs[:, :, :], src[:, :].rearrange("p (t n) -> p t n", t=TT),
                                          grs[:, :, :], ALU.mult).then_inc(s["z_dve"], 1)
                        dve.wait_ge(s["z_dve"], 4 * l + 4)
                conv_steps(2 * CONV)
                if l == 0:
                    angles()
                dve.memset(tiny[:, :], 0.0).then_inc(s["conv_done"], 1)

                dve.wait_ge(s["piece_used"], n0 + N_IN)
                dve.wait_ge(s["gateb_in"], 32)
                chain.done(dve.tensor_tensor(gb[:, :, :], zif[:, :, 0:8], bc(gate_b[:, l:l + 1, :], [P, TT, 8]), ALU.add))
                chain.wait()
                chain.done(dve.tensor_scalar(gmn[:, :, :], gb[:, :, 4:8], 0.0, None, ALU.min))
                chain.done(dve.tensor_scalar(gab[:, :, :], gb[:, :, 4:8], 0.0, None, ALU.max))
                chain.wait()
                dve.tensor_tensor(gab[:, :, :], gmn[:, :, :], gab[:, :, :], ALU.subtract).then_inc(s["gates_abs"], 1)
                dve.wait_ge(s["lat_rstd"], l + 1)
                for t in range(TT):
                    dve.tensor_scalar(zif[:, t, 8:200], zif[:, t, 8:200], lrs[:, 0, t:t + 1], None, ALU.mult)
                    last = dve.tensor_scalar(zkv[:, t, 0:128], zkv[:, t, 0:128], lrs[:, 1, t:t + 1], None, ALU.mult)
                last.then_inc(s["lat_ready"], 1)
                dve.wait_ge(s["gates_ln"], l + 1)
                dve.tensor_tensor(gb[:, :, 4:8], gmn[:, :, :], gln[:, :, :], ALU.subtract).then_inc(s["lf_ready"], 1)
                dve.wait_ge(s["gpre_ready"], l + 1)
                chain.done(dve.tensor_scalar(gx[:, :], bank[0][:, 0:S], col(GLAB + l), None, ALU.add))
                chain.wait()
                chain.done(dve.tensor_scalar(gmn2[:, :], gx[:, :], 0.0, None, ALU.min))
                chain.done(dve.tensor_scalar(gab2[:, :], gx[:, :], 0.0, None, ALU.max))
                chain.wait()
                dve.tensor_tensor(gab2[:, :], gmn2[:, :], gab2[:, :], ALU.subtract).then_inc(s["gla_abs"], 1)
                dve.wait_ge(s["lat_tr"], l + 1)
                dve.tensor_scalar(cqT[:, 0, :], bank[4][:, 0:S], col(QG1 + l), None, ALU.mult)
                dve.tensor_scalar(cqT[0:64, 1, :], bank[4][0:64, S:2 * S], cols[0:64, 0, QG2 + l:QG2 + l + 1], None, ALU.mult)
                dve.tensor_scalar(ckvT[:, :], bank[7][:, 0:S], col(KVG + l), None, ALU.mult).then_inc(s["lat_T"], 1)
                dve.wait_ge(s["gate_tr"], l + 1)
                chain.done(dve.tensor_tensor_scan(cumf[:, :], ones[0:4, :], bank[2][0:4, S:2 * S], 0.0, ALU.mult, ALU.add))
                chain.wait()
                chain.done(dve.tensor_tensor(aj[:, :], bank[2][0:4, 0:S], cumf[:, :], ALU.subtract))
                chain.wait()
                chain.done(dve.tensor_tensor_scan(mrun[:, :], aj[:, :], aj[:, :], 0.0, ALU.max, ALU.max))
                chain.wait()
                dve.tensor_scalar(negm[:, :], mrun[:, :], -1.0, None, ALU.mult)
                dve.tensor_tensor(mrun[:, :], mrun[:, :], cumf[:, :], ALU.add).then_inc(s["mcum_ready"], 1)
                dve.wait_ge(s["gla_ln"], l + 1)
                chain.done(dve.tensor_tensor(gmn2[:, :], gmn2[:, :], gab2[:, :], ALU.subtract))
                chain.wait()
                chain.done(dve.tensor_tensor_scan(b16[:, :], ones[:, :], gmn2[:, :], 0.0, ALU.mult, ALU.add))
                chain.wait()
                for i in range(2):
                    mid = b16[:, i * P + P // 2:i * P + P // 2 + 1]
                    dve.tensor_scalar(gref[:, 0, i:i + 1], mid, -1.0 / 16, None, ALU.mult)
                    last = dve.tensor_scalar(gref[:, 1, i:i + 1], mid, 1.0 / 16, None, ALU.mult)
                last.then_inc(s["gla_cum"], 1)
                dve.wait_ge(s["mcol_tr"], l + 1)
                dve.tensor_copy(mcol[:, :], bank[0][:, 0:16]).then_inc(s["mcol_ready"], 1)
                if l == 0:
                    dve.wait_ge(s["sin_ready"], 1)
                dve.wait_ge(s["qkv_evac"], l + 1)
                cos = bc(cossin[:, 0, :, :].unsqueeze(2), [P, TT, 5, 16])
                sin = bc(cossin[:, 1, :, :].unsqueeze(2), [P, TT, 5, 16])
                x1, x2 = rin[:, :, :, 0:16], rin[:, :, :, 16:32]
                for lo, (a, ca, b, cb, op) in ((0, (x1, cos, x2, sin, ALU.subtract)), (16, (x2, cos, x1, sin, ALU.add))):
                    chain.done(dve.tensor_tensor(rt1[:, :, :, :], a, ca, ALU.mult))
                    chain.done(dve.tensor_tensor(rt2[:, :, :, :], b, cb, ALU.mult))
                    chain.wait()
                    chain.done(dve.tensor_tensor(rot[:, :, :, lo:lo + 16], rt1[:, :, :, :], rt2[:, :, :, :], op))
                    chain.wait()
                for t in range(TT):
                    dve.tensor_copy(qtok[:, t, :, 64:96], rot[:, t, 0:4, :])
                    last = dve.tensor_copy(ktok[:, t, :, 64:96], bc(rot[:, t, 4:5, :], [P, HEADS, 32]))
                last.then_inc(s["rot_ready"], 1)
                for hd in range(HEADS):
                    dve.wait_ge(s["dt_ready"], HEADS * l + hd + 1)
                    dve.wait_ge(s["s_ready"], HEADS * l + hd + 1)
                    dve.scalar_tensor_tensor(out=dec[:, hd, :], in0=bank[(1, 3, 5, 6)[hd]][:, 0:384], scalar=DH ** -0.5,
                                             in1=dec[:, hd, :], op0=ALU.mult, op1=ALU.mult).then_inc(s["pt_ready"], 1)
                for i in range(2):
                    dve.wait_ge(s["qkT_tr"], 4 * l + 2 + i + 1)
                    dve.tensor_copy(kT[:, 2 * i:2 * i + 2, :], bank[(7, 0)[i]][0:96, :].rearrange("p (h n) -> p h n", h=2)).then_inc(s["kT_ready"], 1)
                dve.wait_ge(s["conf_tr"], l + 1)
                for t in range(TT):
                    chain.done(dve.bn_stats(bst[:, t, :], bank[1][:, t * 256:(t + 1) * 256]))
                chain.wait()
                for t in range(TT):
                    last = dve.bn_aggr(bag[:, t, :], bst[:, t, :])
                last.then_inc(s["bn_ready"], 1)
                for hd in range(HEADS):
                    dve.wait_ge(s["ga_ready"], HEADS * l + hd + 1)
                    dve.tensor_tensor(gS[:, hd, :, :], bank[(3, 5, 6, 7)[hd]][:, 0:384].rearrange("p (b n) -> p b n", b=3),
                                      gla_mask[:, :, :], ALU.mult).then_inc(s["gs_ready"], 1)
                dve.wait_ge(s["conf_rstd"], l + 1)
                for t in range(TT):
                    last = dve.tensor_scalar(ctok[:, t, :], bank[1][:, t * 256:(t + 1) * 256], bag[:, t, 0:1],
                                             bst[:, t, 1:2], ALU.subtract, ALU.mult)
                last.then_inc(s["conf_n"], 1)
                dve.wait_ge(s["num_ready"], l + 1)
                den = lambda t: bank[(2, 4)[t]][:, 0:260].rearrange("p (h n) -> p h n", h=HEADS)[:, :, DH]
                for t in range(TT):
                    chain.done(dve.scalar_tensor_tensor(out=mden[:, t, :], in0=den(t), scalar=-1.0,
                                                        in1=mcol[:, 8 + 4 * t:12 + 4 * t], op0=ALU.mult, op1=ALU.max))
                chain.wait()
                for t in range(TT):
                    chain.done(dve.tensor_tensor(mden[:, t, :], den(t), mden[:, t, :], ALU.max))
                chain.wait()
                chain.done(dve.reciprocal(mden[:, :, :], mden[:, :, :]))
                chain.wait()
                for t in range(TT):
                    nb = bank[(2, 4)[t]][:, 0:260].rearrange("p (h n) -> p h n", h=HEADS)
                    chain.done(dve.tensor_tensor(y[:, t, 0:256].rearrange("p (h n) -> p h n", h=HEADS), nb[:, :, 0:DH],
                                                 bc(mden[:, t, :].unsqueeze(2), [P, HEADS, DH]), ALU.mult))
                chain.wait()
                dve.tensor_tensor(y[:, :, 0:256], y[:, :, 0:256],
                                  osig[:, :, :], ALU.mult).then_inc(s["y_m"], 1)
                dve.wait_ge(s["sc_ready"], l + 1)
                chain.done(dve.tensor_reduce(smax[:, 0, :], bank[6][:, :].rearrange("p (h n) -> p h n", h=HEADS), AX_X, ALU.max))
                for i in range(2):
                    chain.done(dve.tensor_reduce(smax[:, 1, 2 * i:2 * i + 2],
                                                 bank[(0, 1)[i]][:, :].rearrange("p (h n) -> p h n", h=2), AX_X, ALU.max))
                chain.wait()
                dve.tensor_scalar(smax[:, :, :], smax[:, :, :], -(96.0 ** -0.5), None, ALU.mult).then_inc(s["smax_ready"], 1)
                dve.wait_ge(s["osq_ready"], l + 1)
                dve.tensor_reduce(gss[:, :, :], osq[:, :, :, :], AX_X, ALU.add).then_inc(s["gss_ready"], 1)
                dve.wait_ge(s["grd_ready"], l + 1)
                chain.done(dve.tensor_tensor(osq[:, :, :, :], bank[7][:, :].rearrange("p (t h n) -> p t h n", t=TT, h=HEADS),
                                             bc(grd[:, :, :].unsqueeze(3), [P, TT, HEADS, DH]), ALU.mult))
                chain.wait()
                dve.tensor_tensor(y[:, :, 512:768], osq[:, :, :, :].rearrange("p t h n -> p t (h n)"), grs[:, :, :],
                                  ALU.mult).then_inc(s["y_g"], 1)
                dve.wait_ge(s["conf_sig"], l + 1)
                dve.tensor_tensor(y[:, :, 768:1024], ctok[:, :, :], cacc[:, :, :], ALU.mult).then_inc(s["y_c"], 1)
                dve.wait_ge(s["pv_ready"], l + 1)
                chain.done(dve.reciprocal(psums[:, :, :], psums[:, :, :]))
                chain.wait()
                dve.tensor_tensor(y[:, :, 256:512].rearrange("p t (h n) -> p t h n", h=HEADS),
                                  bank[4][:, :].rearrange("p (t h n) -> p t h n", t=TT, h=HEADS),
                                  bc(psums[:, :, :].unsqueeze(3), [P, TT, HEADS, DH]), ALU.mult).then_inc(s["y_a"], 1)

                normalize(3 * l + 1, y, 4)
                for n in range(SPLIT):
                    split_low(n0 + N_IN + n)
                gains(3 * l + 1, FUSE + KD * l)
                split_low(n0 + N_IN + SPLIT)
                add_to_h((2, 3, 5, 6), s["piece_used"], [n0 + N_IN + N_OUT] * 4)
                if l == 0:
                    gains(3 * l + 2, NORM2 + KD * l)
                    ffn(DENSE0, None, 0, TT, scale=rstd)
                    add_to_h((2, 3, 5, 6), s["piece_used"], [DENSE0 + N_FFN] * 4)

            for g in (2, 3):
                dve.wait_ge(s["norm_tr"], 4 * 5 + g + 1)
                for i in range(2):
                    kd = 2 * g + i
                    last = dve.tensor_scalar(u32[:, kd, :], bank[NORM_BANKS[g]][:, i * S:(i + 1) * S], col(NORM2 + KD + kd),
                                             None, ALU.mult)
                last.then_inc(s["u32_dve"], 1)
            dve.wait_ge(s["moe_g_in"], 16)
            dve.wait_ge(s["rstd_ready"], 6)
            for t in range(TT):
                dve.scalar_tensor_tensor(out=un[:, t, :], in0=h[:, t, :], scalar=rstd[:, t, 0:1], in1=moe_g[:, :],
                                         op0=ALU.mult, op1=ALU.mult).then_inc(s["ung_ready"], 1)
            dve.wait_ge(s["logit_ready"], 1)
            for t in range(TT):
                chain.done(dve.tensor_scalar(logits[:, t, :], bank[2][:, t * E:(t + 1) * E], rstd[:, t, 0:1], None, ALU.mult))
            chain.wait()
            for t in range(TT):
                chain.done(dve.max(top8[:, t, :], logits[:, t, :]))
            chain.wait()
            for t in range(TT):
                chain.done(dve.max_index(idx8[:, t, :], top8[:, t, :], logits[:, t, :]))
            dve.tensor_tensor(gap[:, :], top8[:, :, 1], top8[:, :, 0], ALU.subtract).then_inc(s["gap_ready"], 1)
            chain.wait()
            chain.done(dve.tensor_copy(idf[:, :, :], idx8[:, :, :]))
            chain.wait()
            for t in range(TT):
                chain.done(dve.tensor_scalar(oh1[:, t, :], iota[:, 0:E], idf[:, t, 0:1], None, ALU.is_equal))
                chain.done(dve.tensor_scalar(oh2[:, t, :], iota[:, 0:E], idf[:, t, 1:2], None, ALU.is_equal))
            chain.wait()
            dve.tensor_tensor(routed[:, :, :], oh1[:, :, :], oh2[:, :, :], ALU.add).then_inc(s["routed_ready"], 1)
            for t in range(TT):
                dve.wait_ge(s["unh_ready"], t + 1)
                last = dve.tensor_tensor(unl[:, t, :], un[:, t, :], unh[:, t, :].bitcast(F32), ALU.subtract)
            last.then_inc(s["unl_ready"], 1)
            dve.wait_ge(s["rank_ready"], 1)
            for t in range(TT):
                chain.done(dve.scalar_tensor_tensor(out=rank1[:, t, :], in0=bank[3][:, t * E:(t + 1) * E], scalar=1.0,
                                                    in1=routed[:, t, :], op0=ALU.add, op1=ALU.mult))
            chain.wait()
            chain.done(dve.tensor_scalar(keys[:, :, 0:E], rank1[:, :, :], -1.0, None, ALU.add))
            chain.wait()

            def route_weights():
                dve.tensor_scalar(over[:, :], bank[3][:, TT * E:(TT + 1) * E], float(P), None, ALU.is_gt).then_inc(s["over_ready"], 1)
                dve.wait_ge(s["over_ready"], 1)
                dve.wait_ge(s["egap_ready"], 1)
                chain.done(dve.tensor_scalar(w1[:, :], egap[:, :], 1.0, None, ALU.add))
                chain.wait()
                chain.done(dve.reciprocal(w1[:, :], w1[:, :]))
                chain.wait()
                chain.done(dve.tensor_tensor(w2[:, :], w1[:, :], egap[:, :], ALU.mult))
                chain.wait()
                for t in range(TT):
                    chain.done(dve.tensor_scalar(wts[:, t, 0:E], oh2[:, t, :], w2[:, t:t + 1], None, ALU.mult))
                chain.wait()
                for t in range(TT):
                    chain.done(dve.scalar_tensor_tensor(out=wts[:, t, 0:E], in0=oh1[:, t, :], scalar=w1[:, t:t + 1],
                                                        in1=wts[:, t, 0:E], op0=ALU.mult, op1=ALU.add))
                chain.wait()

            def route_overflow():
                chain.done(dve.tensor_tensor_scan(over_n[:, :], ones[:, 0:E], over[:, :], 0.0, ALU.mult, ALU.add))
                chain.done(dve.tensor_reduce(jobs_f[:, 3:4], over[:, :], AX_X, ALU.add))
                chain.wait()
                for o in range(OVER):
                    chain.done(dve.scalar_tensor_tensor(out=over_oh[:, o, :], in0=over_n[:, :], scalar=float(o + 1),
                                                        in1=over[:, :], op0=ALU.is_equal, op1=ALU.mult))
                chain.wait()
                for o in range(OVER):
                    oh = bc(over_oh[:, o:o + 1, :], [P, TT, E])
                    chain.done(dve.tensor_tensor(pick[:, :, :], rank1[:, :, :], oh, ALU.mult))
                    chain.wait()
                    chain.done(dve.tensor_reduce(keys[:, :, E + o], pick[:, :, :], AX_X, ALU.add))
                    chain.wait()
                    chain.done(dve.tensor_tensor(pick[:, :, :], wts[:, :, 0:E], oh, ALU.mult))
                    chain.wait()
                    chain.done(dve.tensor_reduce(wts[:, :, E + o], pick[:, :, :], AX_X, ALU.add))
                    chain.wait()
                    chain.done(dve.tensor_tensor(pick[:, 0, :], over_oh[:, o, :], iota[:, 0:E], ALU.mult))
                    chain.wait()
                    chain.done(dve.tensor_reduce(jobs_f[:, o:o + 1], pick[:, 0, :], AX_X, ALU.add))
                    chain.wait()
                dve.memset(keys[:, :, JOBS:JOBS + 1], -1.0)
                chain.done(dve.tensor_scalar(keys[:, :, E:JOBS], keys[:, :, E:JOBS], -float(P + 1), None, ALU.add))
                chain.wait()
                dve.tensor_copy(jobs_i[:, :], jobs_f[:, :]).then_inc(s["jobs_ready"], 1)

            def column(n):
                return slice(n, n + 1) if isinstance(n, int) else bass.ds(n, 1)

            def select(n):
                dve.tensor_copy(keycol[:, :], keys[:, :, column(n)].rearrange("p t a -> p (t a)")).then_inc(s["key_copied"], 1)
                dve.wait_ge(s["key_copied"], n + 1)
                for t in range(TT):
                    last = dve.tensor_scalar(sel[:, t, :], iota[:, :], keycol[:, t:t + 1], None, ALU.is_equal)
                last.then_inc(s["sel_ready"], 1)

            def tokens_out(n):
                dve.wait_ge(s["gath_ready"], n + 1)
                dve.tensor_copy(xs[:, 4:8, :], bank[6][:, :].rearrange("p (k n) -> p k n", k=4)).then_inc(s["xs_dve"], 1)

            def tokens_low(n):
                dve.wait_ge(s["xh_ready"], n + 1)
                for i in range(2):
                    last = dve.tensor_tensor(xl[:, 4 * i:4 * i + 4, :], bank[5 + i][:, :].rearrange("p (k n) -> p k n", k=4),
                                             xh[:, 4 * i:4 * i + 4, :].bitcast(F32), ALU.subtract)
                last.then_inc(s["xl_ready"], 1)

            def result_low(n):
                dve.wait_ge(s["yh_ready"], n)
                for i in range(2):
                    last = dve.scalar_tensor_tensor(out=yl[:, i * 512:(i + 1) * 512], in0=bank[2 + i][:, :], scalar=wslot[:, :],
                                                    in1=yh[:, i * 512:(i + 1) * 512].bitcast(F32), op0=ALU.mult, op1=ALU.subtract)
                last.then_inc(s["yl_ready"], 1)

            def add_result(n, t):
                for half in range(2):
                    i = 2 * t + half
                    dve.wait_ge(s["scat_ready"], 4 * n - (3 - i))
                    dst = h[:, t, half * 512:(half + 1) * 512]
                    last = dve.tensor_tensor(dst, bank[SCATTER_BANKS[i]][:, :], dst, ALU.add).then_inc(s["added"], 1)

            def job(j, first):
                def weights():
                    if not first:
                        dve.wait_ge(s["selT_tr"], j)
                    dve.tensor_copy(wcol[:, :], wts[:, :, column(j)].rearrange("p t a -> p (t a)")).then_inc(s["wcol_ready"], 1)

                def next_select():
                    dve.wait_ge(s["selT_tr"], j + 1)
                    select(j + 1)

                def chunk0():
                    weights()
                    if not first:
                        add_result(j, 0)

                def chunk1():
                    if first:
                        route_overflow()
                    else:
                        add_result(j, 1)

                ffn(MOE0, j, j + 1, 1, {} if first else {2: lambda: result_low(j)},
                    {0: chunk0, 1: chunk1, SELECT_AT: next_select, GATHER_AT: lambda: tokens_out(j + 1),
                     CHUNKS - 1: lambda: tokens_low(j + 1)})

            select(0)
            route_weights()
            tokens_out(0)
            tokens_low(0)
            n_jobs = jobs(dve, job)
            result_low(n_jobs)
            for t in range(TT):
                add_result(n_jobs, t)
            dve.memset(tiny[:, :], 0.0).then_inc(s["h_ready"], 2)
            dve.wait_ge(s["rstd_ready"], 7)
            dve.wait_ge(s["final_in"], 16)
            for t in range(TT):
                last = dve.scalar_tensor_tensor(out=h[:, t, :], in0=h[:, t, :], scalar=rstd[:, t, 0:1], in1=fin_g,
                                                op0=ALU.mult, op1=ALU.mult)
            last.then_inc(s["out_ready"], 1)

        @block.tensor
        def _(pe):
            owner = {}

            def claim(b, sem, value):
                if b in owner:
                    pe.wait_ge(*owner[b])
                owner[b] = (s[sem], value)

            def norm_transposes(k, source, ready, readers):
                sem, values = ready
                for g in range(4):
                    claim(NORM_BANKS[g], *readers[g])
                for t in range(TT):
                    pe.wait_ge(s[sem], values[t])
                    for g in range(4):
                        for i in range(2):
                            last = pe.transpose(bank[NORM_BANKS[g]][:, i * S + t * P:i * S + (t + 1) * P],
                                                source[:, t, (2 * g + i) * P:(2 * g + i + 1) * P], ident[:, :])
                        if t == TT - 1:
                            last.then_inc(s["norm_tr"], 1)

            def split_readers(n):
                return [("utl_ready", 4 * n + g + 1) for g in range(4)]

            def product(dst, terms):
                for i, ((ah, al), (bh, bl)) in enumerate(terms):
                    first, final = i == 0, i == len(terms) - 1
                    pe.matmul(dst, ah, bh, start=first, stop=False)
                    pe.matmul(dst, ah, bl, start=False, stop=False)
                    last = pe.matmul(dst, al, bh, start=False, stop=final)
                return last

            def part(n, lo, hi):
                return high[:, n % SPLIT, lo:hi], low[:, n % SPLIT, lo:hi]

            def uT(k, lo, hi):
                return uTh[:, k, lo:hi], uTl[:, k, lo:hi]

            def ffn(n0, job, job_n, tiles, xT, accs, first_claims, after_products={}):
                pieces = N_FFN * job if job is not None else 0
                at = lambda c: job_n * CHUNKS + c

                def down(c):
                    n = n0 + FFN_AT[("d", c)]
                    pe.wait_ge(s["hTl_ready"], at(c + 1))
                    pe.wait_ge(s["low_ready"], pieces + (n + 1))
                    for f in range(2):
                        for t in range(tiles):
                            for half in range(2):
                                o = bank[accs[t][half]][:, :]
                                ah, al = hTh[:, f, t, :], hTl[:, f, t, :]
                                bh, bl = part(n, f * 1024 + half * 512, f * 1024 + half * 512 + 512)
                                pe.matmul(o, ah, bh, start=(c == 0 and f == 0), stop=False)
                                pe.matmul(o, ah, bl, start=False, stop=False)
                                last = pe.matmul(o, al, bh, start=False, stop=(c == CHUNKS - 1 and f == 1))
                    last.then_inc(s["piece_used"], 1)
                    return last

                for c in range(CHUNKS):
                    if c:
                        pe.wait_ge(s["hid_ready"], at(c))
                    else:
                        first_claims()
                    for kh, kind in enumerate("ab"):
                        n = n0 + FFN_AT[(kind, c)]
                        pe.wait_ge(s["low_ready"], pieces + (n + 1))
                        for t in range(tiles):
                            for k in range(4):
                                kd = 4 * kh + k
                                ah, al = xT(kd, t)
                                bh, bl = part(n, k * 512, (k + 1) * 512)
                                o = bank[t][:, :]
                                pe.matmul(o, ah, bh, start=(kd == 0), stop=False)
                                pe.matmul(o, ah, bl, start=False, stop=False)
                                last = pe.matmul(o, al, bh, start=False, stop=(kd == KD - 1))
                        last.then_inc(s["piece_used"], 1)
                    if c:
                        down(c - 1)
                        pe.wait_ge(s["hTl_ready"], at(c))
                    after_products.get(c, lambda: None)()
                    pe.wait_ge(s["hid_ready"], at(c + 1))
                    for f in range(2):
                        for t in range(tiles):
                            o = (f * tiles + t) * P
                            last = pe.transpose(bank[4][:, o:o + P], hid[:, t, f * P:(f + 1) * P], ident[:, :])
                    last.then_inc(s["hid_tr"], 1)
                down(CHUNKS - 1)

            pe.wait_ge(s["consts"], 1)
            pe.wait_ge(s["rows_in"], 16 * 11)
            claim(7, "cols_ready", 1)
            pe.transpose(bank[7][:, 0:P], stage[:, 0, :], ident[:, :])
            pe.transpose(bank[7][:, P:2 * P], stage[:, 1, :], ident[:, :]).then_inc(s["cols_tr"], 1)

            for l in range(DEPTH):
                n0 = LAYER_PIECES[l]
                norm_transposes(3 * l, un, ("un_ready", [2 * l + 1] * TT), split_readers(3 * l))
                pe.wait_ge(s["utl_ready"], 4 * (3 * l + 1))
                act_reads = {1: 1, 4: 2, 5: 3, 6: 5, 7: 6, 8: 7, 9: 8}
                dve_reads = {0: 1, 2: 2, 3: 3, 10: 4}
                for p in range(N_IN):
                    n = n0 + p
                    w = sum(v for _, v in W_IN_PIECES[p])
                    pe.wait_ge(s["low_ready"], n + 1)
                    b = Z_BANKS[p % 4]
                    claim(b, *(("z_act", 9 * l + act_reads[p]) if p in act_reads else ("z_dve", 4 * l + dve_reads[p])))
                    if p in FEATURE_MAJOR:
                        for c in range(2):
                            last = product(bank[b][:, c * S:(c + 1) * S],
                                           [(part(n, k * w + c * P, k * w + (c + 1) * P), uT(k, 0, S)) for k in range(KD)])
                    else:
                        for t in range(TT):
                            last = product(bank[b][:, t * w:(t + 1) * w],
                                           [(uT(k, t * P, (t + 1) * P), part(n, k * w, (k + 1) * w)) for k in range(KD)])
                    last.then_inc(s["piece_used"], 1)
                    if p == 6:
                        pe.wait_ge(s["z_act"], 9 * l + 3)
                        claim(7, "z_act", 9 * l + 4)
                        for t in range(TT):
                            last = pe.transpose(bank[7][0:16, t * P:(t + 1) * P], zkv[:, t, 160:176], ident[:, :])
                        last.then_inc(s["aT_tr"], 1)

                pe.wait_ge(s["ukv_in"], 64 * (l + 1))
                claim(0, "gla_abs", l + 1)
                pe.wait_ge(s["z_act"], 9 * l + 4)
                pe.matmul(bank[0][:, 0:S], walpha[:, :], aT[:, :], start=True, stop=True).then_inc(s["gpre_ready"], 1)
                pe.wait_ge(s["lat_ready"], l + 1)
                claim(4, "lat_T", l + 1)
                claim(7, "lat_T", l + 1)
                for t in range(TT):
                    pe.transpose(bank[4][:, t * P:(t + 1) * P], zif[:, t, 8:136], ident[:, :])
                    pe.transpose(bank[4][0:64, S + t * P:S + (t + 1) * P], zif[:, t, 136:200], ident[:, :])
                    last = pe.transpose(bank[7][:, t * P:(t + 1) * P], zkv[:, t, 0:P], ident[:, :])
                last.then_inc(s["lat_tr"], 1)
                pe.wait_ge(s["lf_ready"], l + 1)
                claim(2, "mcum_ready", l + 1)
                for t in range(TT):
                    pe.transpose(bank[2][0:4, t * P:(t + 1) * P], gb[:, t, 0:4], ident[:, :])
                    last = pe.transpose(bank[2][0:4, S + t * P:S + (t + 1) * P], gb[:, t, 4:8], ident[:, :])
                last.then_inc(s["gate_tr"], 1)
                pe.wait_ge(s["lat_T"], l + 1)
                for t in range(TT):
                    b = (3, 5)[t]
                    claim(b, "qkv_evac", l + 1)
                    pe.matmul(bank[b][:, 0:384], cqT[:, 0, t * P:(t + 1) * P], uq[:, 0, :], start=True, stop=False)
                    last = pe.matmul(bank[b][:, 0:384], cqT[0:64, 1, t * P:(t + 1) * P], uq[0:64, 1, :], start=False, stop=True)
                last.then_inc(s["q_ready"], 1)
                for t in range(TT):
                    b = (6, 1)[t]
                    claim(b, "qkv_evac", l + 1)
                    last = pe.matmul(bank[b][:, :], ckvT[:, t * P:(t + 1) * P], ukv[:, :], start=True, stop=True)
                last.then_inc(s["kv_ready"], 1)
                pe.wait_ge(s["expnm_ready"], l + 1)
                claim(0, "mcol_ready", l + 1)
                for t in range(TT):
                    pe.transpose(bank[0][:, 4 * t:4 * t + 4], aj[:, t * P:(t + 1) * P], ident[0:4, 0:4])
                    last = pe.transpose(bank[0][:, 8 + 4 * t:12 + 4 * t], expnm[:, t * P:(t + 1) * P], ident[0:4, 0:4])
                last.then_inc(s["mcol_tr"], 1)
                pe.wait_ge(s["qk_ready"], l + 1)
                for hd in range(HEADS):
                    b = (2, 4, 7, 0)[hd]
                    claim(b, "dt_ready", HEADS * l + hd + 1)
                    row = bc(ident[0:4, hd:hd + 1], [4, P])
                    pe.matmul(bank[b][:, 0:S], row, negm[:, :], start=True, stop=False)
                    pe.matmul(bank[b][:, 0:P], ident[:, :], mask_kt[:, :], start=False, stop=True)
                    pe.matmul(bank[b][:, S:S + P], row, negm[:, P:S], start=True, stop=False)
                    pe.matmul(bank[b][:, S:S + P], ident[:, :], mask_kt[:, :], start=False, stop=True).then_inc(s["x_ready"], 1)
                    b = (1, 3, 5, 6)[hd]
                    claim(b, "pt_ready", HEADS * l + hd + 1)
                    r = slice(64 * (hd % 2), 64 * (hd % 2) + 64)
                    q, k = qkc[r, hd // 2, :], qkc[r, 2 + hd // 2, :]
                    pe.matmul(bank[b][:, 0:S], k[:, 0:P], q, start=True, stop=True)
                    pe.matmul(bank[b][:, S:S + P], k[:, P:S], q[:, P:S], start=True, stop=True).then_inc(s["s_ready"], 1)
                pe.wait_ge(s["rot_ready"], l + 1)
                for i, (b, src, sem, v) in enumerate(((2, qtok, "qT_ready", 1), (4, qtok, "qT_ready", 2),
                                                      (7, ktok, "kT_ready", 1), (0, ktok, "kT_ready", 2))):
                    claim(b, sem, 2 * l + v)
                    for a in range(2):
                        for t in range(TT):
                            last = pe.transpose(bank[b][0:96, a * S + t * P:a * S + (t + 1) * P],
                                                src[:, t, 2 * (i % 2) + a, :], ident[:, :])
                    last.then_inc(s["qkT_tr"], 1)
                pe.wait_ge(s["conv_done"], l + 1)
                claim(1, "conf_n", l + 1)
                for t in range(TT):
                    for c in range(2):
                        last = pe.transpose(bank[1][:, t * 256 + c * P:t * 256 + (c + 1) * P],
                                            cacc[:, c, t * P:(t + 1) * P], ident[:, :])
                last.then_inc(s["conf_tr"], 1)
                pe.wait_ge(s["gla_qk"], l + 1)
                for hd in range(HEADS):
                    b = (3, 5, 6, 7)[hd]
                    claim(b, "gs_ready", HEADS * l + hd + 1)
                    r = slice(32 * hd, 32 * hd + 32)
                    for i, (k, q) in enumerate(((2, 0), (3, 1), (4, 1))):
                        last = pe.matmul(bank[b][:, i * P:(i + 1) * P], gE[r, k, :], gE[r, q, :], start=True, stop=True,
                                         tile_position=(32 * hd, 0))
                    last.then_inc(s["ga_ready"], 1)
                for hd in range(HEADS):
                    pe.wait_ge(s["pt_ready"], HEADS * l + hd + 1)
                    for t in range(TT):
                        b = (2, 4)[t]
                        if hd == 0:
                            claim(b, "y_m", l + 1)
                        o = bank[b][:, hd * 65:(hd + 1) * 65]
                        if t == 0:
                            last = pe.matmul(o, dec[:, hd, 0:P], vaug[:, 0, hd, :], start=True, stop=True)
                        else:
                            pe.matmul(o, dec[:, hd, P:S], vaug[:, 0, hd, :], start=True, stop=False)
                            last = pe.matmul(o, dec[:, hd, S:S + P], vaug[:, 1, hd, :], start=False, stop=True)
                last.then_inc(s["num_ready"], 1)
                pe.wait_ge(s["qT_ready"], 2 * (l + 1))
                pe.wait_ge(s["kT_ready"], 2 * (l + 1))
                for hd in range(HEADS):
                    if hd == 0:
                        claim(6, "p_ready", l + 1)
                    o = bank[6][:, hd * P:(hd + 1) * P]
                    pe.matmul(o, qT[:, hd, 0:P], kT[:, hd, 0:P], start=True, stop=False)
                    pe.matmul(o, ident[:, :], mask_qt[:, :], start=False, stop=True)
                for hd in range(HEADS):
                    b = (0, 1)[hd // 2]
                    if hd % 2 == 0:
                        claim(b, "p_ready", l + 1)
                    o = bank[b][:, (hd % 2) * S:(hd % 2 + 1) * S]
                    pe.matmul(o, qT[:, hd, P:S], kT[:, hd, :], start=True, stop=False)
                    last = pe.matmul(o[:, P:S], ident[:, :], mask_qt[:, :], start=False, stop=True)
                last.then_inc(s["sc_ready"], 1)
                for hd in range(HEADS):
                    pe.wait_ge(s["gs_ready"], HEADS * l + hd + 1)
                    if hd == HEADS - 1:
                        break
                claim(7, "y_g", l + 1)
                for t in range(TT):
                    for hd in range(HEADS):
                        o = bank[7][:, t * 256 + hd * DH:t * 256 + (hd + 1) * DH]
                        v = gv[:, :, hd * DH:(hd + 1) * DH]
                        if t == 0:
                            last = pe.matmul(o, gS[:, hd, 0, :], v[:, 0, :], start=True, stop=True)
                        else:
                            pe.matmul(o, gS[:, hd, 1, :], v[:, 0, :], start=True, stop=False)
                            last = pe.matmul(o, gS[:, hd, 2, :], v[:, 1, :], start=False, stop=True)
                last.then_inc(s["go_ready"], 1)
                pe.wait_ge(s["p_ready"], l + 1)
                for i, b in enumerate((3, 5, 6)):
                    claim(b, "pT_ready", 3 * l + i + 1)
                    for hd in range(HEADS):
                        src = probs[:, hd * P:(hd + 1) * P] if i == 0 else \
                            probs[:, 512 + hd * S + (i - 1) * P:512 + hd * S + i * P]
                        last = pe.transpose(bank[b][:, hd * P:(hd + 1) * P], src, ident[:, :])
                    last.then_inc(s["p_tr"], 1)
                pe.wait_ge(s["pT_ready"], 3 * (l + 1))
                claim(4, "y_a", l + 1)
                for t in range(TT):
                    for hd in range(HEADS):
                        o = bank[4][:, t * 256 + hd * DH:t * 256 + (hd + 1) * DH]
                        v = vm[:, :, hd * DH:(hd + 1) * DH]
                        if t == 0:
                            last = pe.matmul(o, probT[:, 0, hd, :], v[:, 0, :], start=True, stop=True)
                        else:
                            pe.matmul(o, probT[:, 1, hd, :], v[:, 0, :], start=True, stop=False)
                            last = pe.matmul(o, probT[:, 2, hd, :], v[:, 1, :], start=False, stop=True)
                last.then_inc(s["pv_ready"], 1)

                norm_transposes(3 * l + 1, un, ("un_ready", [2 * l + 2] * TT), split_readers(3 * l + 1))
                for i, b in enumerate((2, 3, 5, 6)):
                    claim(b, "h_ready", 4 * l + 1 + i // 2)
                for p in range(N_OUT):
                    n = n0 + N_IN + p
                    pe.wait_ge(s["utl_ready"], 4 * (3 * l + 1) + p + 1)
                    pe.wait_ge(s["low_ready"], n + 1)
                    for i, b in enumerate((2, 3, 5, 6)):
                        t, half = divmod(i, 2)
                        for k in range(2):
                            (ah, al), (bh, bl) = uT(2 * p + k, t * P, (t + 1) * P), part(n, k * D + half * 512, k * D + (half + 1) * 512)
                            pe.matmul(bank[b][:, :], ah, bh, start=(p == 0 and k == 0), stop=False)
                            pe.matmul(bank[b][:, :], ah, bl, start=False, stop=False)
                            last = pe.matmul(bank[b][:, :], al, bh, start=False, stop=(p == N_OUT - 1 and k == 1))
                    last.then_inc(s["piece_used"], 1)
                norm_transposes(3 * l + 2, h, ("h_ready", [4 * l + 1, 4 * l + 2]),
                                [("u32_act", 1), ("u32_act", 2), ("u32_dve", 1), ("u32_dve", 2)] if l else split_readers(3 * l + 2))
                if l == 0:
                    pe.wait_ge(s["utl_ready"], 4 * (3 * l + 3))
                    def dense_claims():
                        for b, v in ((0, ("hid_ready", CHUNKS)), (1, ("hid_ready", CHUNKS)), (4, ("hTl_ready", CHUNKS)),
                                     (2, ("h_ready", 3)), (3, ("h_ready", 3)), (5, ("h_ready", 4)), (6, ("h_ready", 4))):
                            claim(b, *v)
                    ffn(DENSE0, None, 0, TT, lambda kd, t: uT(kd, t * P, (t + 1) * P), ((2, 3), (5, 6)), dense_claims)

            pe.wait_ge(s["router_in"], 16)
            pe.wait_ge(s["u32_act"], 2)
            pe.wait_ge(s["u32_dve"], 2)
            claim(2, "routed_ready", 1)
            for t in range(TT):
                for k in range(KD):
                    last = pe.matmul(bank[2][:, t * E:(t + 1) * E], u32[:, k, t * P:(t + 1) * P], router[:, k, :],
                                     start=(k == 0), stop=(k == KD - 1))
            last.then_inc(s["logit_ready"], 1)
            pe.wait_ge(s["routed_ready"], 1)
            claim(3, "over_ready", 1)
            pe.matmul(bank[3][:, 0:E], before[:, :], routed[:, 0, :], start=True, stop=True)
            pe.matmul(bank[3][:, E:2 * E], ones[:, 0:P], routed[:, 0, :], start=True, stop=False)
            pe.matmul(bank[3][:, E:2 * E], before[:, :], routed[:, 1, :], start=False, stop=True)
            pe.matmul(bank[3][:, 2 * E:3 * E], ones[:, 0:P], routed[:, 0, :], start=True, stop=False)
            pe.matmul(bank[3][:, 2 * E:3 * E], ones[:, 0:P], routed[:, 1, :], start=False, stop=True).then_inc(s["rank_ready"], 1)
            pe.wait_ge(s["unl_ready"], 1)
            pe.wait_ge(*owner[5])
            pe.wait_ge(*owner[6])

            def gather(n):
                pe.wait_ge(s["sel_ready"], n + 1)
                for half in range(2):
                    for t in range(TT):
                        for i, a in enumerate((unh, unl)):
                            last = pe.matmul(bank[5 + half][:, :], sel[:, t, :], a[:, t, half * 512:(half + 1) * 512],
                                             start=(t == 0 and i == 0), stop=(t == TT - 1 and i == 1))
                last.then_inc(s["gath_ready"], 1)

            def gathered_transposes(n):
                pe.wait_ge(s["xs_act"], n + 1)
                pe.wait_ge(s["xs_dve"], n + 1)
                for kd in range(KD):
                    last = pe.transpose(bank[5 + kd // 4][:, (kd % 4) * P:(kd % 4 + 1) * P], xs[:, kd, :], ident[:, :])
                last.then_inc(s["xT_tr"], 1)

            def scatter(n):
                pe.wait_ge(s["selT_ready"], n)
                pe.wait_ge(s["yl_ready"], n)
                for i, b in enumerate(SCATTER_BANKS):
                    t, half = divmod(i, 2)
                    pe.matmul(bank[b][:, :], selT[:, t, :], yh[:, half * 512:(half + 1) * 512], start=True, stop=False)
                    pe.matmul(bank[b][:, :], selT[:, t, :], yl[:, half * 512:(half + 1) * 512], start=False, stop=True).then_inc(s["scat_ready"], 1)

            def job(j, first):
                def slots():
                    if not first:
                        pe.wait_ge(s["added"], 4 * j)
                    pe.wait_ge(s["wcol_ready"], j + 1)
                    for t in range(TT):
                        pe.transpose(bank[7][:, t * P:(t + 1) * P], sel[:, t, :].bitcast(F32), ident[:, :])
                    for t in range(TT):
                        last = pe.matmul(bank[7][:, 2 * P:2 * P + 1], sel[:, t, :].bitcast(F32), wcol[:, t:t + 1],
                                         start=(t == 0), stop=(t == TT - 1))
                    last.then_inc(s["selT_tr"], 1)

                pe.wait_ge(s["xl_ready"], j + 1)
                work = {SLOTS_AT: slots, GATHER_AT: lambda: gather(j + 1),
                        GATHER_AT + 2: lambda: gathered_transposes(j + 1)}
                if not first:
                    work[0] = lambda: scatter(j)
                ffn(MOE0, j, j + 1, 1, lambda kd, t: (xh[:, kd, :], xl[:, kd, :]), ((2, 3),), lambda: None, work)

            gather(0)
            gathered_transposes(0)
            for b in (0, 1, 2, 3, 4, 7):
                pe.wait_ge(*owner[b])
            n_jobs = jobs(pe, job)
            scatter(n_jobs)


_INS = ['x', 'positions', 'norm1_g', 'w_in', 'mlstm_conv_w', 'mlstm_conv_b', 'mlstm_gate_b', 'mla_q_norm_g',
        'mla_w_uq', 'mla_kv_norm_g', 'mla_w_ukv', 'gla_w_alpha', 'gla_b_alpha', 'conv_w', 'conv_b', 'conv_ln_g',
        'conv_ln_b', 'fuse_g', 'w_out', 'norm2_g', 'ffn_w_gate', 'ffn_w_up', 'ffn_w_down', 'moe_router',
        'moe_w_gate', 'moe_w_up', 'moe_w_down', 'final_norm_g']


def kernel(**inputs):
    import numpy as _np
    import concourse.bacc as _bacc
    from concourse import mybir as _mybir
    from concourse.bass_utils import run_bass_kernel_spmd as _run

    nc = _bacc.Bacc("TRN2", target_bir_lowering=False, num_devices=1)
    arrays, args = {}, []
    for name in _INS:
        a = _np.ascontiguousarray(inputs[name])
        arrays[f"in_{name}_dram"] = a
        args.append(nc.dram_tensor(f"in_{name}_dram", a.shape, _mybir.dt.from_np(a.dtype), kind="ExternalInput").ap())
    out = nc.dram_tensor("out_0_dram", inputs["x"].shape, _mybir.dt.from_np(_np.dtype("float32")), kind="ExternalOutput").ap()
    build(nc, *args, out)
    r = _run(nc, [arrays], core_ids=[0])
    return r.results[0]["out_0_dram"]
```

```python
import math
from contextlib import ExitStack

import numpy as np
import concourse.bass as bass
from concourse import mybir

F32 = mybir.dt.float32
F32R = mybir.dt.float32r
I32 = mybir.dt.int32
U32 = mybir.dt.uint32
ALU = mybir.AluOpType
ACT = mybir.ActivationFunctionType
AX_X = mybir.AxisListType.X
LN_EXP = "natural_log_exp_and_others"

P = 128
EPS = 1e-6
NEG = -1e30

PIECE = 2048
RING = 11
SPLIT = 3

W_IN_PIECES = [
    [(2168, 256)],
    [(2424, 256)],
    [(0, 256)],
    [(256, 256)],
    [(1024, 200)],
    [(1224, 160), (2152, 16)],
    [(1384, 256)],
    [(512, 256)],
    [(768, 256)],
    [(1896, 256)],
    [(1640, 256)],
]
N_IN = len(W_IN_PIECES)
FEATURE_MAJOR = (0, 1, 2, 3, 6)
N_OUT = 4
CHUNKS = 11
N_FFN = 3 * CHUNKS


def ffn_pieces():
    order = []
    for c in range(CHUNKS):
        order += [("a", c), ("b", c)]
        if c:
            order.append(("d", c - 1))
    return order + [("d", CHUNKS - 1)]


FFN_ORDER = ffn_pieces()
FFN_AT = {key: n for n, key in enumerate(FFN_ORDER)}


class Chain:

    def __init__(self, eng, sem):
        self.eng, self.sem, self.n = eng, sem, 0

    def done(self, ins):
        self.n += 1
        ins.then_inc(self.sem, 1)

    def wait(self, lag=0):
        if self.n > lag:
            self.eng.wait_ge(self.sem, self.n - lag)


def build(nc, x, positions, norm1_g, w_in, mlstm_conv_w, mlstm_conv_b, mlstm_gate_b,
          mla_q_norm_g, mla_w_uq, mla_kv_norm_g, mla_w_ukv, gla_w_alpha, gla_b_alpha,
          conv_w, conv_b, conv_ln_g, conv_ln_b, fuse_g, w_out, norm2_g,
          ffn_w_gate, ffn_w_up, ffn_w_down, moe_router, moe_w_gate, moe_w_up, moe_w_down,
          final_norm_g, out):
    DEPTH, D, _ = w_in.shape
    S = x.shape[1]
    TT = S // P
    KD = D // P
    HEADS = 4
    DH = 64
    CONV, MCONV = conv_w.shape[1], mlstm_conv_w.shape[1]
    E = moe_w_gate.shape[1]
    OVER = 3
    JOBS = E + OVER
    F_CH = moe_w_gate.shape[3] // CHUNKS
    assert (TT, KD, F_CH, E) == (2, 8, 256, 8)
    LAYER_PIECES = [0, N_IN + N_OUT + N_FFN]
    MOE0 = LAYER_PIECES[1] + N_IN + N_OUT
    DENSE0 = N_IN + N_OUT
    assert N_FFN % RING == 0 and N_FFN % SPLIT == 0

    ctx = ExitStack()

    def sb(name, shape, dt=F32, where=ctx):
        return where.enter_context(nc.sbuf_tensor(name, shape, dt))

    with ctx:
        ring = sb("ring", [P, RING, PIECE])
        h = sb("h", [P, TT, D])
        ident = sb("ident", [P, P])
        ones = sb("ones", [P, S])
        iota = sb("iota", [P, P])
        mask_kt = sb("mask_kt", [P, P])
        mask_qt = sb("mask_qt", [P, P])
        gla_mask = sb("gla_mask", [P, 3, P])
        before = sb("before", [P, P])
        cols = sb("cols", [P, 3, P])
        gate_b = sb("gate_b", [P, DEPTH, 8])
        ln_gb = sb("ln_gb", [P, 2, 256])
        router = sb("router", [P, KD, E])
        invf = sb("invf", [P, 16])
        pos_i = sb("pos_i", [P, TT], I32)
        pos_f = sb("pos_f", [P, TT])
        ang = sb("ang", [P, 2, TT, 16])
        turn = sb("turn", [P, 2, TT, 16])
        cossin = sb("cossin", [P, 2, TT, 16])
        epst = sb("epst", [P, 1])
        ss = sb("ss", [P, TT, 4])
        lnv = sb("lnv", [P, TT, 4])
        rstd = sb("rstd", [P, TT, 4])
        tiny = sb("tiny", [P, 1])
        gb = sb("gb", [P, TT, 8])
        gmn = sb("gmn", [P, TT, 4])
        gab = sb("gab", [P, TT, 4])
        gln = sb("gln", [P, TT, 4])
        lss = sb("lss", [P, 2, TT])
        lln = sb("lln", [P, 2, TT])
        lrs = sb("lrs", [P, 2, TT])
        logits = sb("logits", [P, TT, E])
        top8 = sb("top8", [P, TT, 8])
        idx8 = sb("idx8", [P, TT, 8], U32)
        idf = sb("idf", [P, TT, 8])
        gap = sb("gap", [P, TT])
        egap = sb("egap", [P, TT])
        w1 = sb("w1", [P, TT])
        w2 = sb("w2", [P, TT])
        oh1 = sb("oh1", [P, TT, E])
        oh2 = sb("oh2", [P, TT, E])
        routed = sb("routed", [P, TT, E])
        rank1 = sb("rank1", [P, TT, E])
        keys = sb("keys", [P, TT, JOBS + 1])
        wts = sb("wts", [P, TT, JOBS])
        over = sb("over", [P, E])
        over_n = sb("over_n", [P, E])
        over_oh = sb("over_oh", [P, OVER, E])
        pick = sb("pick", [P, TT, E])
        jobs_f = sb("jobs_f", [P, 4])
        jobs_i = sb("jobs_i", [P, 4], I32)
        keycol = sb("keycol", [P, TT])
        wcol = sb("wcol", [P, TT])
        wslot = sb("wslot", [P, 1])

        with ExitStack() as part:
            un = sb("un", [P, TT, D], F32, part)
            probs = un[:, :, :].rearrange("p t d -> p (t d)")
        with ExitStack() as part:
            uq = sb("uq", [P, 2, 384], F32, part)
            ukv = sb("ukv", [P, 512], F32, part)
            walpha = sb("walpha", [16, P], F32, part)
            gx = sb("gx", [P, S], F32, part)
            gmn2 = sb("gmn2", [P, S], F32, part)
            b16 = gx
        with ExitStack() as part:
            yh = sb("yh", [P, D], F32R, part)
            yl = sb("yl", [P, D], F32R, part)
        keep_un = ctx.enter_context(nc.sbuf_tensor("keep_un", [P, TT, D], F32))

        with ExitStack() as part:
            glu = sb("glu", [P, 2, CONV - 1 + S], F32, part)
            gsig = sb("gsig", [P, 2, S], F32, part)
            qkpre = sb("qkpre", [P, 4, MCONV - 1 + S], F32, part)
            cacc = sb("cacc", [P, 2, S], F32, part)
            qkc = sb("qkc", [P, 4, S], F32, part)
            vaug = sb("vaug", [P, TT, HEADS, DH + 1], F32, part)
            osig = sb("osig", [P, TT, 256], F32, part)
            zif = sb("zif", [P, TT, 200], F32, part)
            zkv = sb("zkv", [P, TT, 176], F32, part)
            gab2 = sb("gab2", [P, S], F32, part)
            aT = gab2[0:16, :]
            gqk = sb("gqk", [P, 2, S], F32, part)
            gv = sb("gv", [P, TT, 256], F32, part)
            grs = sb("grs", [P, TT, 256], F32, part)
            size_b = 4 * (2 * (CONV - 1 + S) + 4 * S + 4 * (MCONV - 1 + S) + 4 * S + 2 * 260 + 512
                          + 400 + 352 + S + 2 * S + 512 + 512)
        with ExitStack() as part:
            y = sb("y", [P, TT, D], F32, part)
            stage = y[:, 0, 0:3 * P].rearrange("p (a n) -> p a n", a=3)
        with ExitStack() as part:
            moe_g = sb("moe_g", [P, D], F32, part)
        with ExitStack() as part:
            sg = sb("sg", [P, TT, 256], F32, part)
            hid = sb("hid", [P, TT, 256], F32, part)
            hTh = sb("hTh", [P, 2, TT, P], F32R, part)
            hTl = sb("hTl", [P, 2, TT, P], F32R, part)
            unh = sb("unh", [P, TT, D], F32R, part)
            unl = sb("unl", [P, TT, D], F32R, part)
            sel = sb("sel", [P, TT, P], F32R, part)
            selT = sb("selT", [P, TT, P], F32R, part)
            size_f = 4 * (512 + 512 + 512 + 512 + 4096 + 256 + 256)
        ctx.enter_context(nc.sbuf_tensor("keep_b", [P, max(size_b, size_f) // 4 + 8], F32))

        with ExitStack() as part:
            sb("pad_w", [P, 1408], F32, part)
            ckvT = sb("ckvT", [P, S], F32, part)
            qtok = sb("qtok", [P, TT, HEADS, 96], F32, part)
            ktok = sb("ktok", [P, TT, HEADS, 96], F32, part)
            rin = sb("rin", [P, TT, 5, 32], F32, part)
            rot = sb("rot", [P, TT, 5, 32], F32, part)
            rt1 = sb("rt1", [P, TT, 5, 16], F32, part)
            sb("pad_u", [P, 96], F32, part)
            dec = sb("dec", [P, HEADS, 384], F32, part)
            rt2 = sb("rt2", [P, TT, 5, 16], F32, part)
            gref = sb("gref", [P, 2, 2], F32, part)
            sb("pad_0", [P, 344], F32, part)
            gS = sb("gS", [P, HEADS, 3, P], F32, part)
            vm = sb("vm", [P, TT, 256], F32, part)
            gE = sb("gE", [P, 5, P], F32, part)
            cumf = sb("cumf", [4, S], F32, part)
            aj = sb("aj", [4, S], F32, part)
            mrun = sb("mrun", [4, S], F32, part)
            negm = sb("negm", [4, S], F32, part)
            expnm = sb("expnm", [4, S], F32, part)
            sb("pad_2", [P, 128], F32, part)
            probT = sb("probT", [P, 3, HEADS, P], F32, part)
            sb("pad_3", [P, 512], F32, part)
            osq = sb("osq", [P, TT, HEADS, DH], F32, part)
            cqT = sb("cqT", [P, 2, S], F32, part)
            ctok = cqT[:, :, :]
            smax = sb("smax", [P, TT, HEADS], F32, part)
            psums = sb("psums", [P, TT, HEADS], F32, part)
            mcol = sb("mcol", [P, 16], F32, part)
            mden = sb("mden", [P, TT, HEADS], F32, part)
            gss = sb("gss", [P, TT, HEADS], F32, part)
            gls = sb("gls", [P, TT, HEADS], F32, part)
            grd = sb("grd", [P, TT, HEADS], F32, part)
            bst = sb("bst", [P, TT, 6], F32, part)
            bag = sb("bag", [P, TT, 2], F32, part)
            junk = sb("junk", [P, 256], F32, part)
            sb("pad_4", [P, 768 - 88], F32, part)
            qT = sb("qT", [96, HEADS, S], F32, part)
            kT = sb("kT", [96, HEADS, S], F32, part)
        with ExitStack() as part:
            u32 = sb("u32", [P, KD, S], F32, part)
        uTh = sb("uTh", [P, KD, S], F32R)
        uTl = sb("uTl", [P, KD, S], F32R)
        high = sb("high", [P, SPLIT, PIECE], F32R)
        low = sb("low", [P, SPLIT, PIECE], F32R)

        bank = [ctx.enter_context(nc.psum_tensor(f"bank{i}", [P, 512], F32)) for i in range(8)]
        NORM_BANKS = (0, 1, 4, 7)
        Z_BANKS = (2, 3, 5, 6)
        NORM2_BANKS = (0, 1, 4, 2)
        FUSE_ORDER = (0, 3, 2, 1)
        FUSE_DONE = ("y_m", "y_c", "y_g", "y_a")
        FUSE_BANKS = (2, 4, 1, 0)
        OUT_BANKS = (3, 5, 6, 7)
        SCATTER_BANKS = (1, 5, 6, 7)
        SLOTS_AT, SELECT_AT, GATHER_AT = 2, 4, 6

        fin_g = ring[:, 0, 0:D]
        xh, xl = uTh[:, :, 0:P], uTl[:, :, 0:P]
        xs = u32[:, :, P:2 * P]

        sems = {}
        for name in (
                "x_in", "pos_in", "stage_zero", "norm1_in", "rows_in", "gateb_in", "ln_in", "router_in", "moe_g_in", "ung_ready", "ukv_in", "final_in",
                "consts", "cols_tr", "cols_ready", "ang_ready", "sin_ready",
                "high_ready", "low_ready", "piece_used",
                "h_ready", "rstd_ready", "un_ready", "norm_tr", "uth_ready", "utl_ready",
                "z_act", "z_dve", "qk_conv", "qk_sig", "qk_ready", "conv_done",
                "lat_rstd", "lat_ready", "lat_tr", "lat_T", "gates_abs", "gates_ln", "lf_ready",
                "gate_tr", "gpre_ready", "gla_abs", "gla_ln", "gla_cum", "mcum_ready", "expnm_ready",
                "mcol_tr", "mcol_ready", "q_ready", "kv_ready", "qkv_evac", "rot_ready",
                "gla_exp", "gla_qk", "x_ready", "s_ready", "dt_ready", "pt_ready", "num_ready",
                "y_m", "qkT_tr", "qT_ready", "kT_ready", "sc_ready", "smax_ready", "p_ready",
                "p_tr", "pT_ready", "pv_ready", "y_a", "ga_ready", "gs_ready", "go_ready",
                "osq_ready", "gss_ready", "grd_ready", "y_g", "conf_tr", "bn_ready", "conf_rstd",
                "conf_n", "conf_ln", "conf_sig", "y_c",
                "silu_ready", "hid_ready", "hid_tr", "hTh_ready",
                "hTl_ready", "logit_ready", "gap_ready", "egap_ready", "routed_ready",
                "rank_ready", "jobs_ready", "unh_ready", "unl_ready", "key_copied", "u32_act", "u32_dve", "over_ready", "group_rstd", "group_ready", "xs_act", "xs_dve", "xT_tr", "sel_ready", "selT_tr", "wcol_ready",
                "gath_ready", "xh_ready", "xl_ready", "selT_ready", "yh_ready", "yl_ready",
                "scat_ready", "added", "out_ready", "stored",
                "aT_tr", "act_chain", "dve_chain", "pool_chain"):
            sems[name] = ctx.enter_context(nc.semaphore(name))
        loaded = [ctx.enter_context(nc.semaphore(f"loaded{i}")) for i in range(RING)]
        s = sems

        def bc(ap, shape):
            return ap.to_broadcast(shape)

        def col(i):
            return cols[:, i // P, i % P:i % P + 1]

        NORM2, FUSE, CONVB, MCONVB, MCONVW, GLAB, KVG, QG1, QG2 = 16, 32, 48, 52, 60, 92, 94, 96, 98
        CONVW = P
        NORM1 = 2 * P

        def slot(n):
            return ring[:, n % RING, :]

        def jobs(eng, body):
            body(0, True)
            with eng.Fori(1, E) as j:
                body(j, False)
            eng.wait_ge(s["jobs_ready"], 1)
            n_over = eng.value_load(jobs_i[0:1, 3:4], min_val=0, max_val=OVER)
            with eng.If(n_over > 0):
                with eng.Fori(E, n_over + E) as j:
                    body(j, False)
            return n_over + E

        block = ctx.enter_context(nc.Block())

        @block.sync
        def _(sp):
            def load(n, dst_src, rounds=None):
                if rounds is not None:
                    sp.wait_ge(s["low_ready"], rounds * N_FFN + (n - RING + 1))
                elif n >= RING:
                    sp.wait_ge(s["low_ready"], n - RING + 1)
                assert len(dst_src) == 2
                for dst, src in dst_src:
                    sp.dma_start(dst, src).then_inc(loaded[n % RING], 16)

            def load_in(l, p):
                n = LAYER_PIECES[l] + p
                segs = W_IN_PIECES[p]
                width = sum(w for _, w in segs)
                dst = slot(n)[:, 0:KD * width].rearrange("p (k n) -> p k n", k=KD)
                src = w_in[l].rearrange("(k p) n -> p k n", p=P)
                if len(segs) == 2:
                    (c0, a), (c1, b) = segs
                    load(n, [(dst[:, :, 0:a], src[:, :, c0:c0 + a]),
                             (dst[:, :, a:a + b], src[:, :, c1:c1 + b])])
                else:
                    c0, a = segs[0]
                    half = KD // 2
                    load(n, [(dst[:, i:i + half, :], src[:, i:i + half, c0:c0 + a]) for i in (0, half)])

            def load_out(l, p):
                n = LAYER_PIECES[l] + N_IN + p
                dst = slot(n).rearrange("p (k n) -> p k n", k=2)
                src = w_out[l].rearrange("(k p) n -> p k n", p=P)
                g = FUSE_ORDER[p]
                load(n, [(dst[:, i:i + 1, :], src[:, 2 * g + i:2 * g + i + 1, :]) for i in (0, 1)])

            def load_ffn(n0, wg, wu, wd, rounds=None):
                for i, (kind, c) in enumerate(FFN_ORDER):
                    n = n0 + i
                    if kind == "d":
                        dst = slot(n).rearrange("p (f n) -> p f n", f=2)
                        src = wd.rearrange("(f p) n -> p f n", p=P)
                        load(n, [(dst[:, f:f + 1, :], src[:, 2 * c + f:2 * c + f + 1, :]) for f in (0, 1)], rounds)
                    else:
                        dst = slot(n).rearrange("p (k n) -> p k n", k=4)
                        k0 = 0 if kind == "a" else 4
                        load(n, [(dst[:, :, g * 256:(g + 1) * 256],
                                  w.rearrange("(k p) n -> p k n", p=P)[:, k0:k0 + 4, c * F_CH:(c + 1) * F_CH])
                                 for g, w in enumerate((wg, wu))], rounds)

            for t in range(TT):
                sp.dma_start(h[:, t, :], x[0, t * P:(t + 1) * P, :]).then_inc(s["x_in"], 16)
            for p in range(RING):
                if p == 4:
                    sp.wait_ge(s["rows_in"], 16 * 10)
                load_in(0, p)
            for p in range(N_OUT):
                load_out(0, p)
            load_ffn(DENSE0, ffn_w_gate[0], ffn_w_up[0], ffn_w_down[0])
            for p in range(N_IN):
                load_in(1, p)
            for p in range(N_OUT):
                load_out(1, p)

            def expert(e, j):
                pick_e = lambda w: w[0, bass.ds(e, 1)].rearrange("a k n -> (a k) n")
                load_ffn(MOE0, pick_e(moe_w_gate), pick_e(moe_w_up), pick_e(moe_w_down), j)

            with sp.Fori(0, E) as j:
                expert(j, j)
            sp.wait_ge(s["jobs_ready"], 1)
            n_over = sp.value_load(jobs_i[0:1, 3:4], min_val=0, max_val=OVER)
            with sp.If(n_over > 0):
                with sp.Fori(0, n_over) as o:
                    e = sp.value_load(jobs_i[0:1, bass.ds(o, 1)], min_val=0, max_val=E - 1)
                    expert(e, o + E)
            sp.wait_ge(s["low_ready"], N_FFN * n_over + (MOE0 + N_FFN * E))
            sp.dma_start(fin_g, bc(final_norm_g.rearrange("(a d) -> a d", a=1), [P, D])).then_inc(s["final_in"], 16)
            for t in range(TT):
                sp.wait_ge(s["out_ready"], t + 1)
                sp.dma_start(out[0, t * P:(t + 1) * P, :], h[:, t, :]).then_inc(s["stored"], 16)
            sp.wait_ge(s["stored"], 16 * TT)

        @block.gpsimd
        def _(pool):
            chain = Chain(pool, s["pool_chain"])
            pool.dma_start(pos_i[:, :], positions.rearrange("a (t p) -> p (a t)", p=P),
                           allow_slow_non_contiguous=True).then_inc(s["pos_in"], 16)
            for tile, value in ((ident[:, :], 0.0), (ones[:, :], 1.0), (epst[:, :], EPS), (mask_kt[:, :], 0.0),
                                (mask_qt[:, :], 0.0), (gla_mask[:, :, :], 32.0 ** -0.5), (before[:, :], 1.0)):
                pool.memset(tile, value)
            for i in range(16):
                pool.memset(invf[:, i:i + 1], float(np.float32(1.0) / np.float32(10000.0) ** np.float32(i / 16)))
            chain.done(pool.iota(iota[:, :], [[1, P]], base=0, channel_multiplier=0,
                                 allow_small_or_imprecise_dtypes=True))
            chain.wait()
            pool.affine_select(out=ident[:, :], in_=ident[:, :], compare_op=ALU.not_equal, fill=1.0,
                               base=0, pattern=[[-1, P]], channel_multiplier=1)
            pool.affine_select(out=mask_kt[:, :], in_=mask_kt[:, :], compare_op=ALU.is_ge, fill=NEG,
                               base=0, pattern=[[1, P]], channel_multiplier=-1)
            pool.affine_select(out=mask_qt[:, :], in_=mask_qt[:, :], compare_op=ALU.is_ge, fill=NEG,
                               base=0, pattern=[[-1, P]], channel_multiplier=1)
            for b in (0, 2):
                pool.affine_select(out=gla_mask[:, b, :], in_=gla_mask[:, b, :], compare_op=ALU.is_ge, fill=0.0,
                                   base=0, pattern=[[1, P]], channel_multiplier=-1)
            pool.affine_select(out=before[:, :], in_=before[:, :], compare_op=ALU.is_ge, fill=0.0,
                               base=-1, pattern=[[1, P]], channel_multiplier=-1).then_inc(s["consts"], 1)

            pool.wait_ge(s["stage_zero"], 1)
            rows = lambda i, n: stage[i:i + n, 0, :]
            for dst, src in [
                    (rows(NORM2, 16), norm2_g.rearrange("l (k p) -> (l k) p", p=P)),
                    (rows(FUSE, 16), fuse_g.rearrange("l (k p) -> (l k) p", p=P)),
                    (rows(CONVB, 4), conv_b.rearrange("l (k p) -> (l k) p", p=P)),
                    (rows(MCONVB, 8), mlstm_conv_b.rearrange("l (k p) -> (l k) p", p=P)),
                    (rows(MCONVW, 32), mlstm_conv_w.rearrange("l i (k p) -> (l i k) p", p=P)),
                    (rows(GLAB, 2), gla_b_alpha),
                    (rows(KVG, 2), mla_kv_norm_g),
                    (rows(QG1, 2), mla_q_norm_g[:, 0:P]),
                    (stage[QG2:QG2 + 2, 0, 0:64], mla_q_norm_g[:, P:192]),
                    (stage[0:2 * CONV * DEPTH, 1, :], conv_w.rearrange("l i (k p) -> (l i k) p", p=P))]:
                pool.dma_start(dst, src).then_inc(s["rows_in"], 16)
            for l in range(DEPTH):
                pool.dma_start(gate_b[:, l, :], bc(mlstm_gate_b[l:l + 1, :], [P, 8])).then_inc(s["gateb_in"], 16)
            pool.dma_start(router[:, :, :], moe_router[0].rearrange("(k p) e -> p k e", p=P)).then_inc(s["router_in"], 16)
            for l in range(DEPTH):
                if l:
                    pool.wait_ge(s["conf_ln"], l)
                for i, src in enumerate((conv_ln_g, conv_ln_b)):
                    pool.dma_start(ln_gb[:, i, :], bc(src[l:l + 1, :], [P, 256])).then_inc(s["ln_in"], 16)
                pool.wait_ge(s["norm_tr"], 4 * (3 * l + 1))
                pool.dma_start(walpha[:, :], gla_w_alpha[l]).then_inc(s["ukv_in"], 16)
                pool.dma_start(uq[:, 0, :], mla_w_uq[l, 0:P, :]).then_inc(s["ukv_in"], 16)
                pool.dma_start(uq[0:64, 1, :], mla_w_uq[l, P:192, :]).then_inc(s["ukv_in"], 16)
                pool.dma_start(ukv[:, :], mla_w_ukv[l]).then_inc(s["ukv_in"], 16)
                pool.wait_ge(s["qk_sig"], l + 1)
                pool.tensor_tensor(qkc[:, :, :], qkc[:, :, :], qkpre[:, :, 0:S], ALU.mult).then_inc(s["qk_ready"], 1)
                pool.wait_ge(s["gla_exp"], l + 1)
                q, k = gqk[:, 0, :], gqk[:, 1, :]
                for i, part in enumerate((q[:, 0:P], q[:, P:S], k[:, 0:P], k[:, 0:P], k[:, P:S])):
                    last = pool.tensor_tensor(gE[:, i, :], gE[:, i, :], part, ALU.mult)
                last.then_inc(s["gla_qk"], 1)
                pool.wait_ge(s["ln_in"], 32 * (l + 1))
                pool.wait_ge(s["conf_n"], l + 1)
                chain.done(pool.tensor_tensor(ctok[:, :, :], ctok[:, :, :],
                                              bc(ln_gb[:, 0:1, :], [P, TT, 256]), ALU.mult))
                chain.wait()
                pool.tensor_tensor(ctok[:, :, :], ctok[:, :, :], bc(ln_gb[:, 1:2, :], [P, TT, 256]),
                                   ALU.add).then_inc(s["conf_ln"], 1)
            pool.wait_ge(s["utl_ready"], 4 * 5)
            pool.dma_start(moe_g[:, :], bc(norm2_g[DEPTH - 1:DEPTH, :], [P, D])).then_inc(s["moe_g_in"], 16)

        @block.scalar
        def _(act):
            chain = Chain(act, s["act_chain"])

            def split_high(n, job=None, width=PIECE):
                jobbed = job is not None
                rounds, pieces = (3 * job, N_FFN * job) if jobbed else (0, 0)
                act.wait_ge(loaded[n % RING], 32 * rounds + 32 * (n // RING + 1))
                if jobbed or n >= SPLIT:
                    act.wait_ge(s["piece_used"], pieces + (n - SPLIT + 1))
                act.activation(high[:, n % SPLIT, 0:width], slot(n)[:, 0:width], ACT.Copy).then_inc(s["high_ready"], 1)

            def in_width(p):
                return KD * sum(w for _, w in W_IN_PIECES[p])

            def norm(ready, squares=un):
                act.preload_act_table_set(LN_EXP)
                for t in range(TT):
                    if ready:
                        act.wait_ge(s["h_ready"], ready[t])
                    chain.done(act.activation(squares[:, t, :], h[:, t, :], ACT.Square, accum_out=ss[:, t, 0:1]))
                chain.wait()
                chain.done(act.activation(lnv[:, :, 0:1], ss[:, :, 0:1], ACT.Ln, bias=epst[:, :], scale=1.0 / D))
                chain.wait()
                act.activation(rstd[:, :, 0:1], lnv[:, :, 0:1], ACT.Exp, scale=-0.5).then_inc(s["rstd_ready"], 1)

            def gains(k, first, banks=NORM_BANKS):
                for g in range(4):
                    gains_of(k, first, g, g, banks[g])

            def gains_of(k, first, at, g, b):
                act.wait_ge(s["norm_tr"], 4 * k + at + 1)
                for i in range(2):
                    kd = 2 * g + i
                    last = act.activation(uTh[:, kd, :], bank[b][:, i * S:(i + 1) * S], ACT.Copy, scale=col(first + kd))
                last.then_inc(s["uth_ready"], 1)

            def group_rstd(l, at):
                g = FUSE_ORDER[at]
                act.wait_ge(s[FUSE_DONE[at]], l + 1)
                for t in range(TT):
                    chain.wait()
                    chain.done(act.activation(junk[:, :], y[:, t, g * 256:(g + 1) * 256],
                                              ACT.Square, accum_out=ss[:, t, g:g + 1]))
                chain.wait()
                chain.done(act.activation(lnv[:, :, g:g + 1], ss[:, :, g:g + 1], ACT.Ln, bias=epst[:, :], scale=1.0 / 256))
                chain.wait()
                act.activation(rstd[:, :, g:g + 1], lnv[:, :, g:g + 1], ACT.Exp, scale=-0.5).then_inc(s["group_rstd"], 1)

            def ffn(n0, job, job_n, tiles, after_split={}, after_chunk={}, after_last=None, scale=None, start=0):
                done = [start]

                def upto(i):
                    while done[0] <= min(i, N_FFN - 1):
                        split_high(n0 + done[0], job)
                        after_split.get(done[0], lambda: None)()
                        done[0] += 1

                for c in range(CHUNKS):
                    at = FFN_AT[("b", c)]
                    upto(at + 2)
                    act.wait_ge(s["piece_used"], (N_FFN * job if job is not None else 0) + (n0 + at + 1))
                    for t in range(tiles):
                        last = act.activation(sg[:, t, :], bank[t][:, 0:256], ACT.Silu,
                                              scale=1.0 if scale is None else scale[:, t, 0:1])
                    last.then_inc(s["silu_ready"], 1)
                    if c == CHUNKS - 1 and after_last:
                        after_last()
                    upto(at + 3)
                    act.wait_ge(s["hid_tr"], job_n * CHUNKS + (c + 1))
                    act.activation(hTh[:, :, 0:tiles, :],
                                   bank[4][:, 0:2 * tiles * P].rearrange("p (f t n) -> p f t n", f=2, t=tiles),
                                   ACT.Copy).then_inc(s["hTh_ready"], 1)
                    after_chunk.get(c, lambda: None)()

            act.wait_ge(s["stage_zero"], 1)
            act.dma_start(stage[0:16, 2, :], norm1_g.rearrange("l (k p) -> (l k) p", p=P)).then_inc(s["norm1_in"], 16)
            act.preload_act_table_set(LN_EXP)
            act.wait_ge(s["x_in"], 32)
            act.wait_ge(s["consts"], 1)
            for l in range(DEPTH):
                n0 = LAYER_PIECES[l]
                if l:
                    for n in range(2):
                        split_high(n0 + n, width=in_width(n))
                norm((3, 4) if l else None)
                if not l:
                    for n in range(2):
                        split_high(n0 + n, width=in_width(n))
                if l == 0:
                    act.wait_ge(s["cols_ready"], 1)
                gains(3 * l, NORM1 + KD * l)
                if l == 0:
                    act.wait_ge(s["ang_ready"], 1)
                    act.activation(cossin[:, :, :, :], ang[:, :, :, :], ACT.Sin).then_inc(s["sin_ready"], 1)
                act.preload_act_table(ACT.Sigmoid)
                split_high(n0 + 2, width=in_width(2))
                for p in range(N_IN):
                    if p + SPLIT < N_IN:
                        split_high(n0 + p + SPLIT, width=in_width(p + SPLIT))
                    src = bank[Z_BANKS[p % 4]]
                    tiles2 = lambda w: src[:, 0:TT * w].rearrange("p (t n) -> p t n", t=TT)
                    if p in (1, 4, 5, 6, 7, 8, 9):
                        act.wait_ge(s["piece_used"], n0 + p + 1)
                    if p == 1:
                        act.activation(gsig[:, :, :], tiles2(256), ACT.Sigmoid).then_inc(s["z_act"], 1)
                    if p == 4:
                        act.activation(zif[:, :, :], tiles2(200), ACT.Copy).then_inc(s["z_act"], 1)
                    if p == 5:
                        act.activation(zkv[:, :, :], tiles2(176), ACT.Copy).then_inc(s["z_act"], 1)
                    if p == 6:
                        act.wait_ge(s["aT_tr"], l + 1)
                        act.activation(aT[:, :], bank[7][0:16, 0:S], ACT.Copy).then_inc(s["z_act"], 1)
                        act.activation(gqk[:, :, :], tiles2(256), ACT.Copy).then_inc(s["z_act"], 1)
                    if p == 7:
                        act.activation(vaug[:, :, :, 0:DH], src[:, :].rearrange("p (t h n) -> p t h n", t=TT, h=HEADS),
                                       ACT.Copy).then_inc(s["z_act"], 1)
                        act.wait_ge(s["qk_conv"], l + 1)
                        act.activation(qkpre[:, :, 0:S], qkc[:, :, :], ACT.Sigmoid).then_inc(s["qk_sig"], 1)
                    if p == 8:
                        act.activation(osig[:, :, :], tiles2(256), ACT.Sigmoid).then_inc(s["z_act"], 1)
                    if p == 9:
                        act.activation(grs[:, :, :], tiles2(256), ACT.Sigmoid).then_inc(s["z_act"], 1)
                        act.preload_act_table_set(LN_EXP)
                        for t in range(TT):
                            chain.done(act.activation(gv[:, 0, 0:192], zif[:, t, 8:200], ACT.Square, accum_out=lss[:, 0, t:t + 1]))
                            chain.wait()
                            chain.done(act.activation(gv[:, 0, 0:128], zkv[:, t, 0:128], ACT.Square, accum_out=lss[:, 1, t:t + 1]))
                            chain.wait()
                        chain.done(act.activation(lln[:, 0, :], lss[:, 0, :], ACT.Ln, bias=epst[:, :], scale=1.0 / 192))
                        chain.done(act.activation(lln[:, 1, :], lss[:, 1, :], ACT.Ln, bias=epst[:, :], scale=1.0 / 128))
                        chain.wait()
                        act.activation(lrs[:, :, :], lln[:, :, :], ACT.Exp, scale=-0.5).then_inc(s["lat_rstd"], 1)
                        act.wait_ge(s["gates_abs"], l + 1)
                        chain.done(act.activation(gln[:, :, :], gab[:, :, :], ACT.Exp))
                        chain.wait()
                        act.activation(gln[:, :, :], gln[:, :, :], ACT.Ln, bias=1.0).then_inc(s["gates_ln"], 1)
                        act.wait_ge(s["gla_abs"], l + 1)
                        chain.done(act.activation(gab2[:, :], gab2[:, :], ACT.Exp))
                        chain.wait()
                        act.activation(gab2[:, :], gab2[:, :], ACT.Ln, bias=1.0).then_inc(s["gla_ln"], 1)
                    if p == 10:
                        act.wait_ge(s["piece_used"], n0 + p + 1)
                        act.activation(gv[:, :, :], tiles2(256), ACT.Copy).then_inc(s["z_act"], 1)

                act.wait_ge(s["mcum_ready"], l + 1)
                act.activation(expnm[:, :], mrun[:, :], ACT.Exp, scale=-1.0).then_inc(s["expnm_ready"], 1)
                act.wait_ge(s["q_ready"], l + 1)
                for t in range(TT):
                    src = bank[(3, 5)[t]][:, 0:384].rearrange("p (h n) -> p h n", h=HEADS)
                    act.activation(rin[:, t, 0:4, :], src[:, :, 64:96], ACT.Copy)
                    act.activation(qtok[:, t, :, 0:64], src[:, :, 0:64], ACT.Copy)
                act.activation(rin[:, :, 4, :], zkv[:, :, 128:160], ACT.Copy)
                act.wait_ge(s["kv_ready"], l + 1)
                for t in range(TT):
                    src = bank[(6, 1)[t]][:, :].rearrange("p (h n) -> p h n", h=HEADS)
                    act.activation(ktok[:, t, :, 0:64], src[:, :, 0:64], ACT.Copy)
                    last = act.activation(vm[:, t, :].rearrange("p (h n) -> p h n", h=HEADS), src[:, :, 64:128], ACT.Copy)
                last.then_inc(s["qkv_evac"], 1)
                act.wait_ge(s["mcol_ready"], l + 1)
                for hd in (0, 1):
                    act.wait_ge(s["x_ready"], HEADS * l + hd + 1)
                    xb = bank[(2, 4)[hd % 2]]
                    act.activation(dec[:, hd, 0:256], xb[:, 0:256], ACT.Exp, bias=mcol[:, hd:hd + 1])
                    act.activation(dec[:, hd, 256:384], xb[:, 256:384], ACT.Exp,
                                   bias=mcol[:, 4 + hd:5 + hd]).then_inc(s["dt_ready"], 1)
                for i in range(2):
                    act.wait_ge(s["qkT_tr"], 4 * l + i + 1)
                    act.activation(qT[:, 2 * i:2 * i + 2, :], bank[(2, 4)[i]][0:96, :].rearrange("p (h n) -> p h n", h=2),
                                   ACT.Copy).then_inc(s["qT_ready"], 1)
                act.wait_ge(s["gla_cum"], l + 1)
                for i in range(2):
                    act.activation(gE[:, i, :], b16[:, i * P:(i + 1) * P], ACT.Exp, bias=gref[:, 0, i:i + 1], scale=1.0 / 16)
                act.activation(gE[:, 2, :], b16[:, 0:P], ACT.Exp, bias=gref[:, 1, 0:1], scale=-1.0 / 16)
                act.activation(gE[:, 3:5, :].rearrange("p a n -> p (a n)"), b16[:, :], ACT.Exp,
                               bias=gref[:, 1, 1:2], scale=-1.0 / 16).then_inc(s["gla_exp"], 1)
                for hd in (2, 3):
                    act.wait_ge(s["x_ready"], HEADS * l + hd + 1)
                    xb = bank[(2, 4)[hd % 2]]
                    act.activation(dec[:, hd, 0:256], xb[:, 0:256], ACT.Exp, bias=mcol[:, hd:hd + 1])
                    act.activation(dec[:, hd, 256:384], xb[:, 256:384], ACT.Exp,
                                   bias=mcol[:, 4 + hd:5 + hd]).then_inc(s["dt_ready"], 1)
                act.wait_ge(s["smax_ready"], l + 1)
                act.wait_ge(s["gla_exp"], l + 1)
                scale = 96.0 ** -0.5
                for hd in range(HEADS):
                    chain.done(act.activation(probs[:, hd * P:(hd + 1) * P], bank[6][:, hd * P:(hd + 1) * P], ACT.Exp,
                                              bias=smax[:, 0, hd:hd + 1], scale=scale, accum_out=psums[:, 0, hd:hd + 1]))
                for hd in range(HEADS):
                    src = bank[(0, 5)[hd // 2]][:, (hd % 2) * S:(hd % 2 + 1) * S]
                    last = act.activation(probs[:, 512 + hd * S:512 + (hd + 1) * S], src, ACT.Exp,
                                          bias=smax[:, 1, hd:hd + 1], scale=scale, accum_out=psums[:, 1, hd:hd + 1])
                last.then_inc(s["p_ready"], 1)
                act.wait_ge(s["bn_ready"], l + 1)
                chain.done(act.activation(bst[:, :, 0], bag[:, :, 1], ACT.Ln, bias=epst[:, :]))
                chain.wait()
                act.activation(bst[:, :, 1], bst[:, :, 0], ACT.Exp, scale=-0.5).then_inc(s["conf_rstd"], 1)
                act.preload_act_table(ACT.Sigmoid)
                act.wait_ge(s["conf_ln"], l + 1)
                act.activation(cacc[:, :, :], ctok[:, :, :], ACT.Sigmoid).then_inc(s["conf_sig"], 1)
                act.preload_act_table_set(LN_EXP)
                for i in range(3):
                    act.wait_ge(s["p_tr"], 3 * l + i + 1)
                    act.activation(probT[:, i, :, :], bank[(3, 5, 6)[i]][:, :].rearrange("p (h n) -> p h n", h=HEADS),
                                   ACT.Copy).then_inc(s["pT_ready"], 1)
                split_high(n0 + N_IN)
                group_rstd(l, 0)
                group_rstd(l, 1)
                act.wait_ge(s["go_ready"], l + 1)
                act.activation(osq[:, :, :, :].rearrange("p t h n -> p (t h n)"), bank[7][:, :],
                               ACT.Square).then_inc(s["osq_ready"], 1)
                act.wait_ge(s["gss_ready"], l + 1)
                chain.done(act.activation(gls[:, :, :], gss[:, :, :], ACT.Ln, bias=epst[:, :], scale=1.0 / DH))
                chain.wait()
                act.activation(grd[:, :, :], gls[:, :, :], ACT.Exp, scale=-0.5).then_inc(s["grd_ready"], 1)
                gains_of(3 * l + 1, FUSE + KD * l, 0, FUSE_ORDER[0], FUSE_BANKS[0])
                gains_of(3 * l + 1, FUSE + KD * l, 1, FUSE_ORDER[1], FUSE_BANKS[1])
                group_rstd(l, 2)
                split_high(n0 + N_IN + 1)
                gains_of(3 * l + 1, FUSE + KD * l, 2, FUSE_ORDER[2], FUSE_BANKS[2])
                group_rstd(l, 3)
                split_high(n0 + N_IN + 2)
                gains_of(3 * l + 1, FUSE + KD * l, 3, FUSE_ORDER[3], FUSE_BANKS[3])
                split_high(n0 + N_IN + 3)
                if l == 0:
                    for n in range(2):
                        split_high(DENSE0 + n)
                    gains(3 * l + 2, NORM2 + KD * l, NORM2_BANKS)
                    norm((1, 2))
                    act.preload_act_table(ACT.Silu)
                    act.wait_ge(s["rstd_ready"], 2)
                    ffn(DENSE0, None, 0, TT, scale=rstd, start=2)
            for n in range(SPLIT):
                split_high(MOE0 + n)
            for g in (0, 1):
                act.wait_ge(s["norm_tr"], 4 * 5 + g + 1)
                for i in range(2):
                    kd = 2 * g + i
                    last = act.activation(u32[:, kd, :], bank[NORM2_BANKS[g]][:, i * S:(i + 1) * S], ACT.Copy,
                                          scale=col(NORM2 + KD + kd))
                last.then_inc(s["u32_act"], 1)
            norm((5, 6))

            for t in range(TT):
                act.wait_ge(s["ung_ready"], t + 1)
                act.activation(unh[:, t, :], un[:, t, :], ACT.Copy).then_inc(s["unh_ready"], 1)
            act.wait_ge(s["gap_ready"], 1)
            act.activation(egap[:, :], gap[:, :], ACT.Exp).then_inc(s["egap_ready"], 1)
            act.preload_act_table(ACT.Silu)

            def tokens_out(n):
                act.wait_ge(s["gath_ready"], n + 1)
                act.activation(xs[:, 0:4, :], bank[5][:, :].rearrange("p (k n) -> p k n", k=4), ACT.Copy).then_inc(s["xs_act"], 1)

            def tokens_high(j):
                act.wait_ge(s["xT_tr"], j + 1)
                for i in range(2):
                    last = act.activation(xh[:, 4 * i:4 * i + 4, :], bank[5 + i][:, :].rearrange("p (k n) -> p k n", k=4), ACT.Copy)
                last.then_inc(s["xh_ready"], 1)

            def result_high(n):
                act.wait_ge(s["piece_used"], N_FFN * n + MOE0)
                for i in range(2):
                    last = act.activation(yh[:, i * 512:(i + 1) * 512], bank[2 + i][:, :], ACT.Copy, scale=wslot[:, :])
                last.then_inc(s["yh_ready"], 1)

            def job(j, first):
                def slots():
                    act.wait_ge(s["selT_tr"], j + 1)
                    if not first:
                        act.wait_ge(s["yl_ready"], j)
                    act.activation(selT[:, :, :], bank[7][:, 0:2 * P].rearrange("p (t n) -> p t n", t=TT), ACT.Copy)
                    act.activation(wslot[:, :], bank[7][:, 2 * P:2 * P + 1], ACT.Copy).then_inc(s["selT_ready"], 1)

                def next_tokens():
                    act.wait_ge(s["piece_used"], N_FFN * j + (MOE0 + FFN_AT[("b", CHUNKS - 1)] + 1))
                    tokens_high(j + 1)

                ffn(MOE0, j, j + 1, 1, {} if first else {1: lambda: result_high(j)},
                    {SLOTS_AT: slots, GATHER_AT: lambda: tokens_out(j + 1)}, after_last=next_tokens,
                    start=SPLIT if first else 0)

            tokens_out(0)
            tokens_high(0)
            result_high(jobs(act, job))
            norm((7, 8), u32[:, :, :].rearrange("p (t k) n -> p t (k n)", t=TT))

        @block.vector
        def _(dve):
            chain = Chain(dve, s["dve_chain"])

            def split_low(n, job=None, width=PIECE):
                pieces = N_FFN * job if job is not None else 0
                dve.wait_ge(s["high_ready"], pieces + (n + 1))
                dve.tensor_tensor(low[:, n % SPLIT, 0:width], slot(n)[:, 0:width],
                                  high[:, n % SPLIT, 0:width].bitcast(F32), ALU.subtract).then_inc(s["low_ready"], 1)

            def in_width(p):
                return KD * sum(w for _, w in W_IN_PIECES[p])

            def normalize(n):
                dve.wait_ge(s["rstd_ready"], n)
                for t in range(TT):
                    dve.tensor_scalar(un[:, t, :], h[:, t, :], rstd[:, t, 0:1], None, ALU.mult).then_inc(s["un_ready"], 1)

            def normalize_group(l, at):
                g = FUSE_ORDER[at]
                dve.wait_ge(s["group_rstd"], 4 * l + at + 1)
                for t in range(TT):
                    part = y[:, t, g * 256:(g + 1) * 256]
                    last = dve.tensor_scalar(part, part, rstd[:, t, g:g + 1], None, ALU.mult)
                last.then_inc(s["group_ready"], 1)

            def gains(k, first, banks=NORM_BANKS):
                for g in range(4):
                    gains_of(k, first, g, g, banks[g])

            def gains_of(k, first, at, g, b):
                dve.wait_ge(s["uth_ready"], 4 * k + at + 1)
                for i in range(2):
                    kd = 2 * g + i
                    last = dve.scalar_tensor_tensor(
                        out=uTl[:, kd, :], in0=bank[b][:, i * S:(i + 1) * S], scalar=col(first + kd),
                        in1=uTh[:, kd, :].bitcast(F32), op0=ALU.mult, op1=ALU.subtract)
                last.then_inc(s["utl_ready"], 1)

            def ffn(n0, job, job_n, tiles, after_split={}, after_chunk={}, after_last=None, scale=None, start=0):
                done = [start]

                def upto(i):
                    while done[0] <= min(i, N_FFN - 1):
                        split_low(n0 + done[0], job)
                        after_split.get(done[0], lambda: None)()
                        done[0] += 1

                for c in range(CHUNKS):
                    at = FFN_AT[("b", c)]
                    upto(at + (1 if c == 0 else 2))
                    dve.wait_ge(s["silu_ready"], job_n * CHUNKS + (c + 1))
                    for t in range(tiles):
                        if scale is None:
                            last = dve.tensor_tensor(hid[:, t, :], bank[t][:, 256:512], sg[:, t, :], ALU.mult)
                        else:
                            last = dve.scalar_tensor_tensor(out=hid[:, t, :], in0=bank[t][:, 256:512], scalar=scale[:, t, 0:1],
                                                            in1=sg[:, t, :], op0=ALU.mult, op1=ALU.mult)
                    last.then_inc(s["hid_ready"], 1)
                    if c == CHUNKS - 1 and after_last:
                        after_last()
                    upto(at + 3)
                    dve.wait_ge(s["hTh_ready"], job_n * CHUNKS + (c + 1))
                    dve.tensor_tensor(hTl[:, :, 0:tiles, :],
                                      bank[4][:, 0:2 * tiles * P].rearrange("p (f t n) -> p f t n", f=2, t=tiles),
                                      hTh[:, :, 0:tiles, :].bitcast(F32), ALU.subtract).then_inc(s["hTl_ready"], 1)
                    after_chunk.get(c, lambda: None)()

            def add_to_h(banks, sem, values):
                for i, b in enumerate(banks):
                    t, half = divmod(i, 2)
                    dve.wait_ge(sem, values[i])
                    dst = h[:, t, half * 512:(half + 1) * 512]
                    last = dve.tensor_tensor(dst, bank[b][:, :], dst, ALU.add)
                    if half == 1:
                        last.then_inc(s["h_ready"], 1)

            def angles():
                c1 = 6.28125
                c2 = float(np.float32(2 * math.pi - c1))
                c3 = 2 * math.pi - c1 - c2
                magic = 1.5 * 2.0 ** 23
                dve.wait_ge(s["pos_in"], 16)
                chain.done(dve.tensor_copy(pos_f[:, :], pos_i[:, :]))
                chain.wait()
                for i in range(2):
                    for t in range(TT):
                        chain.done(dve.tensor_scalar(ang[:, i, t, :], invf[:, :], pos_f[:, t:t + 1], None, ALU.mult))
                chain.wait()
                for i in range(2):
                    chain.done(dve.tensor_scalar(turn[:, i, :, :], ang[:, i, :, :], 1 / (2 * math.pi),
                                                 0.0 if i else 0.25, ALU.mult, ALU.add))
                chain.wait()
                for v in (magic, -magic):
                    chain.done(dve.tensor_scalar(turn[:, :, :, :], turn[:, :, :, :], v, None, ALU.add))
                    chain.wait()
                flat = lambda a: a[:, :, :, :].rearrange("p i t n -> p (i t n)")
                for c in (c1, c2, c3):
                    chain.done(dve.scalar_tensor_tensor(out=flat(ang), in0=flat(turn), scalar=-c, in1=flat(ang),
                                                        op0=ALU.mult, op1=ALU.add))
                    chain.wait()
                chain.done(dve.tensor_scalar(ang[:, 0, :, :], ang[:, 0, :, :], math.pi / 2, None, ALU.add))
                chain.wait()
                lim = float(np.nextafter(np.float32(math.pi), np.float32(0)))
                dve.tensor_scalar(flat(ang), flat(ang), lim, -lim, ALU.min, ALU.max).then_inc(s["ang_ready"], 1)

            dve.memset(stage[:, :, :], 0.0).then_inc(s["stage_zero"], 1)
            dve.wait_ge(s["consts"], 1)
            angles()
            for l in range(DEPTH):
                n0 = LAYER_PIECES[l]
                if l:
                    split_low(n0, width=in_width(0))
                normalize(2 * l + 1)
                if not l:
                    split_low(n0, width=in_width(0))
                split_low(n0 + 1, width=in_width(1))
                if l == 0:
                    dve.wait_ge(s["cols_tr"], 1)
                    dve.tensor_copy(cols[:, 2, :], bank[7][:, 0:P]).then_inc(s["cols_ready"], 1)
                    dve.wait_ge(s["cols_ready"], 1)
                gains(3 * l, NORM1 + KD * l)
                if l == 0:
                    dve.wait_ge(s["cols_tr"], 2)
                    dve.tensor_copy(cols[:, 0:2, :], bank[3][:, 0:2 * P].rearrange("p (a n) -> p a n", a=2)).then_inc(s["cols_ready"], 1)
                    dve.wait_ge(s["cols_ready"], 2)
                dve.memset(glu[:, :, 0:CONV - 1], 0.0)
                dve.memset(qkpre[:, :, 0:MCONV - 1], 0.0)
                chain.done(dve.memset(vaug[:, :, :, DH:DH + 1], 1.0))
                split_low(n0 + 2, width=in_width(2))

                def conv_step(i):
                    tap, c = divmod(i, 2)
                    taps = glu[:, c, tap:tap + S]
                    w = col(CONVW + (l * CONV + tap) * 2 + c)
                    chain.wait(1)
                    if tap == 0:
                        ins = dve.tensor_scalar(cacc[:, c, :], taps, w, col(CONVB + 2 * l + c), ALU.mult, ALU.add)
                    else:
                        ins = dve.scalar_tensor_tensor(out=cacc[:, c, :], in0=taps, scalar=w, in1=cacc[:, c, :],
                                                       op0=ALU.mult, op1=ALU.add)
                    chain.done(ins)
                    if i == 2 * CONV - 1:
                        chain.wait()

                def qk_step(i):
                    tap, c = divmod(i, 4)
                    taps = qkpre[:, c, tap:tap + S]
                    w = col(MCONVW + (l * MCONV + tap) * 4 + c)
                    chain.wait(3)
                    if tap == 0:
                        ins = dve.tensor_scalar(qkc[:, c, :], taps, w, col(MCONVB + 4 * l + c), ALU.mult, ALU.add)
                    else:
                        ins = dve.scalar_tensor_tensor(out=qkc[:, c, :], in0=taps, scalar=w, in1=qkc[:, c, :],
                                                       op0=ALU.mult, op1=ALU.add)
                    chain.done(ins)

                conv_at = [0]

                def conv_steps(n):
                    for _ in range(n):
                        if conv_at[0] < 2 * CONV:
                            conv_step(conv_at[0])
                            conv_at[0] += 1

                def mlstm_gates():
                    dve.wait_ge(s["z_act"], 9 * l + 2)
                    dve.wait_ge(s["gateb_in"], 32)
                    chain.done(dve.tensor_tensor(gb[:, :, :], zif[:, :, 0:8], bc(gate_b[:, l:l + 1, :], [P, TT, 8]), ALU.add))
                    chain.wait()
                    chain.done(dve.tensor_scalar(gmn[:, :, :], gb[:, :, 4:8], 0.0, None, ALU.min))
                    chain.done(dve.tensor_scalar(gab[:, :, :], gb[:, :, 4:8], 0.0, None, ALU.max))
                    chain.wait()
                    dve.tensor_tensor(gab[:, :, :], gmn[:, :, :], gab[:, :, :], ALU.subtract).then_inc(s["gates_abs"], 1)

                def gla_gates():
                    dve.wait_ge(s["gpre_ready"], l + 1)
                    chain.done(dve.tensor_scalar(gx[:, :], bank[0][:, 0:S], col(GLAB + l), None, ALU.add))
                    chain.wait()
                    chain.done(dve.tensor_scalar(gmn2[:, :], gx[:, :], 0.0, None, ALU.min))
                    chain.done(dve.tensor_scalar(gab2[:, :], gx[:, :], 0.0, None, ALU.max))
                    chain.wait()
                    dve.tensor_tensor(gab2[:, :], gmn2[:, :], gab2[:, :], ALU.subtract).then_inc(s["gla_abs"], 1)

                for p in range(N_IN):
                    if p + SPLIT < N_IN:
                        split_low(n0 + p + SPLIT, width=in_width(p + SPLIT))
                    src = bank[Z_BANKS[p % 4]]
                    if p == 1:
                        dve.wait_ge(s["z_act"], 9 * l + 1)
                        chain.wait()
                        ins = dve.tensor_tensor(glu[:, :, CONV - 1:], bank[Z_BANKS[0]][:, :].rearrange("p (c n) -> p c n", c=2),
                                                gsig[:, :, :], ALU.mult)
                        ins.then_inc(s["z_dve"], 1)
                        dve.wait_ge(s["z_dve"], 4 * l + 1)
                    if p in (2, 3):
                        dve.wait_ge(s["piece_used"], n0 + p + 1)
                        c = 2 * (p - 2)
                        dve.tensor_copy(qkpre[:, c:c + 2, MCONV - 1:], src[:, :].rearrange("p (c n) -> p c n", c=2)).then_inc(s["z_dve"], 1)
                    if p == 4:
                        dve.wait_ge(s["z_dve"], 4 * l + 3)
                        for i in range(4 * MCONV):
                            qk_step(i)
                        chain.wait()
                        dve.memset(tiny[:, :], 0.0).then_inc(s["qk_conv"], 1)
                    elif p >= 1:
                        conv_steps(8)
                    if p == 5:
                        mlstm_gates()
                    if p == 8:
                        gla_gates()
                    if p == 9:
                        dve.wait_ge(s["z_act"], 9 * l + 8)
                        dve.tensor_tensor(grs[:, :, :], src[:, :].rearrange("p (t n) -> p t n", t=TT),
                                          grs[:, :, :], ALU.mult).then_inc(s["z_dve"], 1)
                        dve.wait_ge(s["z_dve"], 4 * l + 4)
                dve.wait_ge(s["lat_rstd"], l + 1)
                for t in range(TT):
                    dve.tensor_scalar(zif[:, t, 8:200], zif[:, t, 8:200], lrs[:, 0, t:t + 1], None, ALU.mult)
                    last = dve.tensor_scalar(zkv[:, t, 0:128], zkv[:, t, 0:128], lrs[:, 1, t:t + 1], None, ALU.mult)
                last.then_inc(s["lat_ready"], 1)
                dve.wait_ge(s["gates_ln"], l + 1)
                dve.tensor_tensor(gb[:, :, 4:8], gmn[:, :, :], gln[:, :, :], ALU.subtract).then_inc(s["lf_ready"], 1)
                conv_steps(2 * CONV)
                dve.memset(tiny[:, :], 0.0).then_inc(s["conv_done"], 1)

                dve.wait_ge(s["piece_used"], n0 + N_IN)
                dve.wait_ge(s["lat_tr"], l + 1)
                dve.tensor_scalar(cqT[:, 0, :], bank[4][:, 0:S], col(QG1 + l), None, ALU.mult)
                dve.tensor_scalar(cqT[0:64, 1, :], bank[4][0:64, S:2 * S], cols[0:64, 0, QG2 + l:QG2 + l + 1], None, ALU.mult)
                dve.tensor_scalar(ckvT[:, :], bank[7][:, 0:S], col(KVG + l), None, ALU.mult).then_inc(s["lat_T"], 1)
                dve.wait_ge(s["gate_tr"], l + 1)
                chain.done(dve.tensor_tensor_scan(cumf[:, :], ones[0:4, :], bank[2][0:4, S:2 * S], 0.0, ALU.mult, ALU.add))
                chain.wait()
                chain.done(dve.tensor_tensor(aj[:, :], bank[2][0:4, 0:S], cumf[:, :], ALU.subtract))
                chain.wait()
                chain.done(dve.tensor_tensor_scan(mrun[:, :], aj[:, :], aj[:, :], 0.0, ALU.max, ALU.max))
                chain.wait()
                dve.tensor_scalar(negm[:, :], mrun[:, :], -1.0, None, ALU.mult)
                dve.tensor_tensor(mrun[:, :], mrun[:, :], cumf[:, :], ALU.add).then_inc(s["mcum_ready"], 1)
                dve.wait_ge(s["gla_ln"], l + 1)
                chain.done(dve.tensor_tensor(gmn2[:, :], gmn2[:, :], gab2[:, :], ALU.subtract))
                chain.wait()
                chain.done(dve.tensor_tensor_scan(b16[:, :], ones[:, :], gmn2[:, :], 0.0, ALU.mult, ALU.add))
                chain.wait()
                for i in range(2):
                    mid = b16[:, i * P + P // 2:i * P + P // 2 + 1]
                    dve.tensor_scalar(gref[:, 0, i:i + 1], mid, -1.0 / 16, None, ALU.mult)
                    last = dve.tensor_scalar(gref[:, 1, i:i + 1], mid, 1.0 / 16, None, ALU.mult)
                last.then_inc(s["gla_cum"], 1)
                dve.wait_ge(s["mcol_tr"], l + 1)
                dve.tensor_copy(mcol[:, :], bank[0][:, 0:16]).then_inc(s["mcol_ready"], 1)
                if l == 0:
                    dve.wait_ge(s["sin_ready"], 1)
                dve.wait_ge(s["qkv_evac"], l + 1)
                cos = bc(cossin[:, 0, :, :].unsqueeze(2), [P, TT, 5, 16])
                sin = bc(cossin[:, 1, :, :].unsqueeze(2), [P, TT, 5, 16])
                x1, x2 = rin[:, :, :, 0:16], rin[:, :, :, 16:32]
                for lo, (a, ca, b, cb, op) in ((0, (x1, cos, x2, sin, ALU.subtract)), (16, (x2, cos, x1, sin, ALU.add))):
                    chain.done(dve.tensor_tensor(rt1[:, :, :, :], a, ca, ALU.mult))
                    chain.done(dve.tensor_tensor(rt2[:, :, :, :], b, cb, ALU.mult))
                    chain.wait()
                    chain.done(dve.tensor_tensor(rot[:, :, :, lo:lo + 16], rt1[:, :, :, :], rt2[:, :, :, :], op))
                    chain.wait()
                for t in range(TT):
                    dve.tensor_copy(qtok[:, t, :, 64:96], rot[:, t, 0:4, :])
                    last = dve.tensor_copy(ktok[:, t, :, 64:96], bc(rot[:, t, 4:5, :], [P, HEADS, 32]))
                last.then_inc(s["rot_ready"], 1)
                for hd in (0, 1):
                    dve.wait_ge(s["dt_ready"], HEADS * l + hd + 1)
                    dve.wait_ge(s["s_ready"], HEADS * l + hd + 1)
                    dve.scalar_tensor_tensor(out=dec[:, hd, :], in0=bank[(1, 3)[hd % 2]][:, 0:384], scalar=DH ** -0.5,
                                             in1=dec[:, hd, :], op0=ALU.mult, op1=ALU.mult).then_inc(s["pt_ready"], 1)
                for i in range(2):
                    dve.wait_ge(s["qkT_tr"], 4 * l + 2 + i + 1)
                    dve.tensor_copy(kT[:, 2 * i:2 * i + 2, :], bank[(7, 0)[i]][0:96, :].rearrange("p (h n) -> p h n", h=2)).then_inc(s["kT_ready"], 1)
                dve.wait_ge(s["sc_ready"], l + 1)
                chain.done(dve.tensor_reduce(smax[:, 0, :], bank[6][:, :].rearrange("p (h n) -> p h n", h=HEADS), AX_X, ALU.max))
                for i in range(2):
                    chain.done(dve.tensor_reduce(smax[:, 1, 2 * i:2 * i + 2],
                                                 bank[(0, 5)[i]][:, :].rearrange("p (h n) -> p h n", h=2), AX_X, ALU.max))
                chain.wait()
                dve.tensor_scalar(smax[:, :, :], smax[:, :, :], -(96.0 ** -0.5), None, ALU.mult).then_inc(s["smax_ready"], 1)
                for hd in (2, 3):
                    dve.wait_ge(s["dt_ready"], HEADS * l + hd + 1)
                    dve.wait_ge(s["s_ready"], HEADS * l + hd + 1)
                    dve.scalar_tensor_tensor(out=dec[:, hd, :], in0=bank[(1, 3)[hd % 2]][:, 0:384], scalar=DH ** -0.5,
                                             in1=dec[:, hd, :], op0=ALU.mult, op1=ALU.mult).then_inc(s["pt_ready"], 1)
                dve.wait_ge(s["conf_tr"], l + 1)
                for t in range(TT):
                    chain.done(dve.bn_stats(bst[:, t, :], bank[7][:, t * 256:(t + 1) * 256]))
                chain.wait()
                for t in range(TT):
                    last = dve.bn_aggr(bag[:, t, :], bst[:, t, :])
                last.then_inc(s["bn_ready"], 1)
                for hd in range(HEADS):
                    dve.wait_ge(s["ga_ready"], HEADS * l + hd + 1)
                    dve.tensor_tensor(gS[:, hd, :, :], bank[(1, 3)[hd % 2]][:, 0:384].rearrange("p (b n) -> p b n", b=3),
                                      gla_mask[:, :, :], ALU.mult).then_inc(s["gs_ready"], 1)
                dve.wait_ge(s["conf_rstd"], l + 1)
                for t in range(TT):
                    last = dve.tensor_scalar(ctok[:, t, :], bank[7][:, t * 256:(t + 1) * 256], bag[:, t, 0:1],
                                             bst[:, t, 1:2], ALU.subtract, ALU.mult)
                last.then_inc(s["conf_n"], 1)
                dve.wait_ge(s["num_ready"], l + 1)
                den = lambda t: bank[(2, 4)[t]][:, 0:260].rearrange("p (h n) -> p h n", h=HEADS)[:, :, DH]
                for t in range(TT):
                    chain.done(dve.scalar_tensor_tensor(out=mden[:, t, :], in0=den(t), scalar=-1.0,
                                                        in1=mcol[:, 8 + 4 * t:12 + 4 * t], op0=ALU.mult, op1=ALU.max))
                chain.wait()
                for t in range(TT):
                    chain.done(dve.tensor_tensor(mden[:, t, :], den(t), mden[:, t, :], ALU.max))
                chain.wait()
                chain.done(dve.reciprocal(mden[:, :, :], mden[:, :, :]))
                chain.wait()
                for t in range(TT):
                    nb = bank[(2, 4)[t]][:, 0:260].rearrange("p (h n) -> p h n", h=HEADS)
                    chain.done(dve.tensor_tensor(y[:, t, 0:256].rearrange("p (h n) -> p h n", h=HEADS), nb[:, :, 0:DH],
                                                 bc(mden[:, t, :].unsqueeze(2), [P, HEADS, DH]), ALU.mult))
                chain.wait()
                dve.tensor_tensor(y[:, :, 0:256], y[:, :, 0:256],
                                  osig[:, :, :], ALU.mult).then_inc(s["y_m"], 1)
                dve.wait_ge(s["conf_sig"], l + 1)
                dve.tensor_tensor(y[:, :, 768:1024], ctok[:, :, :], cacc[:, :, :], ALU.mult).then_inc(s["y_c"], 1)
                split_low(n0 + N_IN)
                normalize_group(l, 0)
                normalize_group(l, 1)
                dve.wait_ge(s["osq_ready"], l + 1)
                dve.tensor_reduce(gss[:, :, :], osq[:, :, :, :], AX_X, ALU.add).then_inc(s["gss_ready"], 1)
                dve.wait_ge(s["grd_ready"], l + 1)
                chain.done(dve.tensor_tensor(osq[:, :, :, :], bank[7][:, :].rearrange("p (t h n) -> p t h n", t=TT, h=HEADS),
                                             bc(grd[:, :, :].unsqueeze(3), [P, TT, HEADS, DH]), ALU.mult))
                chain.wait()
                dve.tensor_tensor(y[:, :, 512:768], osq[:, :, :, :].rearrange("p t h n -> p t (h n)"), grs[:, :, :],
                                  ALU.mult).then_inc(s["y_g"], 1)
                for at in (0, 1):
                    gains_of(3 * l + 1, FUSE + KD * l, at, FUSE_ORDER[at], FUSE_BANKS[at])
                normalize_group(l, 2)
                dve.wait_ge(s["pv_ready"], l + 1)
                chain.done(dve.reciprocal(psums[:, :, :], psums[:, :, :]))
                chain.wait()
                dve.tensor_tensor(y[:, :, 256:512].rearrange("p t (h n) -> p t h n", h=HEADS),
                                  bank[0][:, :].rearrange("p (t h n) -> p t h n", t=TT, h=HEADS),
                                  bc(psums[:, :, :].unsqueeze(3), [P, TT, HEADS, DH]), ALU.mult).then_inc(s["y_a"], 1)
                split_low(n0 + N_IN + 1)

                gains_of(3 * l + 1, FUSE + KD * l, 2, FUSE_ORDER[2], FUSE_BANKS[2])
                normalize_group(l, 3)
                split_low(n0 + N_IN + 2)
                gains_of(3 * l + 1, FUSE + KD * l, 3, FUSE_ORDER[3], FUSE_BANKS[3])
                split_low(n0 + N_IN + 3)
                split_low(n0 + N_IN + N_OUT)
                add_to_h(OUT_BANKS, s["piece_used"], [n0 + N_IN + N_OUT] * 4)
                if l == 0:
                    gains(3 * l + 2, NORM2 + KD * l, NORM2_BANKS)
                    split_low(DENSE0 + 1)
                    dve.wait_ge(s["rstd_ready"], 2)
                    ffn(DENSE0, None, 0, TT, scale=rstd, start=2)
                    add_to_h((2, 3, 5, 6), s["piece_used"], [DENSE0 + N_FFN] * 4)

            for g in (2, 3):
                dve.wait_ge(s["norm_tr"], 4 * 5 + g + 1)
                for i in range(2):
                    kd = 2 * g + i
                    last = dve.tensor_scalar(u32[:, kd, :], bank[NORM2_BANKS[g]][:, i * S:(i + 1) * S], col(NORM2 + KD + kd),
                                             None, ALU.mult)
                last.then_inc(s["u32_dve"], 1)
            split_low(MOE0 + 1)
            dve.wait_ge(s["moe_g_in"], 16)
            dve.wait_ge(s["rstd_ready"], 4)
            for t in range(TT):
                dve.scalar_tensor_tensor(out=un[:, t, :], in0=h[:, t, :], scalar=rstd[:, t, 0:1], in1=moe_g[:, :],
                                         op0=ALU.mult, op1=ALU.mult).then_inc(s["ung_ready"], 1)
            dve.wait_ge(s["logit_ready"], 1)
            for t in range(TT):
                chain.done(dve.tensor_scalar(logits[:, t, :], bank[2][:, t * E:(t + 1) * E], rstd[:, t, 0:1], None, ALU.mult))
            chain.wait()
            for t in range(TT):
                chain.done(dve.max(top8[:, t, :], logits[:, t, :]))
            chain.wait()
            for t in range(TT):
                chain.done(dve.max_index(idx8[:, t, :], top8[:, t, :], logits[:, t, :]))
            dve.tensor_tensor(gap[:, :], top8[:, :, 1], top8[:, :, 0], ALU.subtract).then_inc(s["gap_ready"], 1)
            chain.wait()
            chain.done(dve.tensor_copy(idf[:, :, :], idx8[:, :, :]))
            chain.wait()
            for t in range(TT):
                chain.done(dve.tensor_scalar(oh1[:, t, :], iota[:, 0:E], idf[:, t, 0:1], None, ALU.is_equal))
                chain.done(dve.tensor_scalar(oh2[:, t, :], iota[:, 0:E], idf[:, t, 1:2], None, ALU.is_equal))
            chain.wait()
            dve.tensor_tensor(routed[:, :, :], oh1[:, :, :], oh2[:, :, :], ALU.add).then_inc(s["routed_ready"], 1)
            for t in range(TT):
                dve.wait_ge(s["unh_ready"], t + 1)
                last = dve.tensor_tensor(unl[:, t, :], un[:, t, :], unh[:, t, :].bitcast(F32), ALU.subtract)
            last.then_inc(s["unl_ready"], 1)
            split_low(MOE0 + 2)
            dve.wait_ge(s["rank_ready"], 1)
            for t in range(TT):
                chain.done(dve.scalar_tensor_tensor(out=rank1[:, t, :], in0=bank[3][:, t * E:(t + 1) * E], scalar=1.0,
                                                    in1=routed[:, t, :], op0=ALU.add, op1=ALU.mult))
            chain.wait()
            chain.done(dve.tensor_scalar(keys[:, :, 0:E], rank1[:, :, :], -1.0, None, ALU.add))
            chain.wait()

            def route_weights():
                dve.tensor_scalar(over[:, :], bank[3][:, TT * E:(TT + 1) * E], float(P), None, ALU.is_gt).then_inc(s["over_ready"], 1)
                dve.wait_ge(s["over_ready"], 1)
                dve.wait_ge(s["egap_ready"], 1)
                chain.done(dve.tensor_scalar(w1[:, :], egap[:, :], 1.0, None, ALU.add))
                chain.wait()
                chain.done(dve.reciprocal(w1[:, :], w1[:, :]))
                chain.wait()
                chain.done(dve.tensor_tensor(w2[:, :], w1[:, :], egap[:, :], ALU.mult))
                chain.wait()
                for t in range(TT):
                    chain.done(dve.tensor_scalar(wts[:, t, 0:E], oh2[:, t, :], w2[:, t:t + 1], None, ALU.mult))
                chain.wait()
                for t in range(TT):
                    chain.done(dve.scalar_tensor_tensor(out=wts[:, t, 0:E], in0=oh1[:, t, :], scalar=w1[:, t:t + 1],
                                                        in1=wts[:, t, 0:E], op0=ALU.mult, op1=ALU.add))
                chain.wait()

            def route_overflow():
                chain.done(dve.tensor_tensor_scan(over_n[:, :], ones[:, 0:E], over[:, :], 0.0, ALU.mult, ALU.add))
                chain.done(dve.tensor_reduce(jobs_f[:, 3:4], over[:, :], AX_X, ALU.add))
                chain.wait()
                for o in range(OVER):
                    chain.done(dve.scalar_tensor_tensor(out=over_oh[:, o, :], in0=over_n[:, :], scalar=float(o + 1),
                                                        in1=over[:, :], op0=ALU.is_equal, op1=ALU.mult))
                chain.wait()
                for o in range(OVER):
                    oh = bc(over_oh[:, o:o + 1, :], [P, TT, E])
                    chain.done(dve.tensor_tensor(pick[:, :, :], rank1[:, :, :], oh, ALU.mult))
                    chain.wait()
                    chain.done(dve.tensor_reduce(keys[:, :, E + o], pick[:, :, :], AX_X, ALU.add))
                    chain.wait()
                    chain.done(dve.tensor_tensor(pick[:, :, :], wts[:, :, 0:E], oh, ALU.mult))
                    chain.wait()
                    chain.done(dve.tensor_reduce(wts[:, :, E + o], pick[:, :, :], AX_X, ALU.add))
                    chain.wait()
                    chain.done(dve.tensor_tensor(pick[:, 0, :], over_oh[:, o, :], iota[:, 0:E], ALU.mult))
                    chain.wait()
                    chain.done(dve.tensor_reduce(jobs_f[:, o:o + 1], pick[:, 0, :], AX_X, ALU.add))
                    chain.wait()
                dve.memset(keys[:, :, JOBS:JOBS + 1], -1.0)
                chain.done(dve.tensor_scalar(keys[:, :, E:JOBS], keys[:, :, E:JOBS], -float(P + 1), None, ALU.add))
                chain.wait()
                dve.tensor_copy(jobs_i[:, :], jobs_f[:, :]).then_inc(s["jobs_ready"], 1)

            def column(n):
                return slice(n, n + 1) if isinstance(n, int) else bass.ds(n, 1)

            def select(n):
                dve.tensor_copy(keycol[:, :], keys[:, :, column(n)].rearrange("p t a -> p (t a)")).then_inc(s["key_copied"], 1)
                dve.wait_ge(s["key_copied"], n + 1)
                for t in range(TT):
                    last = dve.tensor_scalar(sel[:, t, :], iota[:, :], keycol[:, t:t + 1], None, ALU.is_equal)
                last.then_inc(s["sel_ready"], 1)

            def tokens_out(n):
                dve.wait_ge(s["gath_ready"], n + 1)
                dve.tensor_copy(xs[:, 4:8, :], bank[6][:, :].rearrange("p (k n) -> p k n", k=4)).then_inc(s["xs_dve"], 1)

            def tokens_low(n):
                dve.wait_ge(s["xh_ready"], n + 1)
                for i in range(2):
                    last = dve.tensor_tensor(xl[:, 4 * i:4 * i + 4, :], bank[5 + i][:, :].rearrange("p (k n) -> p k n", k=4),
                                             xh[:, 4 * i:4 * i + 4, :].bitcast(F32), ALU.subtract)
                last.then_inc(s["xl_ready"], 1)

            def result_low(n):
                dve.wait_ge(s["yh_ready"], n)
                for i in range(2):
                    last = dve.scalar_tensor_tensor(out=yl[:, i * 512:(i + 1) * 512], in0=bank[2 + i][:, :], scalar=wslot[:, :],
                                                    in1=yh[:, i * 512:(i + 1) * 512].bitcast(F32), op0=ALU.mult, op1=ALU.subtract)
                last.then_inc(s["yl_ready"], 1)

            def add_result(n, t):
                for half in range(2):
                    i = 2 * t + half
                    dve.wait_ge(s["scat_ready"], 4 * n - (3 - i))
                    dst = h[:, t, half * 512:(half + 1) * 512]
                    last = dve.tensor_tensor(dst, bank[SCATTER_BANKS[i]][:, :], dst, ALU.add).then_inc(s["added"], 1)

            def job(j, first):
                def weights():
                    if not first:
                        dve.wait_ge(s["selT_tr"], j)
                    dve.tensor_copy(wcol[:, :], wts[:, :, column(j)].rearrange("p t a -> p (t a)")).then_inc(s["wcol_ready"], 1)

                def next_select():
                    dve.wait_ge(s["selT_tr"], j + 1)
                    select(j + 1)

                def chunk0():
                    weights()
                    if not first:
                        add_result(j, 0)

                def chunk1():
                    if first:
                        route_overflow()
                    else:
                        add_result(j, 1)

                ffn(MOE0, j, j + 1, 1, {} if first else {1: lambda: result_low(j)},
                    {0: chunk0, 1: chunk1, SELECT_AT: next_select, GATHER_AT: lambda: tokens_out(j + 1)},
                    after_last=lambda: tokens_low(j + 1), start=SPLIT if first else 0)

            select(0)
            route_weights()
            tokens_out(0)
            tokens_low(0)
            n_jobs = jobs(dve, job)
            result_low(n_jobs)
            for t in range(TT):
                add_result(n_jobs, t)
                dve.wait_ge(s["added"], 4 * n_jobs - (2 - 2 * t))
                dve.memset(tiny[:, :], 0.0).then_inc(s["h_ready"], 1)
            dve.wait_ge(s["rstd_ready"], 5)
            dve.wait_ge(s["final_in"], 16)
            for t in range(TT):
                dve.scalar_tensor_tensor(out=h[:, t, :], in0=h[:, t, :], scalar=rstd[:, t, 0:1], in1=fin_g,
                                         op0=ALU.mult, op1=ALU.mult).then_inc(s["out_ready"], 1)

        @block.tensor
        def _(pe):
            owner = {}

            def claim(b, sem, value):
                if b in owner:
                    pe.wait_ge(*owner[b])
                owner[b] = (s[sem], value)

            def norm_transposes(source, ready, readers, banks=NORM_BANKS):
                sem, values = ready
                for g in range(4):
                    claim(banks[g], *readers[g])
                for t in range(TT):
                    pe.wait_ge(s[sem], values[t])
                    for g in range(4):
                        for i in range(2):
                            last = pe.transpose(bank[banks[g]][:, i * S + t * P:i * S + (t + 1) * P],
                                                source[:, t, (2 * g + i) * P:(2 * g + i + 1) * P], ident[:, :])
                        if t == TT - 1:
                            last.then_inc(s["norm_tr"], 1)

            def fuse_transposes(l, at):
                g, b = FUSE_ORDER[at], FUSE_BANKS[at]
                pe.wait_ge(s["group_ready"], 4 * l + at + 1)
                claim(b, "utl_ready", 4 * (3 * l + 1) + at + 1)
                for i in range(2):
                    for t in range(TT):
                        last = pe.transpose(bank[b][:, i * S + t * P:i * S + (t + 1) * P],
                                            y[:, t, (2 * g + i) * P:(2 * g + i + 1) * P], ident[:, :])
                last.then_inc(s["norm_tr"], 1)

            def split_readers(n):
                return [("utl_ready", 4 * n + g + 1) for g in range(4)]

            def product(dst, terms):
                for i, ((ah, al), (bh, bl)) in enumerate(terms):
                    first, final = i == 0, i == len(terms) - 1
                    pe.matmul(dst, ah, bh, start=first, stop=False)
                    pe.matmul(dst, ah, bl, start=False, stop=False)
                    last = pe.matmul(dst, al, bh, start=False, stop=final)
                return last

            def part(n, lo, hi):
                return high[:, n % SPLIT, lo:hi], low[:, n % SPLIT, lo:hi]

            def uT(k, lo, hi):
                return uTh[:, k, lo:hi], uTl[:, k, lo:hi]

            def ffn(n0, job, job_n, tiles, xT, accs, first_claims, after_products={}):
                pieces = N_FFN * job if job is not None else 0
                at = lambda c: job_n * CHUNKS + c

                def down(c):
                    n = n0 + FFN_AT[("d", c)]
                    pe.wait_ge(s["hTl_ready"], at(c + 1))
                    pe.wait_ge(s["low_ready"], pieces + (n + 1))
                    for f in range(2):
                        for t in range(tiles):
                            for half in range(2):
                                o = bank[accs[t][half]][:, :]
                                ah, al = hTh[:, f, t, :], hTl[:, f, t, :]
                                bh, bl = part(n, f * 1024 + half * 512, f * 1024 + half * 512 + 512)
                                pe.matmul(o, ah, bh, start=(c == 0 and f == 0), stop=False)
                                pe.matmul(o, ah, bl, start=False, stop=False)
                                last = pe.matmul(o, al, bh, start=False, stop=(c == CHUNKS - 1 and f == 1))
                    last.then_inc(s["piece_used"], 1)
                    return last

                for c in range(CHUNKS):
                    if c:
                        pe.wait_ge(s["hid_ready"], at(c))
                    else:
                        first_claims()
                    for kh, kind in enumerate("ab"):
                        n = n0 + FFN_AT[(kind, c)]
                        pe.wait_ge(s["low_ready"], pieces + (n + 1))
                        if job is None and c == 0:
                            pe.wait_ge(s["utl_ready"], 4 * 2 + 2 * (kh + 1))
                        for t in range(tiles):
                            for k in range(4):
                                kd = 4 * kh + k
                                ah, al = xT(kd, t)
                                bh, bl = part(n, k * 512, (k + 1) * 512)
                                o = bank[t][:, :]
                                pe.matmul(o, ah, bh, start=(kd == 0), stop=False)
                                pe.matmul(o, ah, bl, start=False, stop=False)
                                last = pe.matmul(o, al, bh, start=False, stop=(kd == KD - 1))
                        last.then_inc(s["piece_used"], 1)
                    if c:
                        down(c - 1)
                        pe.wait_ge(s["hTl_ready"], at(c))
                    after_products.get(c, lambda: None)()
                    pe.wait_ge(s["hid_ready"], at(c + 1))
                    for f in range(2):
                        for t in range(tiles):
                            o = (f * tiles + t) * P
                            last = pe.transpose(bank[4][:, o:o + P], hid[:, t, f * P:(f + 1) * P], ident[:, :])
                    last.then_inc(s["hid_tr"], 1)
                down(CHUNKS - 1)

            pe.wait_ge(s["consts"], 1)
            pe.wait_ge(s["norm1_in"], 16)
            claim(7, "cols_ready", 1)
            pe.transpose(bank[7][:, 0:P], stage[:, 2, :], ident[:, :]).then_inc(s["cols_tr"], 1)

            for l in range(DEPTH):
                n0 = LAYER_PIECES[l]
                norm_transposes(un, ("un_ready", [2 * l + 1, 2 * l + 2]), split_readers(3 * l))
                if l == 0:
                    pe.wait_ge(s["rows_in"], 16 * 10)
                    claim(3, "cols_ready", 2)
                    pe.transpose(bank[3][:, 0:P], stage[:, 0, :], ident[:, :])
                    pe.transpose(bank[3][:, P:2 * P], stage[:, 1, :], ident[:, :]).then_inc(s["cols_tr"], 1)
                pe.wait_ge(s["utl_ready"], 4 * (3 * l + 1))
                act_reads = {1: 1, 4: 2, 5: 3, 6: 5, 7: 6, 8: 7, 10: 9}
                dve_reads = {0: 1, 2: 2, 3: 3, 9: 4}
                for p in range(N_IN):
                    n = n0 + p
                    w = sum(v for _, v in W_IN_PIECES[p])
                    pe.wait_ge(s["low_ready"], n + 1)
                    b = Z_BANKS[p % 4]
                    claim(b, *(("z_act", 9 * l + act_reads[p]) if p in act_reads else ("z_dve", 4 * l + dve_reads[p])))
                    if p in FEATURE_MAJOR:
                        for c in range(2):
                            last = product(bank[b][:, c * S:(c + 1) * S],
                                           [(part(n, k * w + c * P, k * w + (c + 1) * P), uT(k, 0, S)) for k in range(KD)])
                    else:
                        for t in range(TT):
                            last = product(bank[b][:, t * w:(t + 1) * w],
                                           [(uT(k, t * P, (t + 1) * P), part(n, k * w, (k + 1) * w)) for k in range(KD)])
                    last.then_inc(s["piece_used"], 1)
                    if p == 6:
                        pe.wait_ge(s["z_act"], 9 * l + 3)
                        claim(7, "z_act", 9 * l + 4)
                        for t in range(TT):
                            last = pe.transpose(bank[7][0:16, t * P:(t + 1) * P], zkv[:, t, 160:176], ident[:, :])
                        last.then_inc(s["aT_tr"], 1)
                    if p == 7:
                        pe.wait_ge(s["ukv_in"], 64 * (l + 1))
                        claim(0, "gla_abs", l + 1)
                        pe.wait_ge(s["z_act"], 9 * l + 4)
                        pe.matmul(bank[0][:, 0:S], walpha[:, :], aT[:, :], start=True, stop=True).then_inc(s["gpre_ready"], 1)

                pe.wait_ge(s["lat_ready"], l + 1)
                claim(4, "lat_T", l + 1)
                claim(7, "lat_T", l + 1)
                for t in range(TT):
                    pe.transpose(bank[4][:, t * P:(t + 1) * P], zif[:, t, 8:136], ident[:, :])
                    pe.transpose(bank[4][0:64, S + t * P:S + (t + 1) * P], zif[:, t, 136:200], ident[:, :])
                    last = pe.transpose(bank[7][:, t * P:(t + 1) * P], zkv[:, t, 0:P], ident[:, :])
                last.then_inc(s["lat_tr"], 1)
                pe.wait_ge(s["lf_ready"], l + 1)
                claim(2, "mcum_ready", l + 1)
                for t in range(TT):
                    pe.transpose(bank[2][0:4, t * P:(t + 1) * P], gb[:, t, 0:4], ident[:, :])
                    last = pe.transpose(bank[2][0:4, S + t * P:S + (t + 1) * P], gb[:, t, 4:8], ident[:, :])
                last.then_inc(s["gate_tr"], 1)
                pe.wait_ge(s["lat_T"], l + 1)
                for t in range(TT):
                    b = (3, 5)[t]
                    claim(b, "qkv_evac", l + 1)
                    pe.matmul(bank[b][:, 0:384], cqT[:, 0, t * P:(t + 1) * P], uq[:, 0, :], start=True, stop=False)
                    last = pe.matmul(bank[b][:, 0:384], cqT[0:64, 1, t * P:(t + 1) * P], uq[0:64, 1, :], start=False, stop=True)
                last.then_inc(s["q_ready"], 1)
                for t in range(TT):
                    b = (6, 1)[t]
                    claim(b, "qkv_evac", l + 1)
                    last = pe.matmul(bank[b][:, :], ckvT[:, t * P:(t + 1) * P], ukv[:, :], start=True, stop=True)
                last.then_inc(s["kv_ready"], 1)
                pe.wait_ge(s["expnm_ready"], l + 1)
                claim(0, "mcol_ready", l + 1)
                for t in range(TT):
                    pe.transpose(bank[0][:, 4 * t:4 * t + 4], aj[:, t * P:(t + 1) * P], ident[0:4, 0:4])
                    last = pe.transpose(bank[0][:, 8 + 4 * t:12 + 4 * t], expnm[:, t * P:(t + 1) * P], ident[0:4, 0:4])
                last.then_inc(s["mcol_tr"], 1)
                pe.wait_ge(s["qk_ready"], l + 1)
                for hd in (0, 1):
                    b = (2, 4)[hd % 2]
                    claim(b, "dt_ready", HEADS * l + hd + 1)
                    row = bc(ident[0:4, hd:hd + 1], [4, P])
                    pe.matmul(bank[b][:, 0:S], row, negm[:, :], start=True, stop=False)
                    pe.matmul(bank[b][:, 0:P], ident[:, :], mask_kt[:, :], start=False, stop=True)
                    pe.matmul(bank[b][:, S:S + P], row, negm[:, P:S], start=True, stop=False)
                    pe.matmul(bank[b][:, S:S + P], ident[:, :], mask_kt[:, :], start=False, stop=True).then_inc(s["x_ready"], 1)
                    b = (1, 3)[hd % 2]
                    claim(b, "pt_ready", HEADS * l + hd + 1)
                    r = slice(64 * (hd % 2), 64 * (hd % 2) + 64)
                    q, k = qkc[r, hd // 2, :], qkc[r, 2 + hd // 2, :]
                    pe.matmul(bank[b][:, 0:S], k[:, 0:P], q, start=True, stop=True)
                    pe.matmul(bank[b][:, S:S + P], k[:, P:S], q[:, P:S], start=True, stop=True).then_inc(s["s_ready"], 1)
                pe.wait_ge(s["rot_ready"], l + 1)
                for i, (b, src, sem, v) in enumerate(((2, qtok, "qT_ready", 1), (4, qtok, "qT_ready", 2),
                                                      (7, ktok, "kT_ready", 1), (0, ktok, "kT_ready", 2))):
                    claim(b, sem, 2 * l + v)
                    for a in range(2):
                        for t in range(TT):
                            last = pe.transpose(bank[b][0:96, a * S + t * P:a * S + (t + 1) * P],
                                                src[:, t, 2 * (i % 2) + a, :], ident[:, :])
                    last.then_inc(s["qkT_tr"], 1)
                pe.wait_ge(s["qT_ready"], 2 * (l + 1))
                pe.wait_ge(s["kT_ready"], 2 * (l + 1))
                for hd in range(HEADS):
                    if hd == 0:
                        claim(6, "p_ready", l + 1)
                    o = bank[6][:, hd * P:(hd + 1) * P]
                    pe.matmul(o, qT[:, hd, 0:P], kT[:, hd, 0:P], start=True, stop=False)
                    pe.matmul(o, ident[:, :], mask_qt[:, :], start=False, stop=True)
                for hd in range(HEADS):
                    b = (0, 5)[hd // 2]
                    if hd % 2 == 0:
                        claim(b, "p_ready", l + 1)
                    o = bank[b][:, (hd % 2) * S:(hd % 2 + 1) * S]
                    pe.matmul(o, qT[:, hd, P:S], kT[:, hd, :], start=True, stop=False)
                    last = pe.matmul(o[:, P:S], ident[:, :], mask_qt[:, :], start=False, stop=True)
                last.then_inc(s["sc_ready"], 1)
                for hd in (2, 3):
                    b = (2, 4)[hd % 2]
                    claim(b, "dt_ready", HEADS * l + hd + 1)
                    row = bc(ident[0:4, hd:hd + 1], [4, P])
                    pe.matmul(bank[b][:, 0:S], row, negm[:, :], start=True, stop=False)
                    pe.matmul(bank[b][:, 0:P], ident[:, :], mask_kt[:, :], start=False, stop=True)
                    pe.matmul(bank[b][:, S:S + P], row, negm[:, P:S], start=True, stop=False)
                    pe.matmul(bank[b][:, S:S + P], ident[:, :], mask_kt[:, :], start=False, stop=True).then_inc(s["x_ready"], 1)
                    b = (1, 3)[hd % 2]
                    claim(b, "pt_ready", HEADS * l + hd + 1)
                    r = slice(64 * (hd % 2), 64 * (hd % 2) + 64)
                    q, k = qkc[r, hd // 2, :], qkc[r, 2 + hd // 2, :]
                    pe.matmul(bank[b][:, 0:S], k[:, 0:P], q, start=True, stop=True)
                    pe.matmul(bank[b][:, S:S + P], k[:, P:S], q[:, P:S], start=True, stop=True).then_inc(s["s_ready"], 1)
                pe.wait_ge(s["conv_done"], l + 1)
                claim(7, "conf_n", l + 1)
                for t in range(TT):
                    for c in range(2):
                        last = pe.transpose(bank[7][:, t * 256 + c * P:t * 256 + (c + 1) * P],
                                            cacc[:, c, t * P:(t + 1) * P], ident[:, :])
                last.then_inc(s["conf_tr"], 1)
                pe.wait_ge(s["gla_qk"], l + 1)
                for hd in range(HEADS):
                    b = (1, 3)[hd % 2]
                    claim(b, "gs_ready", HEADS * l + hd + 1)
                    r = slice(32 * hd, 32 * hd + 32)
                    for i, (k, q) in enumerate(((2, 0), (3, 1), (4, 1))):
                        last = pe.matmul(bank[b][:, i * P:(i + 1) * P], gE[r, k, :], gE[r, q, :], start=True, stop=True,
                                         tile_position=(32 * hd, 0))
                    last.then_inc(s["ga_ready"], 1)
                for hd in range(HEADS):
                    pe.wait_ge(s["pt_ready"], HEADS * l + hd + 1)
                    for t in range(TT):
                        b = (2, 4)[t]
                        if hd == 0:
                            claim(b, "y_m", l + 1)
                        o = bank[b][:, hd * 65:(hd + 1) * 65]
                        if t == 0:
                            last = pe.matmul(o, dec[:, hd, 0:P], vaug[:, 0, hd, :], start=True, stop=True)
                        else:
                            pe.matmul(o, dec[:, hd, P:S], vaug[:, 0, hd, :], start=True, stop=False)
                            last = pe.matmul(o, dec[:, hd, S:S + P], vaug[:, 1, hd, :], start=False, stop=True)
                last.then_inc(s["num_ready"], 1)
                pe.wait_ge(s["p_ready"], l + 1)
                for i, b in enumerate((3, 5, 6)):
                    claim(b, "pT_ready", 3 * l + i + 1)
                    for hd in range(HEADS):
                        src = probs[:, hd * P:(hd + 1) * P] if i == 0 else \
                            probs[:, 512 + hd * S + (i - 1) * P:512 + hd * S + i * P]
                        last = pe.transpose(bank[b][:, hd * P:(hd + 1) * P], src, ident[:, :])
                    last.then_inc(s["p_tr"], 1)
                for hd in range(HEADS):
                    pe.wait_ge(s["gs_ready"], HEADS * l + hd + 1)
                    if hd == HEADS - 1:
                        break
                claim(7, "y_g", l + 1)
                for t in range(TT):
                    for hd in range(HEADS):
                        o = bank[7][:, t * 256 + hd * DH:t * 256 + (hd + 1) * DH]
                        v = gv[:, :, hd * DH:(hd + 1) * DH]
                        if t == 0:
                            last = pe.matmul(o, gS[:, hd, 0, :], v[:, 0, :], start=True, stop=True)
                        else:
                            pe.matmul(o, gS[:, hd, 1, :], v[:, 0, :], start=True, stop=False)
                            last = pe.matmul(o, gS[:, hd, 2, :], v[:, 1, :], start=False, stop=True)
                last.then_inc(s["go_ready"], 1)
                fuse_transposes(l, 0)
                fuse_transposes(l, 1)
                pe.wait_ge(s["pT_ready"], 3 * (l + 1))
                claim(0, "y_a", l + 1)
                for t in range(TT):
                    for hd in range(HEADS):
                        o = bank[0][:, t * 256 + hd * DH:t * 256 + (hd + 1) * DH]
                        v = vm[:, :, hd * DH:(hd + 1) * DH]
                        if t == 0:
                            last = pe.matmul(o, probT[:, 0, hd, :], v[:, 0, :], start=True, stop=True)
                        else:
                            pe.matmul(o, probT[:, 1, hd, :], v[:, 0, :], start=True, stop=False)
                            last = pe.matmul(o, probT[:, 2, hd, :], v[:, 1, :], start=False, stop=True)
                last.then_inc(s["pv_ready"], 1)

                fuse_transposes(l, 2)
                for i, b in enumerate(OUT_BANKS):
                    claim(b, "h_ready", 4 * l + 1 + i // 2)
                for at in range(N_OUT):
                    n = n0 + N_IN + at
                    pe.wait_ge(s["utl_ready"], 4 * (3 * l + 1) + at + 1)
                    pe.wait_ge(s["low_ready"], n + 1)
                    for i, b in enumerate(OUT_BANKS):
                        t, half = divmod(i, 2)
                        for k in range(2):
                            (ah, al), (bh, bl) = uT(2 * FUSE_ORDER[at] + k, t * P, (t + 1) * P), part(n, k * D + half * 512, k * D + (half + 1) * 512)
                            pe.matmul(bank[b][:, :], ah, bh, start=(at == 0 and k == 0), stop=False)
                            pe.matmul(bank[b][:, :], ah, bl, start=False, stop=False)
                            last = pe.matmul(bank[b][:, :], al, bh, start=False, stop=(at == N_OUT - 1 and k == 1))
                    last.then_inc(s["piece_used"], 1)
                    if at == 1:
                        fuse_transposes(l, 3)
                norm_transposes(h, ("h_ready", [4 * l + 1, 4 * l + 2]),
                                [("u32_act", 1), ("u32_act", 2), ("u32_dve", 1), ("u32_dve", 2)] if l else split_readers(3 * l + 2),
                                NORM2_BANKS)
                if l == 0:
                    def dense_claims():
                        for b, v in ((0, ("hid_ready", CHUNKS)), (1, ("hid_ready", CHUNKS)), (4, ("hTl_ready", CHUNKS)),
                                     (2, ("h_ready", 3)), (3, ("h_ready", 3)), (5, ("h_ready", 4)), (6, ("h_ready", 4))):
                            claim(b, *v)
                    ffn(DENSE0, None, 0, TT, lambda kd, t: uT(kd, t * P, (t + 1) * P), ((2, 3), (5, 6)), dense_claims)

            pe.wait_ge(s["router_in"], 16)
            pe.wait_ge(s["u32_act"], 2)
            pe.wait_ge(s["u32_dve"], 2)
            claim(2, "routed_ready", 1)
            for t in range(TT):
                for k in range(KD):
                    last = pe.matmul(bank[2][:, t * E:(t + 1) * E], u32[:, k, t * P:(t + 1) * P], router[:, k, :],
                                     start=(k == 0), stop=(k == KD - 1))
            last.then_inc(s["logit_ready"], 1)
            pe.wait_ge(s["routed_ready"], 1)
            claim(3, "over_ready", 1)
            pe.matmul(bank[3][:, 0:E], before[:, :], routed[:, 0, :], start=True, stop=True)
            pe.matmul(bank[3][:, E:2 * E], ones[:, 0:P], routed[:, 0, :], start=True, stop=False)
            pe.matmul(bank[3][:, E:2 * E], before[:, :], routed[:, 1, :], start=False, stop=True)
            pe.matmul(bank[3][:, 2 * E:3 * E], ones[:, 0:P], routed[:, 0, :], start=True, stop=False)
            pe.matmul(bank[3][:, 2 * E:3 * E], ones[:, 0:P], routed[:, 1, :], start=False, stop=True).then_inc(s["rank_ready"], 1)
            pe.wait_ge(s["unl_ready"], 1)
            pe.wait_ge(*owner[5])
            pe.wait_ge(*owner[6])

            def gather(n):
                pe.wait_ge(s["sel_ready"], n + 1)
                for half in range(2):
                    for t in range(TT):
                        for i, a in enumerate((unh, unl)):
                            last = pe.matmul(bank[5 + half][:, :], sel[:, t, :], a[:, t, half * 512:(half + 1) * 512],
                                             start=(t == 0 and i == 0), stop=(t == TT - 1 and i == 1))
                last.then_inc(s["gath_ready"], 1)

            def gathered_transposes(n):
                pe.wait_ge(s["xs_act"], n + 1)
                pe.wait_ge(s["xs_dve"], n + 1)
                for kd in range(KD):
                    last = pe.transpose(bank[5 + kd // 4][:, (kd % 4) * P:(kd % 4 + 1) * P], xs[:, kd, :], ident[:, :])
                last.then_inc(s["xT_tr"], 1)

            def scatter(n):
                pe.wait_ge(s["selT_ready"], n)
                pe.wait_ge(s["yl_ready"], n)
                for i, b in enumerate(SCATTER_BANKS):
                    t, half = divmod(i, 2)
                    pe.matmul(bank[b][:, :], selT[:, t, :], yh[:, half * 512:(half + 1) * 512], start=True, stop=False)
                    pe.matmul(bank[b][:, :], selT[:, t, :], yl[:, half * 512:(half + 1) * 512], start=False, stop=True).then_inc(s["scat_ready"], 1)

            def job(j, first):
                def slots():
                    if not first:
                        pe.wait_ge(s["added"], 4 * j)
                    pe.wait_ge(s["wcol_ready"], j + 1)
                    for t in range(TT):
                        pe.transpose(bank[7][:, t * P:(t + 1) * P], sel[:, t, :].bitcast(F32), ident[:, :])
                    for t in range(TT):
                        last = pe.matmul(bank[7][:, 2 * P:2 * P + 1], sel[:, t, :].bitcast(F32), wcol[:, t:t + 1],
                                         start=(t == 0), stop=(t == TT - 1))
                    last.then_inc(s["selT_tr"], 1)

                pe.wait_ge(s["xl_ready"], j + 1)
                work = {SLOTS_AT: slots, GATHER_AT: lambda: gather(j + 1),
                        GATHER_AT + 2: lambda: gathered_transposes(j + 1)}
                if not first:
                    work[0] = lambda: scatter(j)
                ffn(MOE0, j, j + 1, 1, lambda kd, t: (xh[:, kd, :], xl[:, kd, :]), ((2, 3),), lambda: None, work)

            gather(0)
            gathered_transposes(0)
            for b in (0, 1, 2, 3, 4, 7):
                pe.wait_ge(*owner[b])
            n_jobs = jobs(pe, job)
            scatter(n_jobs)


_INS = ['x', 'positions', 'norm1_g', 'w_in', 'mlstm_conv_w', 'mlstm_conv_b', 'mlstm_gate_b', 'mla_q_norm_g',
        'mla_w_uq', 'mla_kv_norm_g', 'mla_w_ukv', 'gla_w_alpha', 'gla_b_alpha', 'conv_w', 'conv_b', 'conv_ln_g',
        'conv_ln_b', 'fuse_g', 'w_out', 'norm2_g', 'ffn_w_gate', 'ffn_w_up', 'ffn_w_down', 'moe_router',
        'moe_w_gate', 'moe_w_up', 'moe_w_down', 'final_norm_g']


def kernel(**inputs):
    import numpy as _np
    import concourse.bacc as _bacc
    from concourse import mybir as _mybir
    from concourse.bass_utils import run_bass_kernel_spmd as _run

    nc = _bacc.Bacc("TRN2", target_bir_lowering=False, num_devices=1)
    arrays, args = {}, []
    for name in _INS:
        a = _np.ascontiguousarray(inputs[name])
        arrays[f"in_{name}_dram"] = a
        args.append(nc.dram_tensor(f"in_{name}_dram", a.shape, _mybir.dt.from_np(a.dtype), kind="ExternalInput").ap())
    out = nc.dram_tensor("out_0_dram", inputs["x"].shape, _mybir.dt.from_np(_np.dtype("float32")), kind="ExternalOutput").ap()
    build(nc, *args, out)
    r = _run(nc, [arrays], core_ids=[0])
    return r.results[0]["out_0_dram"]
```
